# Optimizing a Trainium2 kernel written in Bass

```python
import math
import jax, jax.numpy as jnp
from jax import lax
import numpy as np

D_MODEL = 1024
BATCH = 1
SEQ = 1024
DEPTH = 2

N_A = max(1, DEPTH // 2)
N_B = DEPTH - N_A
D_CONV = D_MODEL
CONV_K = 3
N_HEADS = 16
HEAD_DIM = D_MODEL // N_HEADS
D_ATTN = N_HEADS * HEAD_DIM
Q_BLOCK = 128
EPS = 1e-6


def rmsnorm(x, g):
    xf = x.astype(jnp.float32)
    y = xf * lax.rsqrt(jnp.mean(xf * xf, axis=-1, keepdims=True) + EPS)
    return (y * g.astype(jnp.float32)).astype(x.dtype)

def modulation(c, w, b, n):
    m = jax.nn.silu(c) @ w + b
    return jnp.split(m, n, axis=-1)

def modulated_norm(x, g, shift, scale):
    return rmsnorm(x, g) * (1.0 + scale[:, None, :]) + shift[:, None, :]

def causal_dwconv(u, w):
    return lax.conv_general_dilated(
        u, w[:, None, :].astype(u.dtype), window_strides=(1,),
        padding=[(CONV_K - 1, 0)], dimension_numbers=("NWC", "WIO", "NWC"),
        feature_group_count=u.shape[-1])

def short_conv_layer(x, c, mod_w, mod_b, norm_g, w_in, conv_w, w_out):
    shift, scale, gate = modulation(c, mod_w, mod_b, 3)
    h = modulated_norm(x, norm_g, shift, scale)
    proj = h @ w_in
    b_gate, c_gate, u, z = jnp.split(proj, 4, axis=-1)
    y = b_gate * causal_dwconv(c_gate * u, conv_w)
    y = y * jax.nn.silu(z)
    return x + gate[:, None, :] * (y @ w_out)

def stick_breaking_attention(q, k, v):
    seq = q.shape[2]
    inv_sqrt_d = 1.0 / math.sqrt(q.shape[-1])
    outs = []
    for i in range(seq // Q_BLOCK):
        q0 = i * Q_BLOCK
        kend = q0 + Q_BLOCK
        qb = q[:, :, q0:kend].astype(jnp.float32)
        kb = k[:, :, :kend].astype(jnp.float32)
        vb = v[:, :, :kend]
        z = jnp.einsum('bhqd,bhkd->bhqk', qb, kb) * inv_sqrt_d
        qpos = q0 + jnp.arange(Q_BLOCK)[:, None]
        kpos = jnp.arange(kend)[None, :]
        mask = kpos < qpos
        log_beta = jax.nn.log_sigmoid(z)
        log_1m_beta = jnp.where(mask, log_beta - z, 0.0)
        suffix = lax.cumsum(log_1m_beta, axis=3, reverse=True) - log_1m_beta
        a = jnp.where(mask, jnp.exp(log_beta + suffix), 0.0)
        outs.append(jnp.einsum('bhqk,bhkd->bhqd', a.astype(vb.dtype), vb))
    return jnp.concatenate(outs, axis=2)

def split_heads(t):
    b, s, _ = t.shape
    return t.reshape(b, s, N_HEADS, HEAD_DIM).transpose(0, 2, 1, 3)

def stick_breaking_layer(x, c, k, v, mod_w, mod_b, norm_g, w_qz, w_out):
    shift, scale, gate = modulation(c, mod_w, mod_b, 3)
    h = modulated_norm(x, norm_g, shift, scale)
    proj = h @ w_qz
    q, z = jnp.split(proj, 2, axis=-1)
    o = stick_breaking_attention(split_heads(q), k, v)
    b, _, s, _ = o.shape
    o = o.transpose(0, 2, 1, 3).reshape(b, s, D_ATTN)
    o = o * jax.nn.silu(z)
    return x + gate[:, None, :] * (o @ w_out)

def first_inputs(seed: int = 0) -> dict:
    key = jax.random.key(seed)
    ks = jax.random.split(key, 20)
    D = D_MODEL
    nrm = lambda k, shape, s: jax.random.normal(k, shape, jnp.float32) * s
    return {
        "x": nrm(ks[0], (BATCH, SEQ, D), 1.0),
        "c": nrm(ks[1], (BATCH, D), 1.0),
        "a_mod_w": nrm(ks[2], (N_A, D, 3 * D), 0.02),
        "a_mod_b": nrm(ks[3], (N_A, 3 * D), 0.01),
        "a_norm_g": 1.0 + nrm(ks[4], (N_A, D), 0.02),
        "a_w_in": nrm(ks[5], (N_A, D, 4 * D_CONV), D ** -0.5),
        "a_conv_w": nrm(ks[6], (N_A, CONV_K, D_CONV), CONV_K ** -0.5),
        "a_w_out": nrm(ks[7], (N_A, D_CONV, D), D_CONV ** -0.5),
        "kv_mod_w": nrm(ks[8], (D, 2 * D), 0.02),
        "kv_mod_b": nrm(ks[9], (2 * D,), 0.01),
        "kv_norm_g": 1.0 + nrm(ks[10], (D,), 0.02),
        "w_kv": nrm(ks[11], (D, 2 * D_ATTN), D ** -0.5),
        "b_mod_w": nrm(ks[12], (N_B, D, 3 * D), 0.02),
        "b_mod_b": nrm(ks[13], (N_B, 3 * D), 0.01),
        "b_norm_g": 1.0 + nrm(ks[14], (N_B, D), 0.02),
        "b_w_qz": nrm(ks[15], (N_B, D, 2 * D_ATTN), D ** -0.5),
        "b_w_out": nrm(ks[16], (N_B, D_ATTN, D), D_ATTN ** -0.5),
        "final_norm_g": 1.0 + nrm(ks[17], (D,), 0.02),
    }

def first_block(x, c, a_mod_w, a_mod_b, a_norm_g, a_w_in, a_conv_w, a_w_out,
              kv_mod_w, kv_mod_b, kv_norm_g, w_kv,
              b_mod_w, b_mod_b, b_norm_g, b_w_qz, b_w_out, final_norm_g):
    k = v = None
    for layer in range(DEPTH):
        if layer < N_A:
            x = short_conv_layer(x, c, a_mod_w[layer], a_mod_b[layer], a_norm_g[layer],
                                 a_w_in[layer], a_conv_w[layer], a_w_out[layer])
        else:
            if layer == N_A:
                kv_shift, kv_scale = modulation(c, kv_mod_w, kv_mod_b, 2)
                hkv = modulated_norm(x, kv_norm_g, kv_shift, kv_scale)
                k_flat, v_flat = jnp.split(hkv @ w_kv, 2, axis=-1)
                k, v = split_heads(k_flat), split_heads(v_flat)
            j = layer - N_A
            x = stick_breaking_layer(x, c, k, v, b_mod_w[j], b_mod_b[j], b_norm_g[j],
                                     b_w_qz[j], b_w_out[j])
    return rmsnorm(x, final_norm_g)


DEPTH_2 = 1

CHUNK = 64
POOL_WINDOWS = (2, 4, 8, 16)
N_POOL_GROUPS = len(POOL_WINDOWS)
POOL_GROUP_DIM = D_MODEL // 8
POOL_DIM = N_POOL_GROUPS * POOL_GROUP_DIM
N_HEADS_2 = 8
HEAD_DIM_2 = D_MODEL // 16
V_HEAD_DIM = 2 * HEAD_DIM_2
QK_DIM = N_HEADS_2 * 2 * HEAD_DIM_2
V_DIM = N_HEADS_2 * V_HEAD_DIM
IN_DIM = POOL_DIM + 2 * QK_DIM + V_DIM
D_FF = 4 * D_MODEL
N_BRANCHES = 2


def rmsnorm_2(x, g):
    xf = x.astype(jnp.float32)
    y = xf * lax.rsqrt(jnp.mean(xf * xf, axis=-1, keepdims=True) + EPS)
    return (y * g.astype(jnp.float32)).astype(x.dtype)

def head_rmsnorm(x, g):
    xf = x.astype(jnp.float32)
    return xf * lax.rsqrt(jnp.mean(xf * xf, axis=-1, keepdims=True) + EPS) * g.astype(jnp.float32)

def alibi_slopes(n):
    return jnp.asarray(np.array([2.0 ** (-8.0 * (i + 1) / n) for i in range(n)], dtype=np.float32))

def pool_mixer(u, w_grp, scale):
    B, S, _ = u.shape
    uf = u.astype(jnp.float32).reshape(B, S, N_POOL_GROUPS, POOL_GROUP_DIM)
    csum = jnp.pad(jnp.cumsum(uf, axis=1), ((0, 0), (1, 0), (0, 0), (0, 0)))
    t = jnp.arange(S)
    pooled = []
    for g, w in enumerate(POOL_WINDOWS):
        lo = jnp.maximum(t + 1 - w, 0)
        win_sum = csum[:, 1:, g] - csum[:, lo, g]
        cnt = (t + 1 - lo).astype(jnp.float32)
        pooled.append(win_sum / cnt[None, :, None])
    mixed = jnp.stack(pooled, axis=2) - uf
    y = jnp.einsum('bsgc,gcd->bsgd', mixed, w_grp.astype(jnp.float32))
    return (y.reshape(B, S, POOL_DIM) * scale.astype(jnp.float32)).astype(u.dtype)

def diff_attention(q, k, v, g_q, g_k, lam, g_sub, lambda_init):
    B, S = q.shape[0], q.shape[1]
    qn = head_rmsnorm(q, g_q) * (HEAD_DIM_2 ** -0.5)
    kn = head_rmsnorm(k, g_k)
    vf = v.astype(jnp.float32)
    lam = lam.astype(jnp.float32)
    slopes = alibi_slopes(N_HEADS_2)
    pos = jnp.arange(S)
    key_chunk = pos // CHUNK
    nb = S // Q_BLOCK
    q_blocks = qn.reshape(B, nb, Q_BLOCK, N_HEADS_2, 2, HEAD_DIM_2).transpose(1, 0, 2, 3, 4, 5)
    q_pos = pos.reshape(nb, Q_BLOCK)
    neg = jnp.finfo(jnp.float32).min

    def block(args):
        qblk, qp = args
        s = jnp.einsum('bqhid,bkhid->bihqk', qblk, kn)
        dist = jnp.abs(qp[:, None] - pos[None, :]).astype(jnp.float32)
        bias = -slopes[:, None, None] * dist
        allowed = key_chunk[None, :] <= (qp // CHUNK)[:, None]
        s = jnp.where(allowed, s + bias, neg)
        p = jax.nn.softmax(s, axis=-1)
        a = p[:, 0] - lam * p[:, 1]
        return jnp.einsum('bhqk,bkhe->bqhe', a, vf)

    o = lax.map(block, (q_blocks, q_pos))
    o = o.transpose(1, 0, 2, 3, 4).reshape(B, S, N_HEADS_2, V_HEAD_DIM)
    o = head_rmsnorm(o, g_sub) * (1.0 - lambda_init)
    return o.reshape(B, S, V_DIM).astype(v.dtype)

def second_inputs(seed: int = 0) -> dict:
    key = jax.random.key(seed)
    ks = jax.random.split(key, 20)
    f32 = jnp.float32

    def nrm(k, shape, fan_in):
        return jax.random.normal(k, shape, f32) * (fan_in ** -0.5)

    def gain(k, shape):
        return 1.0 + 0.05 * jax.random.normal(k, shape, f32)

    return {
        "x": jax.random.normal(ks[0], (BATCH, SEQ, D_MODEL), f32),
        "g_mix": gain(ks[1], (DEPTH_2, D_MODEL)),
        "w_in": nrm(ks[2], (DEPTH_2, D_MODEL, IN_DIM), D_MODEL),
        "w_pool_grp": nrm(ks[3], (DEPTH_2, N_POOL_GROUPS, POOL_GROUP_DIM, POOL_GROUP_DIM), POOL_GROUP_DIM),
        "pool_scale": gain(ks[4], (DEPTH_2, POOL_DIM)),
        "g_q": gain(ks[5], (DEPTH_2, HEAD_DIM_2)),
        "g_k": gain(ks[6], (DEPTH_2, HEAD_DIM_2)),
        "lambda_qk": 0.1 * jax.random.normal(ks[7], (DEPTH_2, 4, HEAD_DIM_2), f32),
        "g_sub": gain(ks[8], (DEPTH_2, V_HEAD_DIM)),
        "w_branch_pool": nrm(ks[9], (DEPTH_2, POOL_DIM, D_MODEL), POOL_DIM),
        "w_branch_attn": nrm(ks[10], (DEPTH_2, V_DIM, D_MODEL), V_DIM),
        "w_gate": nrm(ks[11], (DEPTH_2, D_MODEL, N_BRANCHES * D_MODEL), D_MODEL),
        "b_gate": 0.01 * jax.random.normal(ks[12], (DEPTH_2, N_BRANCHES * D_MODEL), f32),
        "w_out": nrm(ks[13], (DEPTH_2, D_MODEL, D_MODEL), D_MODEL),
        "g_ffn": gain(ks[14], (DEPTH_2, D_MODEL)),
        "w_up": nrm(ks[15], (DEPTH_2, D_MODEL, D_FF), D_MODEL),
        "w_down": nrm(ks[16], (DEPTH_2, D_FF, D_MODEL), D_FF),
    }

def second_block(x, g_mix, w_in, w_pool_grp, pool_scale, g_q, g_k, lambda_qk, g_sub,
              w_branch_pool, w_branch_attn, w_gate, b_gate, w_out, g_ffn, w_up, w_down):
    B, S, _ = x.shape
    for l in range(DEPTH_2):
        lambda_init = 0.8 - 0.6 * math.exp(-0.3 * l)
        h = rmsnorm_2(x, g_mix[l])
        z = h @ w_in[l]
        u_pool = z[..., :POOL_DIM]
        q = z[..., POOL_DIM:POOL_DIM + QK_DIM].reshape(B, S, N_HEADS_2, 2, HEAD_DIM_2)
        k = z[..., POOL_DIM + QK_DIM:POOL_DIM + 2 * QK_DIM].reshape(B, S, N_HEADS_2, 2, HEAD_DIM_2)
        v = z[..., POOL_DIM + 2 * QK_DIM:].reshape(B, S, N_HEADS_2, V_HEAD_DIM)

        y_pool = pool_mixer(u_pool, w_pool_grp[l], pool_scale[l])
        lq = lambda_qk[l].astype(jnp.float32)
        lam = jnp.exp(jnp.sum(lq[0] * lq[1])) - jnp.exp(jnp.sum(lq[2] * lq[3])) + lambda_init
        y_attn = diff_attention(q, k, v, g_q[l], g_k[l], lam, g_sub[l], lambda_init)

        gates = jax.nn.sigmoid(h @ w_gate[l] + b_gate[l])
        merged = (gates[..., :D_MODEL] * (y_pool @ w_branch_pool[l])
                  + gates[..., D_MODEL:] * (y_attn @ w_branch_attn[l]))
        x = x + merged @ w_out[l]

        h2 = rmsnorm_2(x, g_ffn[l])
        x = x + jnp.square(jax.nn.relu(h2 @ w_up[l])) @ w_down[l]
    return x


def setup_inputs(seed=0):
    out = dict(first_inputs(seed))
    for name, value in second_inputs(seed + 1).items():
        if name != "x":
            out[name + "_2"] = value
    return out


def reference(
    x, c, a_mod_w, a_mod_b, a_norm_g, a_w_in, a_conv_w, a_w_out, kv_mod_w, kv_mod_b, kv_norm_g,
    w_kv, b_mod_w, b_mod_b, b_norm_g, b_w_qz, b_w_out, final_norm_g, g_mix_2, w_in_2,
    w_pool_grp_2, pool_scale_2, g_q_2, g_k_2, lambda_qk_2, g_sub_2, w_branch_pool_2,
    w_branch_attn_2, w_gate_2, b_gate_2, w_out_2, g_ffn_2, w_up_2, w_down_2,
):
    x = first_block(
        x, c, a_mod_w, a_mod_b, a_norm_g, a_w_in, a_conv_w, a_w_out, kv_mod_w, kv_mod_b,
        kv_norm_g, w_kv, b_mod_w, b_mod_b, b_norm_g, b_w_qz, b_w_out, final_norm_g,
    )
    return second_block(
        x, g_mix_2, w_in_2, w_pool_grp_2, pool_scale_2, g_q_2, g_k_2, lambda_qk_2, g_sub_2,
        w_branch_pool_2, w_branch_attn_2, w_gate_2, b_gate_2, w_out_2, g_ffn_2, w_up_2,
        w_down_2,
    )


_drawn_inputs = setup_inputs


def setup_inputs(seed=0):
    import zlib

    import numpy as np

    out = dict(_drawn_inputs(seed))
    spreads = {}
    factors = {'a_mod_b': 3.24,
     'a_norm_g': 3.092,
     'kv_mod_b': 8.0,
     'kv_norm_g': 8.0,
     'b_mod_b': 7.354,
     'b_norm_g': 8.0,
     'g_k_2': 3.519,
     'g_sub_2': 2.973,
     'b_gate_2': 8.0,
     'pool_scale_2': 3.918}
    for name, (base, spread) in spreads.items():
        noise = np.random.default_rng([zlib.crc32(name.encode()), seed]).standard_normal(out[name].shape)
        drawn = base * np.exp(spread * noise) if base else spread * noise
        out[name] = __import__('jax').numpy.asarray(drawn.astype(out[name].dtype))
    for name, factor in factors.items():
        out[name] = (out[name] * factor).astype(out[name].dtype)
    return out
```

```python
from contextlib import ExitStack

import numpy as np

import concourse.bass as bass
from concourse import mybir

F32 = mybir.dt.float32
F32R = mybir.dt.float32r
ALU = mybir.AluOpType
ACT = mybir.ActivationFunctionType
AX_X = mybir.AxisListType.X
ds = bass.ds

P = 128
D = 1024
S = 1024
KT = D // P
ST = S // P
HALF = 512
DFF = 4 * D
FFQ = DFF // D
EPS = 1e-6
HD = 64
BIG = 2.0 ** 100

C_AIN = 0
C_AOUT = C_AIN + 4 * KT
C_KV = C_AOUT + KT
C_QZ = C_KV + 2 * KT
C_BOUT = C_QZ + 2 * KT
C_POOL = C_BOUT + KT
C_GP = C_POOL + 5
C_GA = C_GP + 2 * KT
C_QKV2 = C_GA + KT
C_AB = C_QKV2 + 3 * KT
C_WO = C_AB + KT
C_FF = C_WO + KT
N_CHUNKS = C_FF + FFQ * 2 * KT
N_MODS_A = 3 * KT
N_MODS = 8 * KT

_V = {}
_n = 0
for _name, _w in (("c", 8), ("mod_b", 64), ("a_g", 8), ("kv_g", 8), ("b_g", 8), ("conv", 24),
                  ("final_g", 8), ("mix_g", 8), ("pool_scale", 4), ("gq", 1), ("gk", 1),
                  ("gsub", 1), ("b_gate", 16), ("ffn_g", 8), ("slope", 8), ("edge", 64)):
    _V[_name] = _n
    _n += _w
NV = _n
K_ID, K_TRI, K_BD, K_DIST, K_LAM = 0, 128, 256, 384, 384 + S
NC_ = K_LAM + 4 * HD
POOL_W = (2, 4, 8, 16)
PADW = 16
LAMBDA_INIT = 0.2


_USES = (("ain", 16, 16, 0), ("aout", 4, 4, 0), ("kv", 8, 8, 8), ("qz", 16, 64, 64),
         ("bout", 4, 4, 0), ("pool", 2, 2, 0), ("gp", 8, 8, 0), ("ga", 4, 4, 0),
         ("qkv2", 24, 64, 64), ("ab", 4, 4, 0), ("wo", 4, 4, 0), ("ff", 32, 32, 0))
USED = {}
_at = (1, 1, 1)
for _name, *_k in _USES:
    USED[_name] = _at
    _at = tuple(x + y for x, y in zip(_at, _k))

FILL = {name: KT * n for n, name in enumerate(("a", "kv", "qz", "y", "mix", "ab", "ffn"))}
SCALED = {name: KT * n for n, name in enumerate(("a", "kv", "qz", "mix", "ffn"))}


class Links:

    def __init__(self, eng, sem):
        self.eng, self.sem, self.n = eng, sem, 0
        self.i = self.per = self.k = None

    def round(self, i, per):
        self.i, self.per, self.k = i, per, 0

    def end(self, rounds):
        assert self.k == self.per, (self.k, self.per)
        self.n += self.per * rounds
        self.i = None

    def __call__(self, ins):
        ins.then_inc(self.sem, 1)
        if self.i is None:
            self.n += 1
            self.eng.wait_ge(self.sem, self.n)
        else:
            self.k += 1
            self.eng.wait_ge(self.sem, self.i * self.per + (self.n + self.k))


def blocks_of(t, g):
    return range(4 * g, min(t + 1, 4 * g + 4))


GROUPS = np.cumsum([len(range(0, t + 1, 4)) for t in range(ST)]).tolist()
NG = GROUPS[-1]


def group_index(s):
    return NG * (s // ST) + (GROUPS[s % ST - 1] if s % ST else 0)



def block_kernel(nc, xt, vecs, consts, mods, wst, out):
    with ExitStack() as ctx:
        def sem(name):
            return ctx.enter_context(nc.semaphore(name))

        at = [nc.sbuf_base]

        def place(name, cols, dt=F32, where=at):
            where[0] = (where[0] + 31) // 32 * 32
            t = nc.alloc_sbuf_tensor_at(name, [P, cols], dt, offset=where[0])
            where[0] += cols * 4
            assert where[0] <= nc.sbuf_usable_end, (name, where[0] - nc.sbuf_usable_end)
            return t

        X = place("X", KT * S)
        HH = place("HH", KT * S, F32R)
        HL = place("HL", KT * S, F32R)
        WR0 = place("WR0", D)
        WR1 = place("WR1", D)
        WH = [place(f"WH{i}", D, F32R) for i in range(2)]
        WL = [place(f"WL{i}", D, F32R) for i in range(2)]
        VEC = place("VEC", NV)
        MOD = place("MOD", N_MODS)
        COEF = place("COEF", 4 * KT)
        IDF = place("IDF", P)
        IDR = place("IDR", P, F32R)
        TRIR = place("TRIR", P, F32R)
        ONES = place("ONES", P)
        SC = place("SC", KT)
        SM = place("SM", 16)
        EPSC = place("EPSC", 1)
        NLAM = place("NLAM", 1)
        GQ8 = place("GQ8", 1)
        GS8 = place("GS8", 1)
        ATT0 = at[0]
        TMP = [place(f"TMP{i}", PADW + S) for i in range(5)]
        T = [t[:, 0:S] for t in TMP]
        TP = TMP[4][:, PADW:]
        SCR0 = at[0]
        GH = place("GH", KT * S, F32R)
        GL = place("GL", KT * S, F32R)
        r = [SCR0]
        KST, VST, VTT = (place(n, S, F32, r) for n in ("KST", "VST", "VTT"))
        r = [SCR0]
        YPH = place("YPH", 4 * S, F32R, r)
        YPL = place("YPL", 4 * S, F32R, r)
        MXH = place("MXH", 4 * S, F32R, r)
        MXL = place("MXL", 4 * S, F32R, r)
        r = [ATT0]
        bQH, bQL, bKH, bKL, bVH, bVL = (place("b" + n, S, F32R, r) for n in ("QH", "QL", "KH", "KL", "VH", "VL"))
        bQR, bKR, bVR, bSG, bZS, bYO = (place("b" + n, S, F32, r) for n in ("QR", "KR", "VR", "SG", "ZS", "YO"))
        bC = [place(f"bC{i}", S + 8, F32, r) for i in range(2)]
        bB = [place(f"bB{i}", S, F32, r) for i in range(3)]
        bATH = place("bATH", S, F32R, r)
        bATL = place("bATL", S, F32R, r)
        r = [ATT0]
        STG = [place(f"STG{i}", S, F32, r) for i in range(4)]
        r = [ATT0]
        dQH, dQL, dKH, dKL, dVH, dVL = (place("d" + n, S, F32R, r) for n in ("QH", "QL", "KH", "KL", "VH", "VL"))
        dQR, dKR, dVT, dSQ, dRS, dOT, dYO = (place("d" + n, S, F32, r) for n in ("QR", "KR", "VT", "SQ", "RS", "OT", "YO"))
        dP0 = [place(f"dP0{i}", S, F32, r) for i in range(2)]
        dP1 = place("dP1", S, F32, r)
        dATH = place("dATH", S, F32R, r)
        dATL = place("dATL", S, F32R, r)
        dBIAS = place("dBIAS", S, F32R, r)
        dDIST = place("dDIST", S, F32, r)
        dBD = place("dBD", P, F32, r)

        PS = ctx.enter_context(nc.psum_tensor("PS", [P, 8 * HALF], F32))
        PAIR = [PS[:, p * S:(p + 1) * S] for p in range(4)]
        TB = 3 * S
        OB = 3 * S + HALF
        MC = 3 * S

        def scratch(name):
            return nc.dram_tensor(name, [KT, P, S], F32, kind="Internal").ap()

        kv_k, kv_v, y_b, m_p, g_a, y_d = (scratch(n) for n in ("kv_k", "kv_v", "y_b", "m_p", "g_a", "y_d"))

        def row(t, i):
            return t[i] if isinstance(i, int) else t[ds(i, 1)].rearrange("a p c -> (a p) c")

        def kt(t, i):
            return t[:, i * S:(i + 1) * S] if isinstance(i, int) else t[:, ds(i * S, S)]

        def col(t, i):
            return t[:, i:i + 1] if isinstance(i, int) else t[:, ds(i, 1)]

        def vec(name, i=0):
            return col(VEC, i + _V[name])

        ld_c = sem("ld_c")
        ld_x = sem("ld_x")
        ld_mod = [sem(f"ld_mod{i}") for i in range(2)]
        mod_used = sem("mod_used")
        ld_w = sem("ld_w")
        w_hi = sem("w_hi")
        w_lo = sem("w_lo")
        chunk_done = sem("chunk_done")
        free = [sem(f"free{p}") for p in range(3)]
        dve_link = sem("dve_link")
        act_link = sem("act_link")
        s_sig = sem("s_sig")
        s_sc = sem("s_sc")
        s_const = sem("s_const")
        mod_ready = sem("mod_ready")
        sq = sem("sq")
        sq_added = sem("sq_added")
        ss = sem("ss")
        rs = sem("rs")
        ms2 = sem("ms2")
        ftmp = sem("ftmp")
        f_hi = sem("f_hi")
        f_lo = sem("f_lo")
        g_hi = sem("g_hi")
        g_lo = sem("g_lo")
        back = [sem(f"back{i}") for i in range(4)]
        ain_sg = sem("ain_sg")
        ain_y = sem("ain_y")
        kv_t = sem("kv_t")
        st_k = sem("st_k")
        st_v = sem("st_v")
        b_ldk = sem("b_ldk")
        b_ldv = sem("b_ldv")
        b_sg = sem("b_sg")
        b_hi = sem("b_hi")
        b_split = sem("b_split")
        b_s = sem("b_s")
        b_c = sem("b_c")
        b_scan = sem("b_scan")
        b_a = sem("b_a")
        b_t = sem("b_t")
        b_ath = sem("b_ath")
        b_atl = sem("b_atl")
        b_av = sem("b_av")
        b_o = sem("b_o")
        b_st = sem("b_st")
        p_mx = sem("p_mx")
        p_mh = sem("p_mh")
        p_ml = sem("p_ml")
        p_g = sem("p_g")
        p_yh = sem("p_yh")
        p_yl = sem("p_yl")
        gp_st = sem("gp_st")
        ga_st = sem("ga_st")
        d_ld = sem("d_ld")
        d_lam = sem("d_lam")
        d_sq = sem("d_sq")
        d_ss = sem("d_ss")
        d_ln = sem("d_ln")
        d_rs = sem("d_rs")
        d_n = sem("d_n")
        d_v = sem("d_v")
        d_vt = sem("d_vt")
        d_hi = sem("d_hi")
        d_split = sem("d_split")
        d_s = sem("d_s")
        d_max = sem("d_max")
        d_a = sem("d_a")
        d_t = sem("d_t")
        d_ath = sem("d_ath")
        d_atl = sem("d_atl")
        d_av = sem("d_av")
        d_o = sem("d_o")
        d_yo = sem("d_yo")
        d_st = sem("d_st")
        ab_ld = [sem(f"ab_ld{i}") for i in range(2)]
        ab_m = sem("ab_m")
        ff_r = sem("ff_r")
        st_out = sem("st_out")

        block = ctx.enter_context(nc.Block())

        @block.sync
        def _(sp):
            def load_w(c):
                sp.wait_ge(w_lo, c)
                sp.dma_start(WR0[:, :], row(wst, c)).then_inc(ld_w, 16)

            sp.dma_start(VEC[:, :], vecs).then_inc(ld_c, 16)
            sp.dma_start(IDF[:, :], consts[:, K_ID:K_ID + P]).then_inc(ld_c, 16)
            sp.dma_start(T[0][:, 0:P], consts[:, K_TRI:K_TRI + P]).then_inc(ld_c, 16)
            sp.dma_start(X[:, :], xt).then_inc(ld_x, 16)
            for m in range(2):
                sp.dma_start([WR0, WR1][m][:, :], mods[m]).then_inc(ld_mod[m], 16)
            with sp.Fori(1, N_MODS_A // 2) as i:
                for m in range(2):
                    sp.wait_ge(mod_used, 2 * i + (m - 1))
                    sp.dma_start([WR0, WR1][m][:, :], row(mods, 2 * i + m)).then_inc(ld_mod[m], 16)
            sp.wait_ge(mod_used, N_MODS_A - 1)
            sp.dma_start(WR0[:, :], wst[0]).then_inc(ld_w, 16)
            load_w(1)
            with sp.Fori(0, C_KV) as c:
                sp.wait_ge(mod_used, c + N_MODS_A)
                sp.dma_start(WR1[:, :], row(mods, c + N_MODS_A)).then_inc(ld_mod[1], 16)
                load_w(c + 2)
            with sp.Fori(0, KT) as i:
                load_w(2 * i + (C_KV + 2))
                sp.wait_ge(free[0], i + (USED["kv"][0] + 1))
                sp.dma_start(row(kv_k, i), KST[:, :]).then_inc(st_k, 16)
                load_w(2 * i + (C_KV + 3))
                sp.wait_ge(free[2], i + (USED["kv"][2] + 1))
                sp.dma_start(row(kv_v, i), VTT[:, :]).then_inc(st_v, 16)
            sp.wait_ge(st_k, KT * 16)
            sp.wait_ge(st_v, KT * 16)
            load_w(C_QZ + 2)
            load_w(C_QZ + 3)
            sp.wait_ge(f_lo, FILL["qz"] + KT)
            sp.dma_start(bKR[:, :], kv_k[0]).then_inc(b_ldk, 16)
            sp.dma_start(bVR[:, :], kv_v[0]).then_inc(b_ldv, 16)
            with sp.Fori(0, KT - 1) as j:
                sp.wait_ge(b_split, j + 1)
                sp.dma_start(bKR[:, :], row(kv_k, j + 1)).then_inc(b_ldk, 16)
                sp.dma_start(bVR[:, :], row(kv_v, j + 1)).then_inc(b_ldv, 16)
                load_w(2 * j + (C_QZ + 4))
                load_w(2 * j + (C_QZ + 5))
                sp.wait_ge(b_o, 16 * j + 16)
                sp.dma_start(row(y_b, j), bYO[:, :]).then_inc(b_st, 16)
            sp.wait_ge(b_o, 16 * KT)
            sp.dma_start(y_b[KT - 1], bYO[:, :]).then_inc(b_st, 16)
            sp.wait_ge(b_st, 16 * KT)

            def operand_back(src, name):
                for k in range(KT):
                    if k >= 4:
                        sp.wait_ge(f_lo, FILL[name] + k - 3)
                    sp.dma_start(STG[k % 4][:, :], src[k]).then_inc(back[k % 4], 16)

            operand_back(y_b, "y")
            with sp.Fori(0, KT) as c:
                load_w(c + (C_BOUT + 2))
            with sp.Fori(0, 5) as c:
                load_w(c + (C_POOL + 2))
            with sp.Fori(0, KT) as n:
                load_w(2 * n + (C_GP + 2))
                load_w(2 * n + (C_GP + 3))
                sp.wait_ge(free[(C_GP + 1) % 2], n + (USED["gp"][(C_GP + 1) % 2] + 1))
                sp.dma_start(row(m_p, n), T[2]).then_inc(gp_st, 16)
            with sp.Fori(0, KT // 2) as i:
                for m in range(2):
                    s = (C_GA + m) % 2
                    load_w(2 * i + (C_GA + 2 + m))
                    sp.wait_ge(free[s], i + (USED["ga"][s] + 1))
                    sp.dma_start(row(g_a, 2 * i + m), T[3]).then_inc(ga_st, 16)
            sp.wait_ge(gp_st, 16 * KT)
            sp.wait_ge(ga_st, 16 * KT)
            sp.dma_start(dDIST[:, :], consts[:, K_DIST:K_DIST + S]).then_inc(d_ld, 16)
            sp.dma_start(dVT[:, 0:4 * HD], consts[:, K_LAM:K_LAM + 4 * HD]).then_inc(d_ld, 16)
            sp.dma_start(dBD[:, :], consts[:, K_BD:K_BD + P]).then_inc(d_st, 16)
            for c in range(3):
                load_w(C_QKV2 + 2 + c)
            with sp.Fori(0, KT - 1) as j:
                for n in range(3):
                    load_w(3 * j + (C_QKV2 + 5 + n))
                sp.wait_ge(d_yo, j + 1)
                sp.dma_start(row(y_d, j), dYO[:, :]).then_inc(d_st, 16)
            sp.wait_ge(d_yo, KT)
            sp.dma_start(y_d[KT - 1], dYO[:, :]).then_inc(d_st, 16)
            sp.wait_ge(d_st, 16 * KT + 16)
            operand_back(y_d, "ab")
            sp.wait_ge(f_lo, FILL["ab"] + KT)
            for n in range(KT):
                if n >= 2:
                    sp.wait_ge(g_lo, KT + n - 1)
                sp.dma_start(T[n % 2], g_a[n]).then_inc(ab_ld[n % 2], 16)
                sp.dma_start(T[2 + n % 2], m_p[n]).then_inc(ab_ld[n % 2], 16)
                load_w(C_AB + 2 + n)
            with sp.Fori(0, KT) as n:
                load_w(n + (C_WO + 2))
            with sp.Fori(0, FFQ * 2 * KT - 1) as n:
                load_w(n + (C_FF + 2))
            with sp.Fori(0, KT // 2) as i:
                for m in range(2):
                    s = (C_FF + m) % 2
                    sp.wait_ge(free[s], i + (USED["ff"][s] + (2 * FFQ - 1) * KT // 2 + 1))
                    sp.dma_start(row(out, 2 * i + m), kt(X, 2 * i + m)).then_inc(st_out, 16)
            sp.wait_ge(st_out, 16 * KT)

        @block.tensor
        def _(pe):
            def mm3(dst0, lh, ll, RH, RL, k, start, stop):
                for l, rr, a, z in ((lh, RH, start, False), (lh, RL, False, False), (ll, RH, False, stop)):
                    for q in (0, HALF):
                        last = pe.matmul(PS[:, dst0 + q:dst0 + q + HALF], l, rr[:, k * S + q:k * S + q + HALF],
                                         start=a, stop=z)
                return last

            def step(c, slot, pair, RH, RL, k, nk=KT):
                if k == 0:
                    pe.wait_ge(w_hi, c + 1)
                    pe.wait_ge(w_lo, c + 1)
                b = slice(k * P, (k + 1) * P)
                last = mm3(pair * S, WH[slot][:, b], WL[slot][:, b], RH, RL, k, k == 0, k == nk - 1)
                if k == nk - 1:
                    last.then_inc(chunk_done, 1)

            def chunk(c, slot, pair, used, RH=HH, RL=HL, nk=KT, operand=None):
                pe.wait_ge(free[pair], used)
                for k in range(nk):
                    if operand:
                        pe.wait_ge(operand[0], operand[1] + (k + 1))
                    step(c, slot, pair, RH, RL, k, nk)

            def chunks(name, base, n, RH, RL, operand=None, mods=None):
                u = USED[name]
                with pe.Fori(0, n // 2) as i:
                    for m in range(2):
                        s = (base + m) % 2
                        chunk(2 * i + (base + m), s, s, i + u[s], RH, RL, operand=operand if m == 0 else None)
                        if mods is not None:
                            modulation(2 * i + (mods + m), 1, 2 * i + (mods + m - N_MODS_A // 2 + 1))

            def modulation(m, slot, count):
                pe.wait_ge(ld_mod[slot], 16 * count)
                for k in range(KT):
                    last = pe.matmul(PS[:, ds(m + MC, 1)], [WR0, WR1][slot][:, k * P:(k + 1) * P], SC[:, k:k + 1],
                                     start=(k == 0), stop=(k == KT - 1))
                last.then_inc(mod_used, 1)

            def sum_squares(added, acc, dst=2 * S):
                pe.wait_ge(sq_added, added)
                for h in (0, HALF):
                    last = pe.matmul(PS[:, dst + h:dst + h + HALF], ONES[:, :], acc[:, h:h + HALF], start=True, stop=True)
                last.then_inc(ss, 1)

            pe.wait_ge(s_const, 1)
            sum_squares(KT, T[1])
            pe.wait_ge(s_sc, 1)
            with pe.Fori(0, N_MODS_A // 2) as i:
                for m in range(2):
                    modulation(2 * i + m, m, i + 1)
            u = USED["ain"]
            with pe.Fori(0, KT) as j:
                for n in range(4):
                    chunk(4 * j + n, n % 2, n % 2, 2 * j + (u[n % 2] + n // 2),
                          operand=(f_lo, FILL["a"]) if n == 0 else None)
                    modulation(4 * j + (N_MODS_A + n), 1, 4 * j + (N_MODS_A // 2 + n + 1))
            chunks("aout", C_AOUT, KT, GH, GL, operand=(g_lo, 0), mods=N_MODS_A + C_AOUT)
            sum_squares(2 * KT, T[1])
            u = USED["kv"]
            with pe.Fori(0, KT) as i:
                chunk(2 * i + C_KV, 0, 0, i + u[0], operand=(f_lo, FILL["kv"]))
                chunk(2 * i + (C_KV + 1), 1, 1, i + u[1])
                pe.wait_ge(free[1], i + (u[1] + 1))
                pe.wait_ge(free[2], i + u[2])
                for t in range(ST):
                    b = slice(t * P, (t + 1) * P)
                    last = pe.transpose(PS[:, 2 * S + t * P:2 * S + (t + 1) * P], VST[:, b], IDF[:, :])
                last.then_inc(kv_t, 1)

            def score_parts(base, rows, q, n, QH, QL, KH, KL, open_bank=None):
                for l, rr, a in ((QH, KH, True), (QH, KL, False), (QL, KH, False)):
                    for c0 in range(0, n, HALF):
                        w = min(HALF, n - c0)
                        pe.matmul(PS[:, base + c0:base + c0 + w], l[rows, q], rr[rows, c0:c0 + w], start=a,
                                  stop=(l is QL and open_bank is not None and c0 != open_bank))

            def value_sum(t, VH, VL, ATH, ATL):
                for kb in range(t + 1):
                    b = slice(kb * P, (kb + 1) * P)
                    o = PS[:, OB:OB + P]
                    pe.matmul(o, VH[:, b], ATH[:, b], start=(kb == 0), stop=False)
                    pe.matmul(o, VH[:, b], ATL[:, b], start=False, stop=False)
                    last = pe.matmul(o, VL[:, b], ATH[:, b], start=False, stop=(kb == t))
                return last

            u = USED["qz"]
            chunk(C_QZ, 0, 0, u[0], operand=(f_lo, FILL["qz"]))
            chunk(C_QZ + 1, 1, 0, u[0] + 1)

            def attention_b(j, fill):
                def turn(s, g):
                    pe.wait_ge(b_a, 2 * ST * j + (s + 1))
                    if s or g:
                        pe.wait_ge(b_atl, 2 * NG * j + (group_index(s) + g))
                    for n, kb in enumerate(blocks_of(s % ST, g)):
                        last = pe.transpose(PS[:, TB + n * P:TB + (n + 1) * P], bB[s % 3][:, kb * P:(kb + 1) * P], IDF[:, :])
                    last.then_inc(b_t, 1)

                def scores(s):
                    h, t = s // ST, s % ST
                    base = (1 + s % 2) * S
                    pe.wait_ge(free[1 + s % 2], ST * j + (u[1 + s % 2] + s // 2))
                    score_parts(base, slice(h * HD, (h + 1) * HD), slice(t * P, (t + 1) * P), (t + 1) * P,
                                bQH, bQL, bKH, bKL, open_bank=t * P // HALF * HALF)
                    pe.matmul(PS[:, base + t * P:base + (t + 1) * P], IDR[:, :], TRIR[:, :],
                              start=False, stop=True).then_inc(b_s, 1)

                def values(s):
                    if s:
                        pe.wait_ge(b_o, 2 * ST * j + s)
                    pe.wait_ge(b_atl, 2 * NG * j + group_index(s + 1))
                    value_sum(s % ST, bVH, bVL, bATH, bATL).then_inc(b_av, 1)

                pe.wait_ge(b_split, j + 1)
                for s in range(2 * ST + 3):
                    if 0 <= s - 3:
                        values(s - 3)
                    if 0 <= s - 2 < 2 * ST:
                        turn(s - 2, 0)
                    if s < 2 * ST:
                        scores(s)
                    if 0 <= s - 2 < 2 * ST and (s - 2) % ST >= 4:
                        turn(s - 2, 1)
                    if fill and s < 2 * ST:
                        if s % KT == 0:
                            pe.wait_ge(free[0], 2 * j + (u[0] + 2 + s // KT))
                        step(2 * j + (C_QZ + 2 + s // KT), s // KT, 0, HH, HL, s % KT)

            with pe.Fori(0, KT - 1) as j:
                attention_b(j, True)
            attention_b(KT - 1, False)
            chunks("bout", C_BOUT, KT, HH, HL, operand=(f_lo, FILL["y"]))
            sum_squares(4 * KT, T[1])
            sum_squares(4 * KT, TP, dst=3 * S)

            uu = USED["pool"]
            for g in range(4):
                s = (C_POOL + g) % 2
                chunk(C_POOL + g, s, s, uu[s] + g // 2, operand=(f_lo, FILL["mix"]) if g == 0 else None)
            cg = C_POOL + 4
            pe.wait_ge(w_lo, cg + 1)
            for g in range(4):
                b = slice(g * P, (g + 1) * P)
                pe.wait_ge(p_ml, g + 1)
                if g < 2:
                    pe.wait_ge(free[g], uu[g] + 2)
                else:
                    pe.wait_ge(p_yl, g - 1)
                last = mm3((g % 2) * S, WH[cg % 2][:, b], WL[cg % 2][:, b], MXH, MXL, g, True, True)
                last.then_inc(p_g if g < 3 else chunk_done, 1)
            u = USED["gp"]
            s0, s1 = C_GP % 2, (C_GP + 1) % 2
            pe.wait_ge(p_yl, 4)
            with pe.Fori(0, KT) as n:
                chunk(2 * n + C_GP, s0, s0, n + u[s0])
                chunk(2 * n + (C_GP + 1), s1, s1, n + u[s1], YPH, YPL, nk=4)
            chunks("ga", C_GA, KT, HH, HL)

            ud = USED["qkv2"]

            def group_sums(n):
                pe.wait_ge(d_sq, n)
                for h in (0, HALF):
                    last = pe.matmul(PS[:, h:h + HALF], dBD[:, :], dSQ[:, h:h + HALF], start=True, stop=True)
                last.then_inc(d_ss, 1)

            def turn_values(n):
                pe.wait_ge(d_v, n)
                for t in range(ST):
                    b = slice(t * P, (t + 1) * P)
                    last = pe.transpose(PS[:, b], dVT[:, b], IDF[:, :])
                last.then_inc(d_vt, 1)

            pe.wait_ge(d_st, 16)
            for n in range(3):
                chunk(C_QKV2 + n, (C_QKV2 + n) % 2, 0, ud[0] + n)
                if n < 2:
                    group_sums(n + 1)
            turn_values(1)

            def attention_d(j, par, fill):
                def turn(s, g):
                    pe.wait_ge(d_a, ST * j + (s + 1))
                    if s or g:
                        pe.wait_ge(d_atl, NG * j + (group_index(s) + g))
                    else:
                        pe.wait_ge(d_rs, 3 * j + 2)
                    for n, kb in enumerate(blocks_of(s, g)):
                        last = pe.transpose(PS[:, TB + n * P:TB + (n + 1) * P], dP0[s % 2][:, kb * P:(kb + 1) * P], IDF[:, :])
                    last.then_inc(d_t, 1)

                def scores(s, m):
                    n = (s + 1) * P
                    base = (1 + m) * S
                    pe.wait_ge(free[1 + m], ST * j + (ud[1 + m] + s))
                    score_parts(base, slice(m * HD, (m + 1) * HD), slice(s * P, (s + 1) * P), n, dQH, dQL, dKH, dKL)
                    for c0 in range(0, n, HALF):
                        w = min(HALF, n - c0)
                        last = pe.matmul(PS[:, base + c0:base + c0 + w], IDR[:, :], dBIAS[:, S - n + c0:S - n + c0 + w],
                                         start=False, stop=True)
                    last.then_inc(d_s, 1)

                def values(s):
                    if s:
                        pe.wait_ge(d_o, ST * j + s)
                    pe.wait_ge(d_atl, NG * j + group_index(s + 1))
                    value_sum(s, dVH, dVL, dATH, dATL).then_inc(d_av, 1)

                def pieces(n, half):
                    if half == 0:
                        pe.wait_ge(free[0], 3 * j + (ud[0] + 3 + n))
                    for k in range(4 * half, 4 * half + 4):
                        step(3 * j + (C_QKV2 + 3 + n), (C_QKV2 + 3 * par + 3 + n) % 2, 0, HH, HL, k)

                pe.wait_ge(d_split, j + 1)
                for s in range(ST + 1):
                    if s >= 1:
                        turn(s - 1, 0)
                    if s < ST:
                        scores(s, 0)
                        scores(s, 1)
                    if fill and s in (0, 1, 3, 4, 6, 7):
                        pieces(s // 3, s % 3)
                    if s - 1 >= 4:
                        turn(s - 1, 1)
                    if s >= 1:
                        values(s - 1)
                    if fill and s in (2, 5):
                        group_sums(3 * j + (3 + s // 3))
                if fill:
                    turn_values(j + 2)
                pe.wait_ge(d_sq, 3 * j + (5 if fill else 3))
                for h in (0, HALF):
                    last = pe.matmul(PS[:, 3 * S + h:3 * S + h + HALF], ONES[:, :], dSQ[:, h:h + HALF], start=True, stop=True)
                last.then_inc(d_ss, 1)

            with pe.Fori(0, (KT - 2) // 2) as i:
                for m in range(2):
                    attention_d(2 * i + m, m, True)
            attention_d(KT - 2, 0, True)
            attention_d(KT - 1, 1, False)
            chunks("ab", C_AB, KT, HH, HL, operand=(f_lo, FILL["ab"]))
            chunks("wo", C_WO, KT, GH, GL, operand=(g_lo, KT))
            sum_squares(5 * KT, T[1])

            u = USED["ff"]
            with pe.Fori(0, FFQ) as q:
                for down, (RH, RL) in enumerate(((HH, HL), (GH, GL))):
                    with pe.Fori(0, KT // 2) as i:
                        for m in range(2):
                            s = (C_FF + m) % 2
                            used = i + KT * q + (u[s] + KT // 2 * down)
                            need = None if m else (g_lo, KT * q + 2 * KT) if down else (f_lo, FILL["ffn"])
                            chunk(2 * i + 2 * KT * q + (C_FF + KT * down + m), s, s, used, RH, RL, operand=need)

        @block.scalar
        def _(act):
            links = Links(act, act_link)

            def split_w(c, slot):
                act.wait_ge(ld_w, 16 * c + 16)
                if not (isinstance(c, int) and c == 0):
                    act.wait_ge(chunk_done, c)
                act.activation(WH[slot][:, :], WR0[:, :], ACT.Identity).then_inc(w_hi, 1)

            def root(dst, src, tmp):
                links(act.activation(tmp, src, ACT.Ln, bias=EPSC[:, 0:1], scale=1.0 / D))
                act.activation(dst, tmp, ACT.Exp, scale=-0.5).then_inc(rs, 1)

            def fill_hi(name, shift=None):
                for k in range(KT):
                    act.wait_ge(ftmp, SCALED[name] + k + 1)
                    kw = {} if shift is None else {"bias": col(MOD, shift + k)}
                    act.activation(kt(HH, k), T[2 + k % 2], ACT.Identity, **kw).then_inc(f_hi, 1)

            def operand_hi(times):
                for k in range(KT):
                    act.wait_ge(back[k % 4], 16 * (2 * times + k // 4 + 1))
                    act.activation(kt(HH, k), STG[k % 4][:, :], ACT.Identity).then_inc(f_hi, 1)

            act.wait_ge(ld_c, 48)
            act.activation(SM[:, 0:8], VEC[:, _V["c"]:_V["c"] + 8], ACT.Sigmoid).then_inc(s_sig, 1)
            act.activation(IDR[:, :], IDF[:, :], ACT.Identity)
            act.activation(TRIR[:, :], T[0][:, 0:P], ACT.Identity)
            act.wait_ge(s_const, 1)
            act.wait_ge(ld_x, 16)
            for k in range(KT):
                if k >= 2:
                    act.wait_ge(sq_added, k - 1)
                act.activation(T[2 + k % 2], kt(X, k), ACT.Square).then_inc(sq, 1)
            act.wait_ge(ss, 1)
            root(T[0], PAIR[2], TP)
            act.wait_ge(mod_ready, 1)
            split_w(0, 0)
            fill_hi("a", 0)
            with act.Fori(0, KT) as j:
                split_w(4 * j + 1, 1)
                act.wait_ge(chunk_done, 4 * j + 2)
                act.activation(T[2], PAIR[0], ACT.Identity).then_inc(free[0], 1)
                split_w(4 * j + 2, 0)
                split_w(4 * j + 3, 1)
                split_w(4 * j + 4, 0)
                act.wait_ge(chunk_done, 4 * j + 5)
                act.wait_ge(free[1], 2 * j + 2)
                act.activation(T[2], PAIR[1], ACT.Sigmoid).then_inc(ain_sg, 1)
                act.wait_ge(ain_y, j + 1)
                act.activation(kt(GH, j), T[3], ACT.Identity).then_inc(g_hi, 1)

            def squares_of_new(name, base, added):
                with act.Fori(0, KT // 2) as i:
                    for m in range(2):
                        s = (base + m) % 2
                        split_w(2 * i + (base + m + 1), 1 - s)
                        act.wait_ge(free[s], i + (USED[name][s] + 1))
                        act.wait_ge(sq_added, 2 * i + (added + m - 1))
                        act.activation(T[2 + m], kt(X, 2 * i + m), ACT.Square).then_inc(sq, 1)

            squares_of_new("aout", C_AOUT, KT)
            act.wait_ge(ss, 2)
            root(T[0], PAIR[2], TP)
            act.wait_ge(mod_ready, 2)
            fill_hi("kv", 3 * KT)
            with act.Fori(0, KT) as i:
                split_w(2 * i + (C_KV + 1), 1)
                act.wait_ge(chunk_done, 2 * i + (C_KV + 2))
                act.activation(KST[:, :], PAIR[0], ACT.Identity).then_inc(free[0], 1)
                split_w(2 * i + (C_KV + 2), 0)
                act.wait_ge(chunk_done, 2 * i + (C_KV + 3))
                act.activation(VST[:, :], PAIR[1], ACT.Identity).then_inc(free[1], 1)
                act.wait_ge(st_k, 16 * i + 16)
                act.wait_ge(kv_t, i + 1)

            fill_hi("qz", 5 * KT)
            split_w(C_QZ + 1, 1)
            act.wait_ge(f_lo, FILL["qz"] + KT)
            act.wait_ge(chunk_done, C_QZ + 2)
            act.activation(bQR[:, :], PAIR[0], ACT.Identity).then_inc(free[0], 1)
            split_w(C_QZ + 2, 0)
            act.wait_ge(chunk_done, C_QZ + 3)
            act.activation(bSG[:, :], PAIR[0], ACT.Sigmoid).then_inc(b_sg, 1)

            def halves_b(j):
                act.wait_ge(free[0], 2 * j + (USED["qz"][0] + 1))
                act.activation(bQH[:, :], bQR[:, :], ACT.Identity).then_inc(b_hi, 1)
                act.wait_ge(b_ldk, 16 * j + 16)
                act.activation(bKH[:, :], bKR[:, :], ACT.Identity).then_inc(b_hi, 1)
                act.wait_ge(b_ldv, 16 * j + 16)
                act.activation(bVH[:, :], bVR[:, :], ACT.Identity).then_inc(b_hi, 1)

            halves_b(0)

            def attention_b(j, fill):
                def turned(s, g):
                    bl = blocks_of(s % ST, g)
                    lo, hi = bl[0] * P, (bl[-1] + 1) * P
                    act.wait_ge(b_t, 2 * NG * j + (group_index(s) + g + 1))
                    if s and g == 0:
                        act.wait_ge(b_av, 2 * ST * j + s)
                    act.activation(bATH[:, lo:hi], PS[:, TB:TB + hi - lo], ACT.Identity).then_inc(b_ath, 1)

                for s in range(2 * ST + 2):
                    if s >= 2:
                        turned(s - 2, 0)
                    if s < 2 * ST:
                        n = (s % ST + 1) * P
                        src = PS[:, (1 + s % 2) * S:(1 + s % 2) * S + n]
                        act.wait_ge(b_s, 2 * ST * j + (s + 1))
                        if s >= 2:
                            act.wait_ge(b_a, 2 * ST * j + (s - 1))
                        act.activation(bC[s % 2][:, S - n:S], src, ACT.Sigmoid, scale=-HD ** -0.5).then_inc(b_c, 1)
                        if s >= 3:
                            act.wait_ge(b_t, 2 * NG * j + group_index(s - 2))
                        act.activation(bB[s % 3][:, 0:n], src, ACT.Sigmoid, scale=HD ** -0.5).then_inc(free[1 + s % 2], 1)
                    if s >= 2 and (s - 2) % ST >= 4:
                        turned(s - 2, 1)
                    if fill and s == 1:
                        split_w(2 * j + (C_QZ + 3), 1)
                    if fill and s == 8:
                        act.wait_ge(chunk_done, 2 * j + (C_QZ + 4))
                        act.activation(bQR[:, :], PAIR[0], ACT.Identity).then_inc(free[0], 1)
                        split_w(2 * j + (C_QZ + 4), 0)
                if fill:
                    act.wait_ge(chunk_done, 2 * j + (C_QZ + 5))
                    act.activation(bSG[:, :], PAIR[0], ACT.Sigmoid).then_inc(b_sg, 1)
                    act.wait_ge(b_av, 2 * ST * j + 2 * ST)
                    halves_b(j + 1)

            with act.Fori(0, KT - 1) as j:
                attention_b(j, True)
            attention_b(KT - 1, False)
            operand_hi(0)
            act.wait_ge(f_lo, FILL["y"] + KT)
            with act.Fori(0, KT // 2) as i:
                for m in range(2):
                    s = (C_BOUT + m) % 2
                    split_w(2 * i + (C_BOUT + m + 1), 1 - s)
                    act.wait_ge(free[s], i + (USED["bout"][s] + 1))
                    act.wait_ge(sq_added, 4 * i + (2 * KT + 2 * m))
                    act.activation(T[2], kt(X, 2 * i + m), ACT.Square).then_inc(sq, 1)
                    act.activation(T[3], kt(X, 2 * i + m), ACT.Square, scale=vec("final_g", 2 * i + m)).then_inc(sq, 1)
            act.wait_ge(ss, 4)
            links(act.activation(T[2], PAIR[2], ACT.Ln, bias=EPSC[:, 0:1], scale=1.0 / D))
            links(act.activation(T[1], T[2], ACT.Exp, scale=-0.5))
            act.activation(T[2], T[1], ACT.Square).then_inc(ms2, 1)
            act.wait_ge(ms2, 2)
            links(act.activation(T[3], T[3], ACT.Ln, bias=EPSC[:, 0:1], scale=1.0 / D))
            act.activation(T[2], T[3], ACT.Exp, scale=-0.5).then_inc(rs, 1)
            fill_hi("mix")

            act.wait_ge(p_mx, 1)
            for g in range(4):
                c = C_POOL + g
                split_w(c + 1, (c + 1) % 2)
                act.wait_ge(chunk_done, c + 2)
                act.activation(TP, PAIR[c % 2], ACT.Identity).then_inc(free[c % 2], 1)
                act.wait_ge(p_mx, g + 2)
                act.activation(kt(MXH, g), T[3], ACT.Identity).then_inc(p_mh, 1)
            split_w(C_POOL + 5, (C_POOL + 5) % 2)
            for g in range(4):
                if g < 3:
                    act.wait_ge(p_g, g + 1)
                else:
                    act.wait_ge(chunk_done, C_POOL + 6)
                act.activation(kt(YPH, g), PAIR[g % 2], ACT.Identity, scale=vec("pool_scale", g)).then_inc(p_yh, 1)
            s0, s1 = C_GP % 2, (C_GP + 1) % 2
            with act.Fori(0, KT) as n:
                split_w(2 * n + (C_GP + 1), s1)
                act.wait_ge(chunk_done, 2 * n + (C_GP + 2))
                act.activation(T[1], PAIR[s0], ACT.Sigmoid, bias=vec("b_gate", n)).then_inc(free[s0], 1)
                split_w(2 * n + (C_GP + 2), s0)
                act.wait_ge(free[s1], n + (USED["gp"][s1] + 1))
            with act.Fori(0, KT // 2) as i:
                for m in range(2):
                    s = (C_GA + m) % 2
                    split_w(2 * i + (C_GA + m + 1), 1 - s)
                    act.wait_ge(chunk_done, 2 * i + (C_GA + m + 2))
                    act.activation(T[3], PAIR[s], ACT.Sigmoid, bias=vec("b_gate", 2 * i + (8 + m))).then_inc(free[s], 1)
                    act.wait_ge(ga_st, 32 * i + 16 * (m + 1))

            act.wait_ge(d_lam, 1)
            act.activation(SM[:, 10:12], SM[:, 8:10], ACT.Exp).then_inc(d_lam, 1)
            ud = USED["qkv2"]

            def squares_d(c, raw, roots):
                act.wait_ge(chunk_done, c + 2)
                act.activation(raw[:, :], PAIR[0], ACT.Identity)
                if roots is not None:
                    act.wait_ge(d_rs, roots)
                act.activation(dSQ[:, :], PAIR[0], ACT.Square).then_inc(d_sq, 1)

            def ln_d(src, n, width, done):
                act.wait_ge(d_ss, n)
                act.activation(dSQ[:, :], src, ACT.Ln, bias=EPSC[:, 0:1], scale=1.0 / width).then_inc(done, 1)

            def exp_d():
                act.activation(dRS[:, :], dSQ[:, :], ACT.Exp, scale=-0.5).then_inc(d_rs, 1)

            for n, raw in enumerate((dQR, dKR)):
                split_w(C_QKV2 + n + 1, (C_QKV2 + n + 1) % 2)
                if n == 0:
                    act.wait_ge(d_lam, 3)
                squares_d(C_QKV2 + n, raw, n or None)
                ln_d(PAIR[0], n + 1, HD, free[0])
                act.wait_ge(free[0], ud[0] + n + 1)
                if n:
                    act.wait_ge(d_n, n)
                exp_d()
            split_w(C_QKV2 + 3, (C_QKV2 + 3) % 2)
            act.wait_ge(chunk_done, C_QKV2 + 4)
            act.activation(dVT[:, :], PAIR[0], ACT.Identity).then_inc(d_v, 1)

            def halves_d(j):
                act.wait_ge(d_n, 2 * j + 2)
                act.activation(dQH[:, :], dQR[:, :], ACT.Identity).then_inc(d_hi, 1)
                act.activation(dKH[:, :], dKR[:, :], ACT.Identity).then_inc(d_hi, 1)
                act.wait_ge(d_vt, j + 1)
                act.activation(dVH[:, :], PAIR[0], ACT.Identity).then_inc(d_hi, 1)

            halves_d(0)

            def attention_d(j, par, fill):
                def turned(s, g):
                    bl = blocks_of(s, g)
                    lo, hi = bl[0] * P, (bl[-1] + 1) * P
                    act.wait_ge(d_t, NG * j + (group_index(s) + g + 1))
                    if s and g == 0:
                        act.wait_ge(d_av, ST * j + s)
                    act.activation(dATH[:, lo:hi], PS[:, TB:TB + hi - lo], ACT.Identity).then_inc(d_ath, 1)

                for s in range(ST + 1):
                    if fill and s in (3, 6):
                        n = s // 3 - 1
                        ln_d(PAIR[0], 3 * j + (3 + n), HD, free[0])
                        act.wait_ge(free[0], 3 * j + (ud[0] + 4 + n))
                        if n:
                            act.wait_ge(d_n, 2 * j + 3)
                        exp_d()
                    if s >= 1:
                        turned(s - 1, 0)
                    if s < ST:
                        w = (s + 1) * P
                        act.wait_ge(d_max, ST * j + (s + 1))
                        if s >= 2:
                            act.wait_ge(d_t, NG * j + group_index(s - 1))
                        act.activation(dP0[s % 2][:, 0:w], PS[:, S:S + w], ACT.Exp, bias=SM[:, 2:3],
                                       accum_out=SM[:, 4:5]).then_inc(free[1], 1)
                        act.activation(dP1[:, 0:w], PS[:, 2 * S:2 * S + w], ACT.Exp, bias=SM[:, 3:4],
                                       accum_out=SM[:, 5:6]).then_inc(free[2], 1)
                    if s - 1 >= 4:
                        turned(s - 1, 1)
                    if fill and s in (0, 2, 5):
                        n = {0: 1, 2: 2, 5: 3}[s]
                        if s:
                            squares_d(3 * j + (C_QKV2 + 1 + n), (dQR, dKR)[s // 3], 3 * j + (2 + s // 3))
                        split_w(3 * j + (C_QKV2 + 3 + n), (C_QKV2 + 3 * par + 3 + n) % 2)
                if fill:
                    act.wait_ge(chunk_done, 3 * j + (C_QKV2 + 7))
                    act.activation(dVT[:, :], PAIR[0], ACT.Identity).then_inc(d_v, 1)
                act.wait_ge(d_o, ST * j + ST)
                act.wait_ge(d_rs, 3 * j + (4 if fill else 2))
                act.activation(dSQ[:, :], dOT[:, :], ACT.Square).then_inc(d_sq, 1)
                if fill:
                    halves_d(j + 1)
                ln_d(PAIR[3], 3 * j + (5 if fill else 3), P, d_ln)
                act.wait_ge(d_ln, j + 1)
                act.wait_ge(d_n, 2 * j + (4 if fill else 2))
                exp_d()

            with act.Fori(0, (KT - 2) // 2) as i:
                for m in range(2):
                    attention_d(2 * i + m, m, True)
            attention_d(KT - 2, 0, True)
            attention_d(KT - 1, 1, False)
            operand_hi(1)
            for n in range(KT):
                c = C_AB + n
                split_w(c + 1, (c + 1) % 2)
                act.wait_ge(ab_m, n + 1)
                act.activation(kt(GH, n), T[2 + n % 2], ACT.Identity).then_inc(g_hi, 1)
            squares_of_new("wo", C_WO, 4 * KT)
            act.wait_ge(ss, 5)
            root(T[0], PAIR[2], TP)
            fill_hi("ffn")
            u = USED["ff"]
            with act.Fori(0, FFQ) as q:
                with act.Fori(0, KT // 2) as i:
                    for m in range(2):
                        s = (C_FF + m) % 2
                        split_w(2 * i + 2 * KT * q + (C_FF + m + 1), 1 - s)
                        act.wait_ge(chunk_done, 2 * i + 2 * KT * q + (C_FF + m + 2))
                        act.activation(T[m], PAIR[s], ACT.Relu).then_inc(ff_r, 1)
                        act.wait_ge(free[s], i + KT * q + (u[s] + 1))
                        act.activation(kt(GH, 2 * i + m), T[2 + m], ACT.Identity).then_inc(g_hi, 1)
                with act.Fori(0, KT // 2) as i:
                    for m in range(2):
                        split_w(2 * i + 2 * KT * q + (C_FF + KT + m + 1), 1 - (C_FF + m) % 2)

        @block.vector
        def _(dve):
            links = Links(dve, dve_link)

            def mul_mul(dst, src, scalar, other):
                return dve.scalar_tensor_tensor(out=dst, in0=src, scalar=scalar, in1=other, op0=ALU.mult, op1=ALU.mult)

            def mul_add(dst, src, scalar, other):
                return dve.scalar_tensor_tensor(out=dst, in0=src, scalar=scalar, in1=other, op0=ALU.mult, op1=ALU.add)

            def low(dst, value, high):
                return dve.tensor_tensor(dst, value, high.bitcast(F32), ALU.subtract)

            def add_square(n, acc, src):
                dve.wait_ge(sq, n + 1)
                if not (isinstance(n, int) and n == 0):
                    dve.wait_ge(sq_added, n)
                dve.tensor_tensor(acc, acc, src, ALU.add).then_inc(sq_added, 1)

            def fill_lo(name, n_rs, scale, shift=None):
                dve.wait_ge(rs, n_rs)
                for k in range(KT + 1):
                    if k < KT:
                        if k >= 2:
                            dve.wait_ge(f_lo, FILL[name] + k - 1)
                        mul_mul(T[2 + k % 2], kt(X, k), scale(k), T[0]).then_inc(ftmp, 1)
                    if k:
                        dve.wait_ge(f_hi, FILL[name] + k)
                        hi = kt(HH, k - 1).bitcast(F32)
                        tmp = T[2 + (k - 1) % 2]
                        if shift is None:
                            lo = dve.tensor_tensor(kt(HL, k - 1), tmp, hi, ALU.subtract)
                        else:
                            lo = dve.scalar_tensor_tensor(out=kt(HL, k - 1), in0=tmp, scalar=col(MOD, shift + k - 1),
                                                          in1=hi, op0=ALU.add, op1=ALU.subtract)
                        lo.then_inc(f_lo, 1)

            def operand_lo(name):
                for k in range(KT):
                    dve.wait_ge(f_hi, FILL[name] + k + 1)
                    low(kt(HL, k), STG[k % 4][:, :], kt(HH, k)).then_inc(f_lo, 1)

            def coefficients(a, g, c, done=False):
                ins = dve.scalar_tensor_tensor(out=COEF[:, c:c + KT], in0=MOD[:, a:a + KT], scalar=1.0,
                                               in1=VEC[:, _V[g]:_V[g] + KT], op0=ALU.add, op1=ALU.mult)
                if done:
                    ins.then_inc(mod_ready, 1)

            dve.memset(ONES[:, :], 1.0).then_inc(chunk_done, 1)
            dve.memset(EPSC[:, :], EPS).then_inc(free[0], 1)
            dve.memset(T[1], 0.0).then_inc(free[1], 1)
            dve.memset(TMP[4][:, 0:PADW], 0.0).then_inc(free[2], 1)
            dve.memset(NLAM[:, :], 0.0).then_inc(s_const, 1)
            dve.wait_ge(s_const, 1)
            dve.wait_ge(s_sig, 1)
            dve.tensor_tensor(SC[:, :], VEC[:, _V["c"]:_V["c"] + KT], SM[:, 0:KT], ALU.mult).then_inc(s_sc, 1)
            links(dve.tensor_scalar(GQ8[:, :], vec("gq"), HD ** -0.5, None, ALU.mult))
            links(dve.tensor_scalar(GS8[:, :], vec("gsub"), 1.0 - LAMBDA_INIT, None, ALU.mult))
            for k in range(KT):
                add_square(k, T[1], T[2 + k % 2])
            dve.wait_ge(mod_used, N_MODS_A)
            links(dve.tensor_tensor(MOD[:, 0:N_MODS_A], PS[:, MC:MC + N_MODS_A],
                                    VEC[:, _V["mod_b"]:_V["mod_b"] + N_MODS_A], ALU.add))
            coefficients(KT, "a_g", 0, True)
            dve.wait_ge(mod_ready, 1)
            fill_lo("a", 1, lambda k: col(COEF, k), 0)

            with dve.Fori(0, KT) as j:
                links.round(j, 3)
                dve.wait_ge(free[0], 2 * j + 2)
                dve.wait_ge(chunk_done, 4 * j + 3)
                dve.tensor_tensor(TP, PAIR[1], T[2], ALU.mult).then_inc(free[1], 1)
                dve.wait_ge(free[1], 2 * j + 2)
                links(dve.tensor_scalar(T[3], TP, vec("conv", j + 2 * KT), None, ALU.mult))
                links(mul_add(T[3], TMP[4][:, PADW - 1:PADW - 1 + S], vec("conv", j + KT), T[3]))
                links(mul_add(T[3], TMP[4][:, PADW - 2:PADW - 2 + S], vec("conv", j), T[3]))
                dve.wait_ge(chunk_done, 4 * j + 4)
                dve.tensor_tensor(T[3], PAIR[0], T[3], ALU.mult).then_inc(free[0], 1)
                dve.wait_ge(ain_sg, j + 1)
                dve.tensor_tensor(T[2], PAIR[1], T[2], ALU.mult).then_inc(free[1], 1)
                dve.wait_ge(free[0], 2 * j + 3)
                dve.wait_ge(free[1], 2 * j + 3)
                dve.tensor_tensor(T[3], T[3], T[2], ALU.mult).then_inc(ain_y, 1)
                dve.wait_ge(g_hi, j + 1)
                low(kt(GL, j), T[3], kt(GH, j)).then_inc(g_lo, 1)
            links.end(KT)

            def new_residual(name, base, gate, added):
                links(dve.memset(T[1], 0.0))
                with dve.Fori(0, KT // 2) as i:
                    for m in range(2):
                        s = (base + m) % 2
                        dve.wait_ge(chunk_done, 2 * i + (base + m + 2))
                        x = kt(X, 2 * i + m)
                        if gate is None:
                            dve.tensor_tensor(x, PAIR[s], x, ALU.add).then_inc(free[s], 1)
                        else:
                            mul_add(x, PAIR[s], col(MOD, 2 * i + (gate + m)), x).then_inc(free[s], 1)
                        add_square(2 * i + (added + m), T[1], T[2 + m])

            new_residual("aout", C_AOUT, 2 * KT, KT)
            dve.wait_ge(mod_used, N_MODS)
            links(dve.tensor_tensor(MOD[:, N_MODS_A:], PS[:, MC + N_MODS_A:MC + N_MODS],
                                    VEC[:, _V["mod_b"] + N_MODS_A:_V["mod_b"] + N_MODS], ALU.add))
            coefficients(4 * KT, "kv_g", KT)
            coefficients(6 * KT, "b_g", 2 * KT, True)
            dve.wait_ge(mod_ready, 2)
            fill_lo("kv", 2, lambda k: col(COEF, KT + k), 3 * KT)
            with dve.Fori(0, KT) as i:
                dve.wait_ge(kv_t, i + 1)
                dve.tensor_copy(VTT[:, :], PAIR[2]).then_inc(free[2], 1)
                dve.wait_ge(st_v, 16 * i + 16)
            fill_lo("qz", 2, lambda k: col(COEF, 2 * KT + k), 5 * KT)

            dve.wait_ge(f_lo, FILL["qz"] + KT)
            for c in bC:
                links(dve.memset(c[:, S:S + 1], 1.0))

            def halves_b(j):
                dve.wait_ge(b_hi, 3 * j + 1)
                low(bQL[:, :], bQR[:, :], bQH[:, :])
                dve.wait_ge(b_hi, 3 * j + 2)
                low(bKL[:, :], bKR[:, :], bKH[:, :])
                dve.wait_ge(b_hi, 3 * j + 3)
                low(bVL[:, :], bVR[:, :], bVH[:, :]).then_inc(b_split, 1)

            dve.wait_ge(b_sg, 1)
            dve.tensor_tensor(bZS[:, :], PAIR[0], bSG[:, :], ALU.mult).then_inc(free[0], 1)
            halves_b(0)

            def attention_b(j, fill):
                def turned(s, g):
                    bl = blocks_of(s % ST, g)
                    lo, hi = bl[0] * P, (bl[-1] + 1) * P
                    dve.wait_ge(b_ath, 2 * NG * j + (group_index(s) + g + 1))
                    low(bATL[:, lo:hi], PS[:, TB:TB + hi - lo], bATH[:, lo:hi]).then_inc(b_atl, 1)

                for s in range(2 * ST + 3):
                    if s >= 3:
                        rows = slice((s - 3) // ST * HD, ((s - 3) // ST + 1) * HD)
                        t = (s - 3) % ST
                        dve.wait_ge(b_av, 2 * ST * j + (s - 2))
                        dve.tensor_tensor(bYO[rows, t * P:(t + 1) * P], PS[rows, OB:OB + P], bZS[rows, t * P:(t + 1) * P],
                                          ALU.mult).then_inc(b_o, 1)
                    if 2 <= s < 2 * ST + 2:
                        turned(s - 2, 0)
                    if s < 2 * ST:
                        n = (s % ST + 1) * P
                        dve.wait_ge(b_c, 2 * ST * j + (s + 1))
                        c = bC[s % 2][:, S - n:S]
                        dve.tensor_tensor_scan(c[:, ::-1], c[:, ::-1], c[:, ::-1], 1.0, ALU.mult, ALU.bypass).then_inc(b_scan, 1)
                    if 2 <= s < 2 * ST + 2 and (s - 2) % ST >= 4:
                        turned(s - 2, 1)
                if fill:
                    dve.wait_ge(b_sg, j + 2)
                    dve.wait_ge(b_o, 2 * ST * (j + 1))
                    dve.tensor_tensor(bZS[:, :], PAIR[0], bSG[:, :], ALU.mult).then_inc(free[0], 1)
                    halves_b(j + 1)
                    dve.wait_ge(b_st, 16 * j + 16)

            with dve.Fori(0, KT - 1) as j:
                attention_b(j, True)
            attention_b(KT - 1, False)
            operand_lo("y")
            dve.wait_ge(f_lo, FILL["y"] + KT)
            links(dve.memset(T[1], 0.0))
            links(dve.memset(TP, 0.0))
            with dve.Fori(0, KT // 2) as i:
                for m in range(2):
                    s = (C_BOUT + m) % 2
                    dve.wait_ge(chunk_done, 2 * i + (C_BOUT + m + 2))
                    x = kt(X, 2 * i + m)
                    mul_add(x, PAIR[s], col(MOD, 2 * i + (7 * KT + m)), x).then_inc(free[s], 1)
                    add_square(4 * i + (2 * KT + 2 * m), T[1], T[2])
                    add_square(4 * i + (2 * KT + 2 * m + 1), TP, T[3])
            dve.wait_ge(ms2, 1)
            dve.tensor_tensor(T[3], PAIR[3], T[2], ALU.mult).then_inc(ms2, 1)
            dve.wait_ge(rs, 3)
            links(dve.tensor_tensor(T[0], T[1], T[2], ALU.mult))
            links(dve.tensor_tensor(COEF[:, 3 * KT:], VEC[:, _V["final_g"]:_V["final_g"] + KT],
                                    VEC[:, _V["mix_g"]:_V["mix_g"] + KT], ALU.mult))
            fill_lo("mix", 3, lambda k: col(COEF, 3 * KT + k))
            for k in range(KT):
                mul_mul(kt(X, k), kt(X, k), vec("final_g", k), T[1])

            links(dve.memset(TMP[0][:, 0:PADW], 0.0))
            links(dve.memset(TMP[1][:, 0:PADW], 0.0))
            dve.memset(TMP[4][:, 0:PADW], 0.0).then_inc(p_mx, 1)
            for g, w in enumerate(POOL_W):
                c = C_POOL + g
                dve.wait_ge(free[c % 2], USED["pool"][c % 2] + g // 2 + 1)
                cur, sh = TMP[4], 1
                while sh < w:
                    dst = TMP[1] if cur is not TMP[1] else TMP[0]
                    links(dve.tensor_tensor(dst[:, PADW:], cur[:, PADW:], cur[:, PADW - sh:PADW - sh + S], ALU.add))
                    cur, sh = dst, 2 * sh
                e = _V["edge"] + PADW * g
                links(dve.tensor_tensor(cur[:, PADW:2 * PADW], cur[:, PADW:2 * PADW], VEC[:, e:e + PADW], ALU.mult))
                dve.scalar_tensor_tensor(out=T[3], in0=cur[:, PADW:], scalar=1.0 / w, in1=TP,
                                         op0=ALU.mult, op1=ALU.subtract).then_inc(p_mx, 1)
                dve.wait_ge(p_mh, g + 1)
                low(kt(MXL, g), T[3], kt(MXH, g)).then_inc(p_ml, 1)
            for g in range(4):
                dve.wait_ge(p_yh, g + 1)
                dve.scalar_tensor_tensor(out=kt(YPL, g), in0=PAIR[g % 2], scalar=vec("pool_scale", g),
                                         in1=kt(YPH, g).bitcast(F32), op0=ALU.mult, op1=ALU.subtract).then_inc(p_yl, 1)
            s0, s1 = C_GP % 2, (C_GP + 1) % 2
            with dve.Fori(0, KT) as n:
                dve.wait_ge(free[s0], n + (USED["gp"][s0] + 1))
                dve.wait_ge(chunk_done, 2 * n + (C_GP + 3))
                dve.tensor_tensor(T[2], PAIR[s1], T[1], ALU.mult).then_inc(free[s1], 1)
                dve.wait_ge(gp_st, 16 * n + 16)

            dve.wait_ge(d_ld, 32)
            links(dve.tensor_tensor(dSQ[:, 0:HD], dVT[:, 0:HD], dVT[:, HD:2 * HD], ALU.mult))
            links(dve.tensor_tensor(dSQ[:, HD:2 * HD], dVT[:, 2 * HD:3 * HD], dVT[:, 3 * HD:4 * HD], ALU.mult))
            dve.reduce_sum(SM[:, 8:9], dSQ[:, 0:HD], AX_X)
            dve.reduce_sum(SM[:, 9:10], dSQ[:, HD:2 * HD], AX_X).then_inc(d_lam, 1)
            dve.wait_ge(d_lam, 2)
            links(mul_add(NLAM[:, :], SM[:, 10:11], -1.0, SM[:, 11:12]))
            dve.tensor_scalar(NLAM[:, :], NLAM[:, :], -LAMBDA_INIT, None, ALU.add).then_inc(d_lam, 1)

            def norm_d(raw, gain, n):
                dve.wait_ge(d_rs, n)
                mul_mul(raw[:, :], raw[:, :], gain, dRS[:, :]).then_inc(d_n, 1)

            def halves_d(j):
                dve.wait_ge(d_hi, 3 * j + 1)
                low(dQL[:, :], dQR[:, :], dQH[:, :])
                dve.wait_ge(d_hi, 3 * j + 2)
                low(dKL[:, :], dKR[:, :], dKH[:, :])
                dve.wait_ge(d_hi, 3 * j + 3)
                low(dVL[:, :], PAIR[0], dVH[:, :]).then_inc(free[0], 1)
                dve.tensor_scalar(dBIAS[:, :], dDIST[:, :], vec("slope", j), None, ALU.mult).then_inc(d_split, 1)

            norm_d(dQR, GQ8[:, 0:1], 1)
            norm_d(dKR, vec("gk"), 2)
            halves_d(0)
            ud = USED["qkv2"]

            def attention_d(j, fill):
                def turned(s, g):
                    bl = blocks_of(s, g)
                    lo, hi = bl[0] * P, (bl[-1] + 1) * P
                    dve.wait_ge(d_ath, NG * j + (group_index(s) + g + 1))
                    low(dATL[:, lo:hi], PS[:, TB:TB + hi - lo], dATH[:, lo:hi]).then_inc(d_atl, 1)

                for s in range(ST + 1):
                    n = (s + 1) * P
                    if s >= 1:
                        turned(s - 1, 0)
                    if s < ST:
                        dve.wait_ge(d_s, 2 * ST * j + (2 * s + 1))
                        dve.reduce_max(SM[:, 0:1], PS[:, S:S + n], AX_X)
                        dve.wait_ge(d_s, 2 * ST * j + (2 * s + 2))
                        links(dve.reduce_max(SM[:, 1:2], PS[:, 2 * S:2 * S + n], AX_X))
                        dve.tensor_scalar(SM[:, 2:4], SM[:, 0:2], -1.0, None, ALU.mult).then_inc(d_max, 1)
                    if s - 1 >= 4:
                        turned(s - 1, 1)
                    if s >= 1:
                        dve.wait_ge(d_av, ST * j + s)
                        dve.tensor_copy(dOT[:, (s - 1) * P:s * P], PS[:, OB:OB + P]).then_inc(d_o, 1)
                    if s < ST:
                        dve.wait_ge(free[1], ST * j + (ud[1] + s + 1))
                        dve.wait_ge(free[2], ST * j + (ud[2] + s + 1))
                        links(dve.reciprocal(SM[:, 6:8], SM[:, 4:6]))
                        links(dve.tensor_scalar(SM[:, 8:9], SM[:, 7:8], NLAM[:, 0:1], None, ALU.mult))
                        links(dve.tensor_scalar(dP1[:, 0:n], dP1[:, 0:n], SM[:, 8:9], None, ALU.mult))
                        mul_add(dP0[s % 2][:, 0:n], dP0[s % 2][:, 0:n], SM[:, 6:7], dP1[:, 0:n]).then_inc(d_a, 1)
                    if fill and s == 3:
                        norm_d(dQR, GQ8[:, 0:1], 3 * j + 3)
                    if fill and s == 6:
                        norm_d(dKR, vec("gk"), 3 * j + 4)
                if fill:
                    halves_d(j + 1)
                dve.wait_ge(d_rs, 3 * j + (5 if fill else 3))
                dve.wait_ge(d_st, 16 * j + 16)
                mul_mul(dYO[:, :], dOT[:, :], GS8[:, 0:1], dRS[:, :]).then_inc(d_yo, 1)

            with dve.Fori(0, KT - 1) as j:
                links.round(j, 4 * ST)
                attention_d(j, True)
            links.end(KT - 1)
            attention_d(KT - 1, False)
            operand_lo("ab")
            for n in range(KT):
                s = (C_AB + n) % 2
                gate, part = T[n % 2], T[2 + n % 2]
                dve.wait_ge(chunk_done, C_AB + n + 2)
                dve.wait_ge(ab_ld[n % 2], 32 * (n // 2 + 1))
                dve.tensor_tensor(gate, PAIR[s], gate, ALU.mult).then_inc(free[s], 1)
                dve.wait_ge(free[s], USED["ab"][s] + n // 2 + 1)
                dve.tensor_tensor(part, part, gate, ALU.add).then_inc(ab_m, 1)
                dve.wait_ge(g_hi, KT + n + 1)
                low(kt(GL, n), part, kt(GH, n)).then_inc(g_lo, 1)
            new_residual("wo", C_WO, None, 4 * KT)
            fill_lo("ffn", 4, lambda k: vec("ffn_g", k))
            with dve.Fori(0, FFQ) as q:
                with dve.Fori(0, KT // 2) as i:
                    for m in range(2):
                        s = (C_FF + m) % 2
                        dve.wait_ge(ff_r, 2 * i + KT * q + (m + 1))
                        dve.scalar_tensor_tensor(out=T[2 + m], in0=PAIR[s], scalar=0.0, in1=T[m],
                                                 op0=ALU.max, op1=ALU.mult).then_inc(free[s], 1)
                        dve.wait_ge(g_hi, 2 * i + KT * q + (2 * KT + m + 1))
                        low(kt(GL, 2 * i + m), T[2 + m], kt(GH, 2 * i + m)).then_inc(g_lo, 1)
                with dve.Fori(0, KT // 2) as i:
                    for m in range(2):
                        s = (C_FF + m) % 2
                        dve.wait_ge(chunk_done, 2 * i + 2 * KT * q + (C_FF + KT + m + 2))
                        x = kt(X, 2 * i + m)
                        dve.tensor_tensor(x, PAIR[s], x, ALU.add).then_inc(free[s], 1)

        @block.gpsimd
        def _(pool):
            def split_w(c, slot):
                pool.wait_ge(w_hi, c + 1)
                pool.tensor_tensor(WL[slot][:, :], WR0[:, :], WH[slot][:, :].bitcast(F32), ALU.subtract).then_inc(w_lo, 1)

            last = C_QZ + 3
            with pool.Fori(0, last // 2) as i:
                for m in range(2):
                    split_w(2 * i + m, m)
            split_w(last - 1, (last - 1) % 2)

            u = USED["qz"]

            def attention_b(j, fill):
                for s in range(2 * ST):
                    n = (s % ST + 1) * P
                    pool.wait_ge(b_scan, 2 * ST * j + (s + 1))
                    pool.wait_ge(free[1 + s % 2], ST * j + (u[1 + s % 2] + s // 2 + 1))
                    b = bB[s % 3][:, 0:n]
                    pool.tensor_tensor(b, b, bC[s % 2][:, S - n + 1:S + 1], ALU.mult).then_inc(b_a, 1)
                    if fill and s == 1:
                        split_w(2 * j + (C_QZ + 3), 1)
                    if fill and s == 8:
                        split_w(2 * j + (C_QZ + 4), 0)

            with pool.Fori(0, KT - 1) as j:
                attention_b(j, True)
            attention_b(KT - 1, False)
            last = N_CHUNKS + 1
            first = C_BOUT + 1
            with pool.Fori(0, (last - first) // 2) as i:
                for m in range(2):
                    split_w(2 * i + (first + m), (first + m) % 2)
            if (last - first) % 2:
                split_w(last - 1, (last - 1) % 2)


def _chunks(w):
    k, n = w.shape
    a = np.zeros((n // P, P, KT, P), w.dtype)
    a[:, :, :k // P] = w.reshape(k // P, P, n // P, P).transpose(2, 1, 0, 3)
    return a.reshape(n // P, P, D)


def _columns(v):
    return np.asarray(v).reshape(-1, P).T


def kernel(**inputs):
    import concourse.bacc as _bacc
    from concourse.bass_utils import run_bass_kernel_spmd as _run

    f = {k: np.asarray(v) for k, v in inputs.items()}
    ain, kv, qz = _chunks(f["a_w_in"][0]), _chunks(f["w_kv"]), _chunks(f["b_w_qz"][0])
    win, gate = _chunks(f["w_in_2"][0]), _chunks(f["w_gate_2"][0])
    grp = np.zeros((1, P, D), np.float32)
    grp[0, :, 0:4 * P] = f["w_pool_grp_2"][0].transpose(1, 0, 2).reshape(P, 4 * P)
    branch = _chunks(f["w_branch_pool_2"][0])
    up, down = _chunks(f["w_up_2"][0]), f["w_down_2"][0]
    parts = []
    for j in range(KT):
        parts += [ain[KT + j], ain[2 * KT + j], ain[j], ain[3 * KT + j]]
    parts += list(_chunks(f["a_w_out"][0]))
    for j in range(KT):
        parts += [kv[j], kv[KT + j]]
    for j in range(KT):
        parts += [qz[j], qz[KT + j]]
    parts += list(_chunks(f["b_w_out"][0]))
    parts += list(win[0:4]) + [grp[0]]
    for j in range(KT):
        parts += [gate[j], branch[j]]
    parts += list(gate[KT:])
    for j in range(KT):
        parts += [win[4 + j], win[4 + KT + j], win[4 + 2 * KT + j]]
    parts += list(_chunks(f["w_branch_attn_2"][0])) + list(_chunks(f["w_out_2"][0]))
    for q in range(FFQ):
        parts += list(up[q * KT:(q + 1) * KT]) + list(_chunks(down[q * D:(q + 1) * D]))
    parts.append(np.zeros((P, D), np.float32))
    assert len(parts) == N_CHUNKS + 1
    wst = np.stack(parts)
    mods = np.concatenate([_chunks(f["a_mod_w"][0]), _chunks(f["kv_mod_w"]), _chunks(f["b_mod_w"][0])])

    edge = np.ones((4, PADW), np.float32)
    for g, w in enumerate(POOL_W):
        edge[g, :w] = w / np.arange(1, w + 1)
    two = lambda v: np.concatenate([v, v])
    cols = {
        "c": f["c"], "mod_b": np.concatenate([f["a_mod_b"][0], f["kv_mod_b"], f["b_mod_b"][0]]),
        "a_g": f["a_norm_g"], "kv_g": f["kv_norm_g"], "b_g": f["b_norm_g"], "conv": f["a_conv_w"][0],
        "final_g": f["final_norm_g"], "mix_g": f["g_mix_2"], "pool_scale": f["pool_scale_2"],
        "gq": two(f["g_q_2"][0]), "gk": two(f["g_k_2"][0]), "gsub": f["g_sub_2"], "b_gate": f["b_gate_2"],
        "ffn_g": f["g_ffn_2"],
    }
    vecs = np.zeros((P, NV), np.float32)
    for name, v in cols.items():
        v = _columns(v)
        vecs[:, _V[name]:_V[name] + v.shape[1]] = v
    vecs[:, _V["slope"]:_V["slope"] + KT] = 2.0 ** -np.arange(1.0, KT + 1)
    vecs[:, _V["edge"]:_V["edge"] + 4 * PADW] = edge.reshape(-1)

    q, k = np.arange(P)[:, None], np.arange(P)[None, :]
    rel = np.arange(S)[None, :] - (S - P)
    consts = np.zeros((P, NC_), np.float32)
    consts[:, K_ID:K_ID + P] = np.eye(P)
    consts[:, K_TRI:K_TRI + P] = np.where(k >= q, -BIG, 0.0)
    consts[:, K_BD:K_BD + P] = q // HD == k // HD
    consts[:, K_DIST:K_DIST + S] = np.where(np.floor_divide(rel, 64) <= q // 64, -np.abs(q - rel), -BIG)
    consts[:, K_LAM:] = f["lambda_qk_2"].reshape(1, 4 * HD)

    xt = f["x"][0].T.reshape(KT, P, S).transpose(1, 0, 2).reshape(P, KT * S)

    nc = _bacc.Bacc("TRN2", target_bir_lowering=False, num_devices=1)
    arrays = {n: np.ascontiguousarray(a, np.float32) for n, a in
              (("xt", xt), ("vecs", vecs), ("consts", consts), ("mods", mods), ("wst", wst))}
    args = [nc.dram_tensor(n, a.shape, F32, kind="ExternalInput").ap() for n, a in arrays.items()]
    out = nc.dram_tensor("out", [KT, P, S], F32, kind="ExternalOutput").ap()
    block_kernel(nc, *args, out)
    r = _run(nc, [arrays], core_ids=[0])
    return r.results[0]["out"].reshape(D, S).T.reshape(1, S, D)
```

```python
from contextlib import ExitStack

import numpy as np

import concourse.bass as bass
from concourse import mybir

F32 = mybir.dt.float32
F32R = mybir.dt.float32r
ALU = mybir.AluOpType
ACT = mybir.ActivationFunctionType
AX_X = mybir.AxisListType.X
ds = bass.ds

P = 128
D = 1024
S = 1024
KT = D // P
ST = S // P
HALF = 512
DFF = 4 * D
FFQ = DFF // D
EPS = 1e-6
HD = 64
BIG = 2.0 ** 100

C_AIN = 0
C_AOUT = C_AIN + 4 * KT
C_KV = C_AOUT + KT
C_QZ = C_KV + 2 * KT
C_BOUT = C_QZ + 2 * KT
C_POOL = C_BOUT + KT
C_GP = C_POOL + 5
C_GA = C_GP + 2 * KT
C_QKV2 = C_GA + KT
C_AB = C_QKV2 + 3 * KT
C_WO = C_AB + KT
C_FF = C_WO + KT
N_CHUNKS = C_FF + FFQ * 2 * KT
N_MODS_A = 2 * KT
N_MODS = 8 * KT
MODS_J = (N_MODS - N_MODS_A) // KT

_V = {}
_n = 0
for _name, _w in (("mod_b", 64), ("a_g", 8), ("kv_g", 8), ("b_g", 8), ("conv", 24),
                  ("final_g", 8), ("mix_g", 8), ("pool_scale", 4), ("gq", 1), ("gk", 1),
                  ("gsub", 1), ("b_gate", 16), ("ffn_g", 8), ("slope", 8), ("edge", 64)):
    _V[_name] = _n
    _n += _w
NV = _n
K_ID, K_TRI, K_BD, K_DIST, K_LAM = 0, 128, 256, 384, 384 + S
NC_ = K_LAM + 4 * HD
POOL_W = (2, 4, 8, 16)
PADW = 16
LAMBDA_INIT = 0.2


_USES = (("ain", 16, 16, 0), ("aout", 4, 4, 0), ("kv", 8, 8, 8), ("qz", 16, 64, 64),
         ("bout", 4, 4, 0), ("pool", 2, 2, 0), ("gp", 8, 8, 0), ("ga", 4, 4, 0),
         ("qkv2", 32, 64, 64), ("ab", 4, 4, 0), ("wo", 4, 4, 0), ("ff", 32, 32, 0))
USED = {}
_at = (1, 1, 1)
for _name, *_k in _USES:
    USED[_name] = _at
    _at = tuple(x + y for x, y in zip(_at, _k))

FILL = {name: KT * n for n, name in enumerate(("a", "kv", "qz", "y", "mix", "ab", "ffn"))}
SCALED = {name: KT * n for n, name in enumerate(("a", "kv", "qz", "mix", "ffn"))}


class Links:

    def __init__(self, eng, sem):
        self.eng, self.sem, self.n = eng, sem, 0
        self.i = self.per = self.k = None

    def round(self, i, per):
        self.i, self.per, self.k = i, per, 0

    def end(self, rounds):
        assert self.k == self.per, (self.k, self.per)
        self.n += self.per * rounds
        self.i = None

    def __call__(self, ins):
        ins.then_inc(self.sem, 1)
        if self.i is None:
            self.n += 1
            self.eng.wait_ge(self.sem, self.n)
        else:
            self.k += 1
            self.eng.wait_ge(self.sem, self.i * self.per + (self.n + self.k))


def blocks_of(t, g):
    return range(4 * g, min(t + 1, 4 * g + 4))


GROUPS = np.cumsum([len(range(0, t + 1, 4)) for t in range(ST)]).tolist()
NG = GROUPS[-1]
D_STEPS = (0, 2, 3, 3, 3, 5, 3, 5)
GROUP_BLOCKS = [[blocks_of(t, g) for g in range(1 + t // 4)] for t in range(ST)]
B_STEPS = (2, 2, 1, 1, 1, 1, 0, 0) * 2


def group_index(s):
    return NG * (s // ST) + (GROUPS[s % ST - 1] if s % ST else 0)



def block_kernel(nc, xt, cb, vecs, consts, mods, wst, out):
    with ExitStack() as ctx:
        def sem(name):
            return ctx.enter_context(nc.semaphore(name))

        at = [nc.sbuf_base]

        def place(name, cols, dt=F32, where=at):
            where[0] = (where[0] + 31) // 32 * 32
            t = nc.alloc_sbuf_tensor_at(name, [P, cols], dt, offset=where[0])
            where[0] += cols * 4
            assert where[0] <= nc.sbuf_usable_end, (name, where[0] - nc.sbuf_usable_end)
            return t

        X_AT = at[0]
        X = place("X", KT * S)
        HH = place("HH", KT * S, F32R)
        HL = place("HL", KT * S, F32R)
        WR0 = place("WR0", D)
        WH = [place(f"WH{i}", D, F32R) for i in range(2)]
        WL = [place(f"WL{i}", D, F32R) for i in range(2)]
        VEC = place("VEC", NV)
        at[0] = (at[0] + 31) // 32 * 32
        MOD_AT = at[0]
        MOD = place("MOD", N_MODS)
        COEF = place("COEF", 4 * KT + 32)
        IDF = place("IDF", P)
        IDR = place("IDR", P, F32R)
        TRIR = place("TRIR", P, F32R)
        ONES = place("ONES", P)
        SM = place("SM", 16)
        EPSC = place("EPSC", 1)
        NLAM = place("NLAM", 1)
        GQ8 = place("GQ8", 1)
        GS8 = place("GS8", 1)
        ATT0 = at[0]
        TMP = [place(f"TMP{i}", S + (0 if i in (2, 3) else PADW)) for i in range(5)]
        T = [t[:, 0:S] for t in TMP]
        TP = TMP[4][:, PADW:]
        SCR0 = at[0]
        CB = T[1]
        MRAW = nc.alloc_sbuf_tensor_at("MRAW", [P, 2 * KT * D], F32, offset=(SCR0 + 31) // 32 * 32)
        MR = T[0]
        GH = place("GH", KT * S, F32R)
        GL = place("GL", KT * S, F32R)
        r = [SCR0]
        KSH, KSL, VSH, VSL = (place(n, S, F32R, r) for n in ("KSH", "KSL", "VSH", "VSL"))
        VST = place("VST", S, F32, r)
        r = [SCR0]
        YPH = place("YPH", 4 * S, F32R, r)
        YPL = place("YPL", 4 * S, F32R, r)
        MXH = place("MXH", 4 * S, F32R, r)
        MXL = place("MXL", 4 * S, F32R, r)
        r = [ATT0]
        bQH, bQL = ([place(f"b{n}{i}", S, F32R, r) for i in range(2)] for n in ("QH", "QL"))
        bZS = [place(f"bZS{i}", S, F32, r) for i in range(2)]
        bKH, bKL, bVH, bVL = ([place(f"b{n}{i}", S, F32R, r) for i in range(2)] for n in ("KH", "KL", "VH", "VL"))
        bC = [place(f"bC{i}", S + 8, F32, r) for i in range(2)]
        bB = [place(f"bB{i}", S, F32, r) for i in range(4)]
        XAT = (X_AT + 31) // 32 * 32
        ATH = [nc.alloc_sbuf_tensor_at(f"ATH{i}", [P, 2 * S], F32R, offset=XAT + 8 * S * i) for i in range(2)]
        ATL = [nc.alloc_sbuf_tensor_at(f"ATL{i}", [P, 2 * S], F32R, offset=XAT + 8 * S * (2 + i)) for i in range(2)]
        r = [ATT0]
        STG = [place(f"STG{i}", S, F32, r) for i in range(4)]
        r = [ATT0]
        ATT = (ATT0 + 31) // 32 * 32
        dQH, dQL, dKH, dKL, dVH, dVL = ([place(f"d{n}{i}", S, F32R, r) for i in range(2)]
                                        for n in ("QH", "QL", "KH", "KL", "VH", "VL"))
        raw_at = [[ATT + (2 * n + i) * 4 * S for i in range(2)] for n in (1, 3, 5)]
        dQR, dKR, dVR = ([nc.alloc_sbuf_tensor_at(f"d{n}{i}", [P, S], F32, offset=a[i]) for i in range(2)]
                         for n, a in zip(("QR", "KR", "VR"), raw_at))
        dSQ, dRS, dP1 = (place("d" + n, S, F32, r) for n in ("SQ", "RS", "P1"))
        dOT = [place(f"dOT{i}", S, F32, r) for i in range(2)]
        dP0 = [place(f"dP0{i}", S, F32, r) for i in range(2)]
        dDIST = place("dDIST", S, F32R, r)
        dSL = [IDR, TRIR]
        r = [MOD_AT]
        dBD = place("dBD", P, F32, r)
        PS = ctx.enter_context(nc.psum_tensor("PS", [P, 8 * HALF], F32))
        PAIR = [PS[:, p * S:(p + 1) * S] for p in range(4)]
        TB = 3 * S
        OB = 3 * S + HALF

        def scratch(name):
            return nc.dram_tensor(name, [KT, P, S], F32, kind="Internal").ap()

        k_hi, k_lo, v_hi, v_lo = (scratch(n) for n in ("k_hi", "k_lo", "v_hi", "v_lo"))
        y_b, m_p, g_a, y_d, x_b, x_d = (scratch(n) for n in ("y_b", "m_p", "g_a", "y_d", "x_b", "x_d"))

        def at_blocks(t, r, lo, hi):
            return t[:, :].rearrange("p (k r q) -> p k r q", r=2, q=P)[:, lo:hi, r, :]

        def turned_blocks(n):
            return PS[:, TB:TB + n * P].rearrange("p (k q) -> p k q", q=P)

        def row(t, i):
            return t[i] if isinstance(i, int) else t[ds(i, 1)].rearrange("a p c -> (a p) c")

        def kt(t, i):
            return t[:, i * S:(i + 1) * S] if isinstance(i, int) else t[:, ds(i * S, S)]

        def col(t, i):
            return t[:, i:i + 1] if isinstance(i, int) else t[:, ds(i, 1)]

        def vec(name, i=0):
            return col(VEC, i + _V[name])

        ld_c = sem("ld_c")
        ld_cb = sem("ld_cb")
        ld_x = [sem(f"ld_x{i}") for i in range(4)]
        ld_ma = [sem(f"ld_ma{i}") for i in range(4)]
        ld_mod = sem("ld_mod")
        mod_done = sem("mod_done")
        ld_w = sem("ld_w")
        w_hi = sem("w_hi")
        w_lo = sem("w_lo")
        chunk_done = sem("chunk_done")
        free = [sem(f"free{p}") for p in range(3)]
        dve_link = sem("dve_link")
        act_link = sem("act_link")
        s_sig = sem("s_sig")
        s_sc = sem("s_sc")
        s_const = sem("s_const")
        mod_ready = sem("mod_ready")
        sq = sem("sq")
        sq_added = sem("sq_added")
        ss = sem("ss")
        rs = sem("rs")
        ms2 = sem("ms2")
        ftmp = sem("ftmp")
        f_hi = sem("f_hi")
        f_lo = sem("f_lo")
        g_hi = sem("g_hi")
        g_lo = sem("g_lo")
        back = [sem(f"back{i}") for i in range(4)]
        ain_sg = sem("ain_sg")
        ain_y = sem("ain_y")
        kv_t = sem("kv_t")
        kv_kh = sem("kv_kh")
        kv_vh = sem("kv_vh")
        st_k = sem("st_k")
        st_v = sem("st_v")
        b_ld = sem("b_ld")
        b_sg = sem("b_sg")
        b_qh = sem("b_qh")
        b_s = sem("b_s")
        b_c = sem("b_c")
        b_scan = sem("b_scan")
        b_a = sem("b_a")
        b_t = sem("b_t")
        b_ath = sem("b_ath")
        b_atl = sem("b_atl")
        b_av = sem("b_av")
        b_o = sem("b_o")
        b_st = sem("b_st")
        p_mx = sem("p_mx")
        p_mh = sem("p_mh")
        p_ml = sem("p_ml")
        p_g = sem("p_g")
        p_yh = sem("p_yh")
        p_yl = sem("p_yl")
        gp_st = sem("gp_st")
        ga_st = sem("ga_st")
        d_ld = sem("d_ld")
        d_lam = sem("d_lam")
        d_sq = sem("d_sq")
        d_ss = sem("d_ss")
        d_rs = sem("d_rs")
        d_n = sem("d_n")
        d_v = sem("d_v")
        d_vt = sem("d_vt")
        d_hi = sem("d_hi")
        d_split = sem("d_split")
        d_s = sem("d_s")
        d_max = sem("d_max")
        d_a = sem("d_a")
        d_t = sem("d_t")
        d_ath = sem("d_ath")
        d_atl = sem("d_atl")
        d_av = sem("d_av")
        d_o = sem("d_o")
        d_st = sem("d_st")
        ab_ld = [sem(f"ab_ld{i}") for i in range(2)]
        ab_m = sem("ab_m")
        ff_r = sem("ff_r")
        st_out = sem("st_out")
        st_x = sem("st_x")
        ld_xr = sem("ld_xr")
        x_new = sem("x_new")

        block = ctx.enter_context(nc.Block())

        @block.sync
        def _(sp):
            def load_w(c):
                sp.wait_ge(w_lo, c)
                sp.dma_start(WR0[:, :], row(wst, c)).then_inc(ld_w, 16)

            sp.dma_start(CB, cb).then_inc(ld_cb, 16)
            sp.dma_start(VEC[:, :], vecs).then_inc(ld_c, 16)
            for g in range(4):
                sp.dma_start(X[:, 2 * g * S:2 * (g + 1) * S], xt[:, 2 * g * S:2 * (g + 1) * S]).then_inc(ld_x[g], 16)
                sp.dma_start(MRAW[:, 4 * g * D:4 * (g + 1) * D].rearrange("p (a c) -> p a c", a=4),
                             mods[4 * g:4 * (g + 1)].rearrange("a p c -> p a c")).then_inc(ld_ma[g], 16)
                if g == 0:
                    sp.dma_start(IDF[:, :], consts[:, K_ID:K_ID + P]).then_inc(ld_c, 16)
                    sp.dma_start(T[0][:, 0:P], consts[:, K_TRI:K_TRI + P]).then_inc(ld_c, 16)
            sp.dma_start(WR0[:, :], wst[0]).then_inc(ld_w, 16)
            load_w(1)
            sp.wait_ge(f_lo, FILL["a"] + KT)

            def load_mod(m):
                sp.wait_ge(mod_done, m)
                sp.dma_start(MR, row(mods, m)).then_inc(ld_mod, 16)

            with sp.Fori(0, KT) as j:
                m = 0
                for n, k in enumerate((1, 1, 2, 2)):
                    for _ in range(k):
                        load_mod(MODS_J * j + (N_MODS_A + m))
                        m += 1
                    load_w(4 * j + (n + 2))
            with sp.Fori(0, KT) as c:
                load_w(c + (C_AOUT + 2))
            sp.wait_ge(sq_added, 2 * KT)
            with sp.Fori(0, KT) as i:
                load_w(2 * i + (C_KV + 2))
                sp.wait_ge(free[0], i + (USED["kv"][0] + 1))
                sp.dma_start(row(k_hi, i), KSH[:, :].bitcast(F32)).then_inc(st_k, 16)
                sp.dma_start(row(k_lo, i), KSL[:, :].bitcast(F32)).then_inc(st_k, 16)
                sp.dma_start(row(x_b, i), kt(X, i)).then_inc(st_x, 16)
                load_w(2 * i + (C_KV + 3))
                sp.wait_ge(free[2], i + (USED["kv"][2] + 1))
                sp.dma_start(row(v_hi, i), VSH[:, :].bitcast(F32)).then_inc(st_v, 16)
                sp.dma_start(row(v_lo, i), VSL[:, :].bitcast(F32)).then_inc(st_v, 16)
            sp.wait_ge(st_k, KT * 32 + 32)
            sp.wait_ge(st_v, KT * 32 + 32)
            sp.wait_ge(st_x, KT * 16)
            def load_kv(j, par):
                for src, dst in ((k_hi, bKH), (k_lo, bKL), (v_hi, bVH), (v_lo, bVL)):
                    sp.dma_start(dst[par][:, :].bitcast(F32), row(src, j)).then_inc(b_ld, 16)

            load_w(C_QZ + 2)
            sp.wait_ge(f_lo, FILL["qz"] + KT)
            load_kv(0, 0)
            load_w(C_QZ + 3)

            def attention_b(j, par, first=False):
                load_w(2 * j + (C_QZ + 4))
                if not first:
                    sp.wait_ge(b_o, ST * j)
                    sp.dma_start(row(y_b, j - 1), bZS[1 - par][:, :]).then_inc(b_st, 16)
                load_kv(j + 1, 1 - par)
                load_w(2 * j + (C_QZ + 5))

            attention_b(0, 0, first=True)
            with sp.Fori(0, (KT - 2) // 2) as i:
                for m in range(2):
                    attention_b(2 * i + (1 + m), 1 - m)
            for j in (KT - 2, KT - 1):
                sp.wait_ge(b_o, ST * (j + 1))
                sp.dma_start(y_b[j], bZS[j % 2][:, :]).then_inc(b_st, 16)
            for k in range(KT):
                sp.dma_start(kt(X, k), x_b[k]).then_inc(ld_xr, 16)
            sp.wait_ge(b_st, 16 * KT)

            def operand_back(src, name):
                for k in range(KT):
                    if k >= 4:
                        sp.wait_ge(f_lo, FILL[name] + k - 3)
                    sp.dma_start(STG[k % 4][:, :], src[k]).then_inc(back[k % 4], 16)

            operand_back(y_b, "y")
            with sp.Fori(0, KT) as c:
                load_w(c + (C_BOUT + 2))
            with sp.Fori(0, 5) as c:
                load_w(c + (C_POOL + 2))
            with sp.Fori(0, KT) as n:
                load_w(2 * n + (C_GP + 2))
                load_w(2 * n + (C_GP + 3))
                sp.wait_ge(free[(C_GP + 1) % 2], n + (USED["gp"][(C_GP + 1) % 2] + 1))
                sp.dma_start(row(m_p, n), T[2]).then_inc(gp_st, 16)
                sp.wait_ge(x_new, n + 1)
                sp.dma_start(row(x_d, n), kt(X, n)).then_inc(st_x, 16)
            with sp.Fori(0, KT // 2) as i:
                for m in range(2):
                    s = (C_GA + m) % 2
                    load_w(2 * i + (C_GA + 2 + m))
                    sp.wait_ge(free[s], i + (USED["ga"][s] + 1))
                    sp.dma_start(row(g_a, 2 * i + m), T[3]).then_inc(ga_st, 16)
            sp.wait_ge(gp_st, 16 * KT)
            sp.wait_ge(ga_st, 16 * KT)
            sp.wait_ge(st_x, 2 * KT * 16)
            sp.dma_start(dP1[:, :], consts[:, K_DIST:K_DIST + S]).then_inc(d_ld, 16)
            sp.dma_start(dRS[:, 0:4 * HD], consts[:, K_LAM:K_LAM + 4 * HD]).then_inc(d_ld, 16)
            sp.dma_start(dBD[:, :], consts[:, K_BD:K_BD + P]).then_inc(d_st, 16)
            for c in range(3):
                load_w(C_QKV2 + 2 + c)

            def store_outputs(j, par, norms):
                sp.wait_ge(d_n, norms)
                sp.dma_start(row(y_d, j), dOT[par][:, :]).then_inc(d_st, 16)

            def attention_d(j, par, first=False):
                load_w(3 * j + (C_QKV2 + 5))
                if not first:
                    store_outputs(j - 1, 1 - par, 3 * j + 2)
                load_w(3 * j + (C_QKV2 + 6))
                load_w(3 * j + (C_QKV2 + 7))

            attention_d(0, 0, first=True)
            with sp.Fori(0, (KT - 2) // 2) as i:
                for m in range(2):
                    attention_d(2 * i + (1 + m), 1 - m)
            store_outputs(KT - 2, 0, 3 * KT - 1)
            store_outputs(KT - 1, 1, 3 * KT)
            sp.wait_ge(d_st, 16 * KT + 16)
            for k in range(KT):
                sp.dma_start(kt(X, k), x_d[k]).then_inc(ld_xr, 16)
            operand_back(y_d, "ab")
            sp.wait_ge(f_lo, FILL["ab"] + KT)
            for n in range(KT):
                if n >= 2:
                    sp.wait_ge(g_lo, KT + n - 1)
                sp.dma_start(T[n % 2], g_a[n]).then_inc(ab_ld[n % 2], 16)
                sp.dma_start(T[2 + n % 2], m_p[n]).then_inc(ab_ld[n % 2], 16)
                load_w(C_AB + 2 + n)
            with sp.Fori(0, KT) as n:
                load_w(n + (C_WO + 2))
            with sp.Fori(0, FFQ * 2 * KT - 1) as n:
                load_w(n + (C_FF + 2))
            with sp.Fori(0, KT // 2) as i:
                for m in range(2):
                    s = (C_FF + m) % 2
                    sp.wait_ge(free[s], i + (USED["ff"][s] + (2 * FFQ - 1) * KT // 2 + 1))
                    sp.dma_start(row(out, 2 * i + m), kt(X, 2 * i + m)).then_inc(st_out, 16)
            sp.wait_ge(st_out, 16 * KT)

        @block.tensor
        def _(pe):
            def mm3(dst0, lh, ll, RH, RL, k, start, stop):
                for l, rr, a, z in ((lh, RH, start, False), (lh, RL, False, False), (ll, RH, False, stop)):
                    for q in (0, HALF):
                        last = pe.matmul(PS[:, dst0 + q:dst0 + q + HALF], l, rr[:, k * S + q:k * S + q + HALF],
                                         start=a, stop=z)
                return last

            def step(c, slot, pair, RH, RL, k, nk=KT):
                if k == 0:
                    pe.wait_ge(w_hi, c + 1)
                    pe.wait_ge(w_lo, c + 1)
                b = slice(k * P, (k + 1) * P)
                last = mm3(pair * S, WH[slot][:, b], WL[slot][:, b], RH, RL, k, k == 0, k == nk - 1)
                if k == nk - 1:
                    last.then_inc(chunk_done, 1)

            def chunk(c, slot, pair, used, RH=HH, RL=HL, nk=KT, operand=None):
                pe.wait_ge(free[pair], used)
                for k in range(nk):
                    if operand:
                        pe.wait_ge(operand[0], operand[1] + (k + 1))
                    step(c, slot, pair, RH, RL, k, nk)

            def chunks(name, base, n, RH, RL, operand=None):
                u = USED[name]
                with pe.Fori(0, n // 2) as i:
                    for m in range(2):
                        s = (base + m) % 2
                        chunk(2 * i + (base + m), s, s, i + u[s], RH, RL, operand=operand if m == 0 else None)

            def sum_squares(added, acc, dst=2 * S):
                pe.wait_ge(sq_added, added)
                for h in (0, HALF):
                    last = pe.matmul(PS[:, dst + h:dst + h + HALF], ONES[:, :], acc[:, h:h + HALF], start=True, stop=True)
                last.then_inc(ss, 1)

            pe.wait_ge(s_const, 1)
            for k in range(KT):
                pe.wait_ge(sq, k + 1)
                for h in (HALF, 0) if k == KT - 1 else (0, HALF):
                    last = pe.matmul(PS[:, 2 * S + h:2 * S + h + HALF], ONES[:, :], T[2 + k % 2][:, h:h + HALF],
                                     start=(k == 0), stop=(k == KT - 1))
                    if h:
                        last.then_inc(sq_added, 1)
                    elif k == KT - 1:
                        last.then_inc(ss, 1)
            u = USED["ain"]
            with pe.Fori(0, KT) as j:
                for n in range(4):
                    chunk(4 * j + n, n % 2, n % 2, 2 * j + (u[n % 2] + n // 2),
                          operand=(f_lo, FILL["a"]) if n == 0 else None)
            chunks("aout", C_AOUT, KT, GH, GL, operand=(g_lo, 0))
            sum_squares(2 * KT, T[1])
            u = USED["kv"]
            with pe.Fori(0, KT) as i:
                chunk(2 * i + C_KV, 0, 0, i + u[0], operand=(f_lo, FILL["kv"]))
                chunk(2 * i + (C_KV + 1), 1, 1, i + u[1])
                pe.wait_ge(free[1], i + (u[1] + 1))
                pe.wait_ge(free[2], i + u[2])
                for t in range(ST):
                    b = slice(t * P, (t + 1) * P)
                    last = pe.transpose(PS[:, 2 * S + t * P:2 * S + (t + 1) * P], VST[:, b], IDF[:, :])
                last.then_inc(kv_t, 1)

            def score_parts(base, rows, q, n, QH, QL, KH, KL, open_bank=None):
                for l, rr, a in ((QH, KH, True), (QH, KL, False), (QL, KH, False)):
                    for c0 in range(0, n, HALF):
                        w = min(HALF, n - c0)
                        pe.matmul(PS[:, base + c0:base + c0 + w], l[rows, q], rr[rows, c0:c0 + w], start=a,
                                  stop=(l is QL and open_bank is not None and c0 != open_bank))

            def value_sum(t, n, VH, VL):
                h, l = ATH[n], ATL[n]
                parts = [(kb, v, a) for kb in (0, t, *range(1, t)) for v, a in ((VH, h), (VH, l), (VL, h))]
                if t == 1:
                    parts = [parts[i] for i in (0, 3, 4, 5, 1, 2)]
                for i, (kb, v, a) in enumerate(parts):
                    r = 1 if kb == t else 0
                    last = pe.matmul(PS[:, OB + (2 * n + r) * P:OB + (2 * n + 2) * P], v[:, kb * P:(kb + 1) * P],
                                     a[:, (2 * kb + r) * P:(2 * kb + 2) * P], start=(i == 0), stop=(i == len(parts) - 1))
                return last

            u = USED["qz"]
            chunk(C_QZ, 0, 0, u[0], operand=(f_lo, FILL["qz"]))
            chunk(C_QZ + 1, 1, 0, u[0] + 1)

            def attention_b(j, par, fill=True, first=False):
                def turn(s, g):
                    if s < 0 and first or g >= len(GROUP_BLOCKS[s % ST]):
                        return
                    pe.wait_ge(b_a, 2 * ST * j + (s + 1))
                    if not (first and s == 0 and g == 0):
                        pe.wait_ge(b_atl, 2 * NG * j + (group_index(s) + g))
                    for n, kb in enumerate(blocks_of(s % ST, g)):
                        last = pe.transpose(PS[:, TB + n * P:TB + (n + 1) * P], bB[s % 4][:, kb * P:(kb + 1) * P], IDF[:, :])
                    last.then_inc(b_t, 1)

                def scores(s):
                    h, t = s // ST, s % ST
                    base = (1 + s % 2) * S
                    pe.wait_ge(free[1 + s % 2], ST * j + (u[1 + s % 2] + s // 2))
                    score_parts(base, slice(h * HD, (h + 1) * HD), slice(t * P, (t + 1) * P), (t + 1) * P,
                                bQH[par], bQL[par], bKH[par], bKL[par], open_bank=t * P // HALF * HALF)
                    pe.matmul(PS[:, base + t * P:base + (t + 1) * P], IDR[:, :], TRIR[:, :],
                              start=False, stop=True).then_inc(b_s, 1)

                def values(s):
                    if s % 2 == 0 or s < 0 and first:
                        return
                    if not (first and s < 4):
                        pe.wait_ge(b_o, ST * j + (s + 1) // 2 - 2)
                    pe.wait_ge(b_atl, 2 * NG * j + group_index(s + 1))
                    v = par if s >= 0 else 1 - par
                    value_sum(s % ST, s // 2 % 2, bVH[v], bVL[v]).then_inc(b_av, 1)

                pe.wait_ge(free[0], 2 * j + (u[0] + 1))
                pe.wait_ge(b_ld, 64 * j + 64)
                k = 0

                def steps(n):
                    nonlocal k
                    for _ in range(n if fill else 0):
                        if k % KT == 0:
                            pe.wait_ge(free[0], 2 * j + (u[0] + 2 + k // KT))
                        step(2 * j + (C_QZ + 2 + k // KT), k // KT, 0, HH, HL, k % KT)
                        k += 1

                for s in range(2 * ST):
                    scores(s)
                    steps(B_STEPS[s] // 2)
                    turn(s - 3, 0)
                    steps(B_STEPS[s] - B_STEPS[s] // 2)
                    values(s - 4)
                    turn(s - 3, 1)
                if fill:
                    return
                for s in range(2 * ST, 2 * ST + 4):
                    values(s - 4)
                    if s < 2 * ST + 3:
                        turn(s - 3, 0)
                        turn(s - 3, 1)

            attention_b(0, 0, first=True)
            with pe.Fori(0, (KT - 2) // 2) as i:
                for m in range(2):
                    attention_b(2 * i + (1 + m), 1 - m)
            attention_b(KT - 1, 1, fill=False)
            chunks("bout", C_BOUT, KT, HH, HL, operand=(f_lo, FILL["y"]))
            sum_squares(4 * KT, T[1])
            sum_squares(4 * KT, TP, dst=3 * S)

            uu = USED["pool"]
            for g in range(4):
                s = (C_POOL + g) % 2
                chunk(C_POOL + g, s, s, uu[s] + g // 2, operand=(f_lo, FILL["mix"]) if g == 0 else None)
            cg = C_POOL + 4
            pe.wait_ge(w_lo, cg + 1)
            for g in range(4):
                b = slice(g * P, (g + 1) * P)
                pe.wait_ge(p_ml, g + 1)
                if g < 2:
                    pe.wait_ge(free[g], uu[g] + 2)
                else:
                    pe.wait_ge(p_yl, g - 1)
                last = mm3((g % 2) * S, WH[cg % 2][:, b], WL[cg % 2][:, b], MXH, MXL, g, True, True)
                last.then_inc(p_g if g < 3 else chunk_done, 1)
            u = USED["gp"]
            s0, s1 = C_GP % 2, (C_GP + 1) % 2
            pe.wait_ge(p_yl, 4)
            with pe.Fori(0, KT) as n:
                chunk(2 * n + C_GP, s0, s0, n + u[s0])
                chunk(2 * n + (C_GP + 1), s1, s1, n + u[s1], YPH, YPL, nk=4)
            chunks("ga", C_GA, KT, HH, HL)

            ud = USED["qkv2"]

            def group_sums(n):
                pe.wait_ge(d_sq, n)
                for h in (0, HALF):
                    last = pe.matmul(PS[:, h:h + HALF], dBD[:, :], dSQ[:, h:h + HALF], start=True, stop=True)
                last.then_inc(d_ss, 1)

            def turn_values(j, par):
                pe.wait_ge(d_v, j + 1)
                for t in range(ST):
                    b = slice(t * P, (t + 1) * P)
                    last = pe.transpose(PS[:, b], dVR[par][:, b], IDF[:, :])
                last.then_inc(d_vt, 1)

            def output_sums(n):
                pe.wait_ge(d_sq, n)
                for h in (0, HALF):
                    last = pe.matmul(PS[:, h:h + HALF], ONES[:, :], dSQ[:, h:h + HALF], start=True, stop=True)
                last.then_inc(d_ss, 1)

            pe.wait_ge(d_st, 16)
            for n in range(3):
                chunk(C_QKV2 + n, (C_QKV2 + n) % 2, 0, ud[0] + n)
                if n < 2:
                    group_sums(n + 1)

            def attention_d(j, par, fill=True, first=False):
                used = 4 * j + (ud[0] + 1)

                def turn(s, g):
                    if s < 0 and first or g >= len(GROUP_BLOCKS[s % ST]):
                        return
                    pe.wait_ge(d_a, ST * j + (s + 1))
                    if not (first and s == 0 and g == 0):
                        pe.wait_ge(d_atl, NG * j + (group_index(s) + g))
                    for n, kb in enumerate(blocks_of(s % ST, g)):
                        last = pe.transpose(PS[:, TB + n * P:TB + (n + 1) * P], dP0[s % 2][:, kb * P:(kb + 1) * P], IDF[:, :])
                    last.then_inc(d_t, 1)

                def scores(s, m):
                    n = (s + 1) * P
                    base = (1 + m) * S
                    pe.wait_ge(free[1 + m], ST * j + (ud[1 + m] + s))
                    score_parts(base, slice(m * HD, (m + 1) * HD), slice(s * P, (s + 1) * P), n,
                                dQH[par], dQL[par], dKH[par], dKL[par])
                    for c0 in range(0, n, HALF):
                        w = min(HALF, n - c0)
                        last = pe.matmul(PS[:, base + c0:base + c0 + w], dSL[par][:, :], dDIST[:, S - n + c0:S - n + c0 + w],
                                         start=False, stop=True)
                    last.then_inc(d_s, 1)

                def values(s):
                    if s % 2 == 0 or s < 0 and first:
                        return
                    if not (first and s < 4):
                        pe.wait_ge(d_o, ST // 2 * j + (s + 1) // 2 - 2)
                    if s == 1:
                        pe.wait_ge(free[0], used + (2 if first else 1))
                    pe.wait_ge(d_atl, NG * j + group_index(s + 1))
                    v = par if s >= 0 else 1 - par
                    value_sum(s % ST, s // 2 % 2, dVH[v], dVL[v]).then_inc(d_av, 1)

                k = 0

                def steps(n):
                    nonlocal k
                    for _ in range(n if fill else 0):
                        c = k // KT
                        if k % KT == 0:
                            pe.wait_ge(free[0], used + (2 + c))
                        step(3 * j + (C_QKV2 + 3 + c), (C_QKV2 + 3 * par + 3 + c) % 2, 0, HH, HL, k % KT)
                        k += 1

                pe.wait_ge(d_split, j + 1)
                for s in range(ST):
                    scores(s, 0)
                    scores(s, 1)
                    if s == 0:
                        turn_values(j, par)
                    if s == 1 and not first:
                        pe.wait_ge(free[0], used + 1)
                        output_sums(3 * j + 2)
                    if fill and s in (4, 6):
                        group_sums(3 * j + (3 if s == 4 else 4))
                    turn(s - 1, 0)
                    early = 0 if s in (1, 4, 6) else (D_STEPS[s] + 1) // 2
                    steps(early)
                    turn(s - 1, 1)
                    values(s - 1)
                    steps(D_STEPS[s] - early)
                if fill:
                    return
                turn(ST - 1, 0)
                turn(ST - 1, 1)
                values(ST - 1)
                pe.wait_ge(free[0], used + 2)
                output_sums(3 * KT)

            attention_d(0, 0, first=True)
            with pe.Fori(0, (KT - 2) // 2) as i:
                for m in range(2):
                    attention_d(2 * i + (1 + m), 1 - m)
            attention_d(KT - 1, 1, fill=False)
            chunks("ab", C_AB, KT, HH, HL, operand=(f_lo, FILL["ab"]))
            chunks("wo", C_WO, KT, GH, GL, operand=(g_lo, KT))
            sum_squares(5 * KT, T[1])

            u = USED["ff"]
            with pe.Fori(0, FFQ) as q:
                for down, (RH, RL) in enumerate(((HH, HL), (GH, GL))):
                    with pe.Fori(0, KT // 2) as i:
                        for m in range(2):
                            s = (C_FF + m) % 2
                            used = i + KT * q + (u[s] + KT // 2 * down)
                            need = None if m else (g_lo, KT * q + 2 * KT) if down else (f_lo, FILL["ffn"])
                            chunk(2 * i + 2 * KT * q + (C_FF + KT * down + m), s, s, used, RH, RL, operand=need)

        @block.scalar
        def _(act):
            links = Links(act, act_link)

            def split_w(c, slot):
                act.wait_ge(ld_w, 16 * c + 16)
                if not (isinstance(c, int) and c == 0):
                    act.wait_ge(chunk_done, c)
                act.activation(WH[slot][:, :], WR0[:, :], ACT.Identity).then_inc(w_hi, 1)

            def root(dst, src, tmp):
                links(act.activation(tmp, src, ACT.Ln, bias=EPSC[:, 0:1], scale=1.0 / D))
                act.activation(dst, tmp, ACT.Exp, scale=-0.5).then_inc(rs, 1)

            def fill_hi(name, shift=None):
                for k in range(KT):
                    act.wait_ge(ftmp, SCALED[name] + k + 1)
                    kw = {} if shift is None else {"bias": col(MOD, shift + k)}
                    act.activation(kt(HH, k), T[2 + k % 2], ACT.Identity, **kw).then_inc(f_hi, 1)

            def operand_hi(times):
                for k in range(KT):
                    act.wait_ge(back[k % 4], 16 * (2 * times + k // 4 + 1))
                    act.activation(kt(HH, k), STG[k % 4][:, :], ACT.Identity).then_inc(f_hi, 1)

            act.wait_ge(ld_cb, 16)
            act.activation(TP, CB, ACT.Sigmoid).then_inc(s_sig, 1)
            act.wait_ge(ld_c, 48)
            act.activation(IDR[:, :], IDF[:, :], ACT.Identity)
            act.activation(TRIR[:, :], T[0][:, 0:P], ACT.Identity)
            for k in range(KT):
                act.wait_ge(ld_x[k // 2], 16)
                if k >= 2:
                    act.wait_ge(sq_added, k - 1)
                act.activation(T[2 + k % 2], kt(X, k), ACT.Square).then_inc(sq, 1)
            act.wait_ge(s_sc, 1)
            act.wait_ge(ss, 1)
            root(T[0], PAIR[2], TP)
            act.wait_ge(mod_ready, 1)
            split_w(0, 0)
            fill_hi("a", 0)
            with act.Fori(0, KT) as j:
                split_w(4 * j + 1, 1)
                act.wait_ge(chunk_done, 4 * j + 2)
                act.activation(T[2], PAIR[0], ACT.Identity).then_inc(free[0], 1)
                split_w(4 * j + 2, 0)
                split_w(4 * j + 3, 1)
                split_w(4 * j + 4, 0)
                act.wait_ge(chunk_done, 4 * j + 5)
                act.wait_ge(free[1], 2 * j + 2)
                act.activation(T[2], PAIR[1], ACT.Sigmoid).then_inc(ain_sg, 1)
                act.wait_ge(ain_y, j + 1)
                act.activation(kt(GH, j), T[3], ACT.Identity).then_inc(g_hi, 1)

            def squares_of_new(name, base, added):
                with act.Fori(0, KT // 2) as i:
                    for m in range(2):
                        s = (base + m) % 2
                        split_w(2 * i + (base + m + 1), 1 - s)
                        act.wait_ge(free[s], i + (USED[name][s] + 1))
                        act.wait_ge(sq_added, 2 * i + (added + m - 1))
                        act.activation(T[2 + m], kt(X, 2 * i + m), ACT.Square).then_inc(sq, 1)

            squares_of_new("aout", C_AOUT, KT)
            act.wait_ge(ss, 2)
            root(T[0], PAIR[2], TP)
            act.wait_ge(mod_ready, 2)
            fill_hi("kv", 3 * KT)
            with act.Fori(0, KT) as i:
                split_w(2 * i + (C_KV + 1), 1)
                act.wait_ge(chunk_done, 2 * i + (C_KV + 2))
                act.wait_ge(st_k, 32 * i + 32)
                act.activation(KSH[:, :], PAIR[0], ACT.Identity).then_inc(kv_kh, 1)
                split_w(2 * i + (C_KV + 2), 0)
                act.wait_ge(chunk_done, 2 * i + (C_KV + 3))
                act.activation(VST[:, :], PAIR[1], ACT.Identity).then_inc(free[1], 1)
                act.wait_ge(kv_t, i + 1)
                act.wait_ge(st_v, 32 * i + 32)
                act.activation(VSH[:, :], PAIR[2], ACT.Identity).then_inc(kv_vh, 1)

            fill_hi("qz", 5 * KT)
            split_w(C_QZ + 1, 1)
            act.wait_ge(f_lo, FILL["qz"] + KT)
            act.wait_ge(chunk_done, C_QZ + 2)
            act.activation(bQH[0][:, :], PAIR[0], ACT.Identity).then_inc(b_qh, 1)
            split_w(C_QZ + 2, 0)
            act.wait_ge(chunk_done, C_QZ + 3)
            act.activation(bZS[0][:, :], PAIR[0], ACT.Sigmoid).then_inc(b_sg, 1)

            def attention_b(j, par, fill=True, first=False):
                def turned(s, g):
                    if s < 0 and first or g >= len(GROUP_BLOCKS[s % ST]):
                        return
                    bl = blocks_of(s % ST, g)
                    lo, hi = bl[0] * P, (bl[-1] + 1) * P
                    act.wait_ge(b_t, 2 * NG * j + (group_index(s) + g + 1))
                    if g == 0 and s % 2 == 0 and not (first and s < 4):
                        act.wait_ge(b_av, ST * j + s // 2 - 1)
                    act.activation(at_blocks(ATH[s // 2 % 2], s % 2, bl[0], bl[-1] + 1), turned_blocks(len(bl)),
                                   ACT.Identity).then_inc(b_ath, 1)

                for s in range(2 * ST):
                    n = (s % ST + 1) * P
                    src = PS[:, (1 + s % 2) * S:(1 + s % 2) * S + n]
                    act.wait_ge(b_s, 2 * ST * j + (s + 1))
                    if not (first and s < 2):
                        act.wait_ge(b_a, 2 * ST * j + (s - 1))
                    act.activation(bC[s % 2][:, S - n:S], src, ACT.Sigmoid, scale=-HD ** -0.5).then_inc(b_c, 1)
                    act.activation(bB[s % 4][:, 0:n], src, ACT.Sigmoid, scale=HD ** -0.5).then_inc(free[1 + s % 2], 1)
                    turned(s - 3, 0)
                    turned(s - 3, 1)
                    if fill and s == 1:
                        split_w(2 * j + (C_QZ + 3), 1)
                    if fill and s == ST - 1:
                        act.wait_ge(chunk_done, 2 * j + (C_QZ + 4))
                        act.activation(bQH[1 - par][:, :], PAIR[0], ACT.Identity).then_inc(b_qh, 1)
                        split_w(2 * j + (C_QZ + 4), 0)
                    if fill and s == 2 * ST - 1:
                        act.wait_ge(chunk_done, 2 * j + (C_QZ + 5))
                        if not first:
                            act.wait_ge(b_st, 16 * j)
                        act.activation(bZS[1 - par][:, :], PAIR[0], ACT.Sigmoid).then_inc(b_sg, 1)
                if not fill:
                    for s in range(2 * ST - 3, 2 * ST):
                        turned(s, 0)
                        turned(s, 1)

            attention_b(0, 0, first=True)
            with act.Fori(0, (KT - 2) // 2) as i:
                for m in range(2):
                    attention_b(2 * i + (1 + m), 1 - m)
            attention_b(KT - 1, 1, fill=False)
            operand_hi(0)
            act.wait_ge(f_lo, FILL["y"] + KT)
            with act.Fori(0, KT // 2) as i:
                for m in range(2):
                    s = (C_BOUT + m) % 2
                    split_w(2 * i + (C_BOUT + m + 1), 1 - s)
                    act.wait_ge(free[s], i + (USED["bout"][s] + 1))
                    act.wait_ge(sq_added, 4 * i + (2 * KT + 2 * m))
                    act.activation(T[2], kt(X, 2 * i + m), ACT.Square).then_inc(sq, 1)
                    act.activation(T[3], kt(X, 2 * i + m), ACT.Square, scale=vec("final_g", 2 * i + m)).then_inc(sq, 1)
            act.wait_ge(ss, 4)
            links(act.activation(T[2], PAIR[2], ACT.Ln, bias=EPSC[:, 0:1], scale=1.0 / D))
            links(act.activation(T[1], T[2], ACT.Exp, scale=-0.5))
            act.activation(T[2], T[1], ACT.Square).then_inc(ms2, 1)
            act.wait_ge(ms2, 2)
            links(act.activation(T[3], T[3], ACT.Ln, bias=EPSC[:, 0:1], scale=1.0 / D))
            act.activation(T[2], T[3], ACT.Exp, scale=-0.5).then_inc(rs, 1)
            fill_hi("mix")

            act.wait_ge(p_mx, 1)
            for g in range(4):
                c = C_POOL + g
                split_w(c + 1, (c + 1) % 2)
                act.wait_ge(chunk_done, c + 2)
                act.activation(TP, PAIR[c % 2], ACT.Identity).then_inc(free[c % 2], 1)
                act.wait_ge(p_mx, g + 2)
                act.activation(kt(MXH, g), T[3], ACT.Identity).then_inc(p_mh, 1)
            split_w(C_POOL + 5, (C_POOL + 5) % 2)
            for g in range(4):
                if g < 3:
                    act.wait_ge(p_g, g + 1)
                else:
                    act.wait_ge(chunk_done, C_POOL + 6)
                act.activation(kt(YPH, g), PAIR[g % 2], ACT.Identity, scale=vec("pool_scale", g)).then_inc(p_yh, 1)
            s0, s1 = C_GP % 2, (C_GP + 1) % 2
            with act.Fori(0, KT) as n:
                split_w(2 * n + (C_GP + 1), s1)
                act.wait_ge(chunk_done, 2 * n + (C_GP + 2))
                act.activation(T[1], PAIR[s0], ACT.Sigmoid, bias=vec("b_gate", n)).then_inc(free[s0], 1)
                split_w(2 * n + (C_GP + 2), s0)
                act.wait_ge(free[s1], n + (USED["gp"][s1] + 1))
            with act.Fori(0, KT // 2) as i:
                for m in range(2):
                    s = (C_GA + m) % 2
                    split_w(2 * i + (C_GA + m + 1), 1 - s)
                    act.wait_ge(chunk_done, 2 * i + (C_GA + m + 2))
                    act.activation(T[3], PAIR[s], ACT.Sigmoid, bias=vec("b_gate", 2 * i + (8 + m))).then_inc(free[s], 1)
                    act.wait_ge(ga_st, 32 * i + 16 * (m + 1))

            act.wait_ge(d_lam, 1)
            act.activation(SM[:, 10:12], SM[:, 8:10], ACT.Exp).then_inc(d_lam, 1)
            act.activation(dDIST[:, :], dP1[:, :], ACT.Identity)
            ud = USED["qkv2"]

            def squares_d(c, raw, n):
                act.wait_ge(chunk_done, c + 2)
                act.activation(raw[:, :], PAIR[0], ACT.Identity)
                if not (isinstance(n, int) and n == 1):
                    act.wait_ge(d_rs, n - 1)
                act.activation(dSQ[:, :], PAIR[0], ACT.Square).then_inc(d_sq, 1)

            def root_d(n, width, used):
                act.wait_ge(d_ss, n)
                act.activation(dSQ[:, :], PAIR[0], ACT.Ln, bias=EPSC[:, 0:1], scale=1.0 / width).then_inc(free[0], 1)
                act.wait_ge(free[0], used)
                if not (isinstance(n, int) and n == 1):
                    act.wait_ge(d_n, n - 1)
                act.activation(dRS[:, :], dSQ[:, :], ACT.Exp, scale=-0.5).then_inc(d_rs, 1)

            def hi_d(dst, src, n):
                act.wait_ge(d_n, n)
                act.activation(dst[:, :], src[:, :], ACT.Identity).then_inc(d_hi, 1)

            def stage_values(c, par):
                act.wait_ge(chunk_done, c + 2)
                act.activation(dVR[par][:, :], PAIR[0], ACT.Identity).then_inc(d_v, 1)

            act.wait_ge(d_lam, 3)
            for n, (hi, raw) in enumerate(((dQH[0], dQR[0]), (dKH[0], dKR[0]))):
                split_w(C_QKV2 + n + 1, (C_QKV2 + n + 1) % 2)
                squares_d(C_QKV2 + n, raw, n + 1)
                root_d(n + 1, HD, ud[0] + n + 1)
                hi_d(hi, raw, n + 1)
            split_w(C_QKV2 + 3, (C_QKV2 + 3) % 2)
            stage_values(C_QKV2 + 2, 0)

            def attention_d(j, par, fill=True, first=False):
                used = 4 * j + (ud[0] + 1)
                nxt = 1 - par

                def turned(s, g):
                    if s < 0 and first or g >= len(GROUP_BLOCKS[s % ST]):
                        return
                    bl = blocks_of(s % ST, g)
                    act.wait_ge(d_t, NG * j + (group_index(s) + g + 1))
                    if g == 0 and s % 2 == 0 and not (first and s < 4):
                        act.wait_ge(d_av, ST // 2 * j + s // 2 - 1)
                    act.activation(at_blocks(ATH[s // 2 % 2], s % 2, bl[0], bl[-1] + 1), turned_blocks(len(bl)),
                                   ACT.Identity).then_inc(d_ath, 1)

                for s in range(ST):
                    turned(s - 1, 0)
                    turned(s - 1, 1)
                    w = (s + 1) * P
                    act.wait_ge(d_max, ST * j + (s + 1))
                    act.activation(dP0[s % 2][:, 0:w], PS[:, S:S + w], ACT.Exp, bias=SM[:, 2:3],
                                   accum_out=SM[:, 4:5]).then_inc(free[1], 1)
                    act.activation(dP1[:, 0:w], PS[:, 2 * S:2 * S + w], ACT.Exp, bias=SM[:, 3:4],
                                   accum_out=SM[:, 5:6]).then_inc(free[2], 1)
                    if s == 0:
                        act.wait_ge(d_vt, j + 1)
                        act.activation(dVH[par][:, :], PAIR[0], ACT.Identity).then_inc(d_hi, 1)
                        if fill:
                            split_w(3 * j + (C_QKV2 + 4), (C_QKV2 + 3 * par + 4) % 2)
                        if not first:
                            act.wait_ge(d_o, ST // 2 * j)
                            act.wait_ge(d_rs, 3 * j + 1)
                            act.activation(dSQ[:, :], dOT[nxt][:, :], ACT.Square).then_inc(d_sq, 1)
                    if s == 1 and not first:
                        root_d(3 * j + 2, P, used + 2)
                    if not fill:
                        continue
                    if s == 3:
                        squares_d(3 * j + (C_QKV2 + 3), dQR[nxt], 3 * j + 3)
                        split_w(3 * j + (C_QKV2 + 5), (C_QKV2 + 3 * par + 5) % 2)
                    if s == 4:
                        root_d(3 * j + 3, HD, used + 3)
                    if s == 5:
                        hi_d(dQH[nxt], dQR[nxt], 3 * j + 3)
                        squares_d(3 * j + (C_QKV2 + 4), dKR[nxt], 3 * j + 4)
                        split_w(3 * j + (C_QKV2 + 6), (C_QKV2 + 3 * par + 6) % 2)
                    if s == 6:
                        root_d(3 * j + 4, HD, used + 4)
                    if s == 7:
                        hi_d(dKH[nxt], dKR[nxt], 3 * j + 4)
                        stage_values(3 * j + (C_QKV2 + 5), nxt)
                if not fill:
                    turned(ST - 1, 0)
                    turned(ST - 1, 1)
                    act.wait_ge(d_o, ST // 2 * KT)
                    act.wait_ge(d_rs, 3 * KT - 1)
                    act.activation(dSQ[:, :], dOT[par][:, :], ACT.Square).then_inc(d_sq, 1)
                    root_d(3 * KT, P, used + 3)

            attention_d(0, 0, first=True)
            with act.Fori(0, (KT - 2) // 2) as i:
                for m in range(2):
                    attention_d(2 * i + (1 + m), 1 - m)
            attention_d(KT - 1, 1, fill=False)
            operand_hi(1)
            for n in range(KT):
                c = C_AB + n
                split_w(c + 1, (c + 1) % 2)
                act.wait_ge(ab_m, n + 1)
                act.activation(kt(GH, n), T[2 + n % 2], ACT.Identity).then_inc(g_hi, 1)
            squares_of_new("wo", C_WO, 4 * KT)
            act.wait_ge(ss, 5)
            root(T[0], PAIR[2], TP)
            fill_hi("ffn")
            u = USED["ff"]
            with act.Fori(0, FFQ) as q:
                with act.Fori(0, KT // 2) as i:
                    for m in range(2):
                        s = (C_FF + m) % 2
                        split_w(2 * i + 2 * KT * q + (C_FF + m + 1), 1 - s)
                        act.wait_ge(chunk_done, 2 * i + 2 * KT * q + (C_FF + m + 2))
                        act.activation(T[m], PAIR[s], ACT.Relu).then_inc(ff_r, 1)
                        act.wait_ge(free[s], i + KT * q + (u[s] + 1))
                        act.activation(kt(GH, 2 * i + m), T[2 + m], ACT.Identity).then_inc(g_hi, 1)
                with act.Fori(0, KT // 2) as i:
                    for m in range(2):
                        split_w(2 * i + 2 * KT * q + (C_FF + KT + m + 1), 1 - (C_FF + m) % 2)

        @block.vector
        def _(dve):
            links = Links(dve, dve_link)

            def mul_mul(dst, src, scalar, other):
                return dve.scalar_tensor_tensor(out=dst, in0=src, scalar=scalar, in1=other, op0=ALU.mult, op1=ALU.mult)

            def mul_add(dst, src, scalar, other):
                return dve.scalar_tensor_tensor(out=dst, in0=src, scalar=scalar, in1=other, op0=ALU.mult, op1=ALU.add)

            def low(dst, value, high):
                return dve.tensor_tensor(dst, value, high.bitcast(F32), ALU.subtract)

            def add_square(n, acc, src):
                dve.wait_ge(sq, n + 1)
                if not (isinstance(n, int) and n == 0):
                    dve.wait_ge(sq_added, n)
                dve.tensor_tensor(acc, acc, src, ALU.add).then_inc(sq_added, 1)

            def fill_lo(name, n_rs, scale, shift=None):
                dve.wait_ge(rs, n_rs)
                for k in range(KT + 1):
                    if k < KT:
                        if k >= 2:
                            dve.wait_ge(f_lo, FILL[name] + k - 1)
                        mul_mul(T[2 + k % 2], kt(X, k), scale(k), T[0]).then_inc(ftmp, 1)
                    if k:
                        dve.wait_ge(f_hi, FILL[name] + k)
                        hi = kt(HH, k - 1).bitcast(F32)
                        tmp = T[2 + (k - 1) % 2]
                        if shift is None:
                            lo = dve.tensor_tensor(kt(HL, k - 1), tmp, hi, ALU.subtract)
                        else:
                            lo = dve.scalar_tensor_tensor(out=kt(HL, k - 1), in0=tmp, scalar=col(MOD, shift + k - 1),
                                                          in1=hi, op0=ALU.add, op1=ALU.subtract)
                        lo.then_inc(f_lo, 1)

            def operand_lo(name):
                for k in range(KT):
                    dve.wait_ge(f_hi, FILL[name] + k + 1)
                    low(kt(HL, k), STG[k % 4][:, :], kt(HH, k)).then_inc(f_lo, 1)

            def coefficients(a, g, c, done=False):
                ins = dve.scalar_tensor_tensor(out=COEF[:, c:c + KT], in0=MOD[:, a:a + KT], scalar=1.0,
                                               in1=VEC[:, _V[g]:_V[g] + KT], op0=ALU.add, op1=ALU.mult)
                if done:
                    ins.then_inc(mod_ready, 1)

            dve.memset(ONES[:, :], 1.0).then_inc(chunk_done, 1)
            dve.memset(EPSC[:, :], EPS).then_inc(free[0], 1)
            dve.memset(GQ8[:, :], 0.0).then_inc(st_k, 32)
            dve.memset(GS8[:, :], 0.0).then_inc(st_v, 32)
            dve.memset(NLAM[:, :], 0.0).then_inc(free[1], 1)
            dve.memset(TMP[4][:, 0:PADW], 0.0).then_inc(free[2], 1)
            dve.memset(SM[:, :], 0.0).then_inc(s_const, 1)
            dve.wait_ge(s_sig, 1)
            dve.tensor_tensor(CB, CB, TP, ALU.mult).then_inc(s_sc, 1)
            dve.wait_ge(s_sc, 1)

            def modulation(dst, weights):
                dve.tensor_tensor_reduce(out=weights, in0=weights, in1=CB, scale=1.0, scalar=0.0, op0=ALU.mult, op1=ALU.add,
                                         accum_out=dst).then_inc(mod_done, 1)

            def add_bias(lo, hi):
                dve.wait_ge(mod_done, hi)
                links(dve.tensor_tensor(MOD[:, lo:hi], MOD[:, lo:hi], VEC[:, _V["mod_b"] + lo:_V["mod_b"] + hi], ALU.add))

            for m in range(N_MODS_A):
                if m % 4 == 0:
                    dve.wait_ge(ld_ma[m // 4], 16)
                modulation(MOD[:, m:m + 1], MRAW[:, m * D:(m + 1) * D])
            dve.wait_ge(ld_c, 48)
            links(dve.tensor_scalar(GQ8[:, :], vec("gq"), HD ** -0.5, None, ALU.mult))
            links(dve.tensor_scalar(GS8[:, :], vec("gsub"), 1.0 - LAMBDA_INIT, None, ALU.mult))
            add_bias(0, N_MODS_A)
            coefficients(KT, "a_g", 0, True)
            dve.wait_ge(mod_ready, 1)
            fill_lo("a", 1, lambda k: col(COEF, k), 0)

            def modulations(j, first, n):
                for m in range(first, first + n):
                    dve.wait_ge(ld_mod, 16 * MODS_J * j + 16 * (m + 1))
                    modulation(SM[:, m:m + 1], MR)

            with dve.Fori(0, KT) as j:
                links.round(j, 4)
                modulations(j, 0, 2)
                dve.wait_ge(free[0], 2 * j + 2)
                dve.wait_ge(chunk_done, 4 * j + 3)
                dve.tensor_tensor(TP, PAIR[1], T[2], ALU.mult).then_inc(free[1], 1)
                dve.wait_ge(free[1], 2 * j + 2)
                links(dve.tensor_scalar(T[3], TP, vec("conv", j + 2 * KT), None, ALU.mult))
                links(mul_add(T[3], TMP[4][:, PADW - 1:PADW - 1 + S], vec("conv", j + KT), T[3]))
                links(mul_add(T[3], TMP[4][:, PADW - 2:PADW - 2 + S], vec("conv", j), T[3]))
                modulations(j, 2, 2)
                dve.wait_ge(chunk_done, 4 * j + 4)
                dve.tensor_tensor(T[3], PAIR[0], T[3], ALU.mult).then_inc(free[0], 1)
                modulations(j, 4, 2)
                dve.wait_ge(mod_done, MODS_J * j + (N_MODS_A + MODS_J))
                links(dve.tensor_copy(MOD[:, ds(MODS_J * j + N_MODS_A, MODS_J)], SM[:, 0:MODS_J]))
                dve.wait_ge(ain_sg, j + 1)
                dve.tensor_tensor(T[2], PAIR[1], T[2], ALU.mult).then_inc(free[1], 1)
                dve.wait_ge(free[0], 2 * j + 3)
                dve.wait_ge(free[1], 2 * j + 3)
                dve.tensor_tensor(T[3], T[3], T[2], ALU.mult).then_inc(ain_y, 1)
                dve.wait_ge(g_hi, j + 1)
                low(kt(GL, j), T[3], kt(GH, j)).then_inc(g_lo, 1)
            links.end(KT)
            add_bias(N_MODS_A, N_MODS)
            coefficients(4 * KT, "kv_g", KT)
            coefficients(6 * KT, "b_g", 2 * KT, True)

            def new_residual(name, base, gate, added):
                links(dve.memset(T[1], 0.0))
                with dve.Fori(0, KT // 2) as i:
                    for m in range(2):
                        s = (base + m) % 2
                        dve.wait_ge(chunk_done, 2 * i + (base + m + 2))
                        x = kt(X, 2 * i + m)
                        if gate is None:
                            dve.tensor_tensor(x, PAIR[s], x, ALU.add).then_inc(free[s], 1)
                        else:
                            mul_add(x, PAIR[s], col(MOD, 2 * i + (gate + m)), x).then_inc(free[s], 1)
                        add_square(2 * i + (added + m), T[1], T[2 + m])

            new_residual("aout", C_AOUT, 2 * KT, KT)
            dve.wait_ge(mod_ready, 2)
            fill_lo("kv", 2, lambda k: col(COEF, KT + k), 3 * KT)
            with dve.Fori(0, KT) as i:
                dve.wait_ge(kv_kh, i + 1)
                low(KSL[:, :], PAIR[0], KSH[:, :]).then_inc(free[0], 1)
                dve.wait_ge(kv_vh, i + 1)
                low(VSL[:, :], PAIR[2], VSH[:, :]).then_inc(free[2], 1)
            fill_lo("qz", 2, lambda k: col(COEF, 2 * KT + k), 5 * KT)

            dve.wait_ge(f_lo, FILL["qz"] + KT)
            for c in bC:
                links(dve.memset(c[:, S:S + 1], 1.0))

            def queries_lo(j, par):
                dve.wait_ge(b_qh, j + 1)
                low(bQL[par][:, :], PAIR[0], bQH[par][:, :]).then_inc(free[0], 1)

            def gate(j, par):
                dve.wait_ge(b_sg, j + 1)
                dve.tensor_tensor(bZS[par][:, :], PAIR[0], bZS[par][:, :], ALU.mult).then_inc(free[0], 1)

            queries_lo(0, 0)
            gate(0, 0)
            dve.wait_ge(free[0], USED["qz"][0] + 2)

            def attention_b(j, par, fill=True, first=False):
                def turned(s, g):
                    if s < 0 and first or g >= len(GROUP_BLOCKS[s % ST]):
                        return
                    bl = blocks_of(s % ST, g)
                    lo, hi = bl[0] * P, (bl[-1] + 1) * P
                    dve.wait_ge(b_ath, 2 * NG * j + (group_index(s) + g + 1))
                    b = (s % 2, bl[0], bl[-1] + 1)
                    low(at_blocks(ATL[s // 2 % 2], *b), turned_blocks(len(bl)), at_blocks(ATH[s // 2 % 2], *b)).then_inc(b_atl, 1)

                def outputs(s):
                    if s % 2 == 0 or s < 0 and first:
                        return
                    h, t = s % (2 * ST) // ST, s % ST
                    rows, b = slice(h * HD, (h + 1) * HD), slice((t - 1) * P, (t + 1) * P)
                    y = bZS[par if s >= 0 else 1 - par][rows, b]
                    o = OB + s // 2 % 2 * 2 * P
                    dve.wait_ge(b_av, ST * j + (s + 1) // 2)
                    dve.tensor_tensor(y, PS[rows, o:o + 2 * P], y, ALU.mult).then_inc(b_o, 1)

                for s in range(2 * ST):
                    n = (s % ST + 1) * P
                    dve.wait_ge(b_c, 2 * ST * j + (s + 1))
                    c = bC[s % 2][:, S - n:S]
                    dve.tensor_tensor_scan(c[:, ::-1], c[:, ::-1], c[:, ::-1], 1.0, ALU.mult, ALU.bypass).then_inc(b_scan, 1)
                    turned(s - 3, 0)
                    outputs(s - 4)
                    turned(s - 3, 1)
                    if fill and s == ST - 1:
                        queries_lo(j + 1, 1 - par)
                    if fill and s == 2 * ST - 1:
                        gate(j + 1, 1 - par)
                if not fill:
                    for s in range(2 * ST, 2 * ST + 4):
                        outputs(s - 4)
                        if s < 2 * ST + 3:
                            turned(s - 3, 0)
                            turned(s - 3, 1)

            attention_b(0, 0, first=True)
            with dve.Fori(0, (KT - 2) // 2) as i:
                for m in range(2):
                    attention_b(2 * i + (1 + m), 1 - m)
            attention_b(KT - 1, 1, fill=False)
            operand_lo("y")
            dve.wait_ge(f_lo, FILL["y"] + KT)
            links(dve.memset(T[1], 0.0))
            links(dve.memset(TP, 0.0))
            dve.wait_ge(ld_xr, 16 * KT)
            with dve.Fori(0, KT // 2) as i:
                for m in range(2):
                    s = (C_BOUT + m) % 2
                    dve.wait_ge(chunk_done, 2 * i + (C_BOUT + m + 2))
                    x = kt(X, 2 * i + m)
                    mul_add(x, PAIR[s], col(MOD, 2 * i + (7 * KT + m)), x).then_inc(free[s], 1)
                    add_square(4 * i + (2 * KT + 2 * m), T[1], T[2])
                    add_square(4 * i + (2 * KT + 2 * m + 1), TP, T[3])
            dve.wait_ge(ms2, 1)
            dve.tensor_tensor(T[3], PAIR[3], T[2], ALU.mult).then_inc(ms2, 1)
            dve.wait_ge(rs, 3)
            links(dve.tensor_tensor(T[0], T[1], T[2], ALU.mult))
            links(dve.tensor_tensor(COEF[:, 3 * KT:4 * KT], VEC[:, _V["final_g"]:_V["final_g"] + KT],
                                    VEC[:, _V["mix_g"]:_V["mix_g"] + KT], ALU.mult))
            fill_lo("mix", 3, lambda k: col(COEF, 3 * KT + k))
            for k in range(KT):
                mul_mul(kt(X, k), kt(X, k), vec("final_g", k), T[1]).then_inc(x_new, 1)

            links(dve.memset(TMP[0][:, 0:PADW], 0.0))
            links(dve.memset(TMP[1][:, 0:PADW], 0.0))
            dve.memset(TMP[4][:, 0:PADW], 0.0).then_inc(p_mx, 1)
            for g, w in enumerate(POOL_W):
                c = C_POOL + g
                dve.wait_ge(free[c % 2], USED["pool"][c % 2] + g // 2 + 1)
                cur, sh = TMP[4], 1
                while sh < w:
                    dst = TMP[1] if cur is not TMP[1] else TMP[0]
                    links(dve.tensor_tensor(dst[:, PADW:], cur[:, PADW:], cur[:, PADW - sh:PADW - sh + S], ALU.add))
                    cur, sh = dst, 2 * sh
                e = _V["edge"] + PADW * g
                links(dve.tensor_tensor(cur[:, PADW:2 * PADW], cur[:, PADW:2 * PADW], VEC[:, e:e + PADW], ALU.mult))
                dve.scalar_tensor_tensor(out=T[3], in0=cur[:, PADW:], scalar=1.0 / w, in1=TP,
                                         op0=ALU.mult, op1=ALU.subtract).then_inc(p_mx, 1)
                dve.wait_ge(p_mh, g + 1)
                low(kt(MXL, g), T[3], kt(MXH, g)).then_inc(p_ml, 1)
            for g in range(4):
                dve.wait_ge(p_yh, g + 1)
                dve.scalar_tensor_tensor(out=kt(YPL, g), in0=PAIR[g % 2], scalar=vec("pool_scale", g),
                                         in1=kt(YPH, g).bitcast(F32), op0=ALU.mult, op1=ALU.subtract).then_inc(p_yl, 1)
            s0, s1 = C_GP % 2, (C_GP + 1) % 2
            with dve.Fori(0, KT) as n:
                dve.wait_ge(free[s0], n + (USED["gp"][s0] + 1))
                dve.wait_ge(chunk_done, 2 * n + (C_GP + 3))
                dve.tensor_tensor(T[2], PAIR[s1], T[1], ALU.mult).then_inc(free[s1], 1)
                dve.wait_ge(gp_st, 16 * n + 16)

            dve.wait_ge(d_ld, 32)
            links(dve.tensor_tensor(dSQ[:, 0:HD], dRS[:, 0:HD], dRS[:, HD:2 * HD], ALU.mult))
            links(dve.tensor_tensor(dSQ[:, HD:2 * HD], dRS[:, 2 * HD:3 * HD], dRS[:, 3 * HD:4 * HD], ALU.mult))
            dve.reduce_sum(SM[:, 8:9], dSQ[:, 0:HD], AX_X)
            dve.reduce_sum(SM[:, 9:10], dSQ[:, HD:2 * HD], AX_X).then_inc(d_lam, 1)
            dve.wait_ge(d_lam, 2)
            links(mul_add(NLAM[:, :], SM[:, 10:11], -1.0, SM[:, 11:12]))
            dve.tensor_scalar(NLAM[:, :], NLAM[:, :], -LAMBDA_INIT, None, ALU.add).then_inc(d_lam, 1)

            def norm_d(raw, gain, n):
                dve.wait_ge(d_rs, n)
                mul_mul(raw[:, :], raw[:, :], gain, dRS[:, :]).then_inc(d_n, 1)

            def lo_d(dst, raw, hi, n):
                dve.wait_ge(d_hi, n)
                return low(dst[:, :], raw[:, :], hi[:, :])

            def slope(j, par):
                dve.tensor_scalar(dSL[par][:, :], IDF[:, :], vec("slope", j), None, ALU.mult).then_inc(d_split, 1)

            norm_d(dQR[0], GQ8[:, 0:1], 1)
            lo_d(dQL[0], dQR[0], dQH[0], 1)
            norm_d(dKR[0], vec("gk"), 2)
            lo_d(dKL[0], dKR[0], dKH[0], 2)
            slope(0, 0)
            ud = USED["qkv2"]

            def attention_d(j, par, fill=True, first=False):
                nxt = 1 - par

                def turned(s, g):
                    if s < 0 and first or g >= len(GROUP_BLOCKS[s % ST]):
                        return
                    bl = blocks_of(s % ST, g)
                    dve.wait_ge(d_ath, NG * j + (group_index(s) + g + 1))
                    b = (s % 2, bl[0], bl[-1] + 1)
                    low(at_blocks(ATL[s // 2 % 2], *b), turned_blocks(len(bl)), at_blocks(ATH[s // 2 % 2], *b)).then_inc(d_atl, 1)

                def outputs(s):
                    if s % 2 == 0 or s < 0 and first:
                        return
                    o = OB + s // 2 % 2 * 2 * P
                    t = s % ST
                    dve.wait_ge(d_av, ST // 2 * j + (s + 1) // 2)
                    if s == 1 and not first:
                        dve.wait_ge(d_st, 16 * j)
                    dve.tensor_copy(dOT[par if s >= 0 else nxt][:, (t - 1) * P:(t + 1) * P], PS[:, o:o + 2 * P]).then_inc(d_o, 1)

                for s in range(ST):
                    n = (s + 1) * P
                    dve.wait_ge(d_s, 2 * ST * j + (2 * s + 1))
                    dve.reduce_max(SM[:, 0:1], PS[:, S:S + n], AX_X)
                    dve.wait_ge(d_s, 2 * ST * j + (2 * s + 2))
                    links(dve.reduce_max(SM[:, 1:2], PS[:, 2 * S:2 * S + n], AX_X))
                    dve.tensor_scalar(SM[:, 2:4], SM[:, 0:2], -1.0, None, ALU.mult).then_inc(d_max, 1)
                    turned(s - 1, 0)
                    turned(s - 1, 1)
                    dve.wait_ge(free[1], ST * j + (ud[1] + s + 1))
                    dve.wait_ge(free[2], ST * j + (ud[2] + s + 1))
                    links(dve.reciprocal(SM[:, 6:8], SM[:, 4:6]))
                    links(dve.tensor_scalar(SM[:, 8:9], SM[:, 7:8], NLAM[:, 0:1], None, ALU.mult))
                    links(dve.tensor_scalar(dP1[:, 0:n], dP1[:, 0:n], SM[:, 8:9], None, ALU.mult))
                    mul_add(dP0[s % 2][:, 0:n], dP0[s % 2][:, 0:n], SM[:, 6:7], dP1[:, 0:n]).then_inc(d_a, 1)
                    outputs(s - 1)
                    if s == 0:
                        dve.wait_ge(d_hi, 3 * j + 3)
                        low(dVL[par][:, :], PAIR[0], dVH[par][:, :]).then_inc(free[0], 1)
                    if s == 1 and not first:
                        norm_d(dOT[nxt], GS8[:, 0:1], 3 * j + 2)
                    if not fill:
                        continue
                    if s == 4:
                        norm_d(dQR[nxt], GQ8[:, 0:1], 3 * j + 3)
                    if s == 5:
                        lo_d(dQL[nxt], dQR[nxt], dQH[nxt], 3 * j + 4)
                    if s == 6:
                        norm_d(dKR[nxt], vec("gk"), 3 * j + 4)
                    if s == 7:
                        lo_d(dKL[nxt], dKR[nxt], dKH[nxt], 3 * j + 5)
                        slope(j + 1, nxt)
                if not fill:
                    turned(ST - 1, 0)
                    turned(ST - 1, 1)
                    outputs(ST - 1)
                    norm_d(dOT[par], GS8[:, 0:1], 3 * KT)

            links_round = 4 * ST
            attention_d(0, 0, first=True)
            with dve.Fori(0, (KT - 2) // 2) as i:
                links.round(i, 2 * links_round)
                for m in range(2):
                    attention_d(2 * i + (1 + m), 1 - m)
            links.end((KT - 2) // 2)
            attention_d(KT - 1, 1, fill=False)
            operand_lo("ab")
            for n in range(KT):
                s = (C_AB + n) % 2
                gate, part = T[n % 2], T[2 + n % 2]
                dve.wait_ge(chunk_done, C_AB + n + 2)
                dve.wait_ge(ab_ld[n % 2], 32 * (n // 2 + 1))
                dve.tensor_tensor(gate, PAIR[s], gate, ALU.mult).then_inc(free[s], 1)
                dve.wait_ge(free[s], USED["ab"][s] + n // 2 + 1)
                dve.tensor_tensor(part, part, gate, ALU.add).then_inc(ab_m, 1)
                dve.wait_ge(g_hi, KT + n + 1)
                low(kt(GL, n), part, kt(GH, n)).then_inc(g_lo, 1)
            dve.wait_ge(ld_xr, 2 * KT * 16)
            new_residual("wo", C_WO, None, 4 * KT)
            fill_lo("ffn", 4, lambda k: vec("ffn_g", k))
            with dve.Fori(0, FFQ) as q:
                with dve.Fori(0, KT // 2) as i:
                    for m in range(2):
                        s = (C_FF + m) % 2
                        dve.wait_ge(ff_r, 2 * i + KT * q + (m + 1))
                        dve.scalar_tensor_tensor(out=T[2 + m], in0=PAIR[s], scalar=0.0, in1=T[m],
                                                 op0=ALU.max, op1=ALU.mult).then_inc(free[s], 1)
                        dve.wait_ge(g_hi, 2 * i + KT * q + (2 * KT + m + 1))
                        low(kt(GL, 2 * i + m), T[2 + m], kt(GH, 2 * i + m)).then_inc(g_lo, 1)
                with dve.Fori(0, KT // 2) as i:
                    for m in range(2):
                        s = (C_FF + m) % 2
                        dve.wait_ge(chunk_done, 2 * i + 2 * KT * q + (C_FF + KT + m + 2))
                        x = kt(X, 2 * i + m)
                        dve.tensor_tensor(x, PAIR[s], x, ALU.add).then_inc(free[s], 1)

        @block.gpsimd
        def _(pool):
            def split_w(c, slot):
                pool.wait_ge(w_hi, c + 1)
                pool.tensor_tensor(WL[slot][:, :], WR0[:, :], WH[slot][:, :].bitcast(F32), ALU.subtract).then_inc(w_lo, 1)

            last = C_QZ + 3
            with pool.Fori(0, last // 2) as i:
                for m in range(2):
                    split_w(2 * i + m, m)
            split_w(last - 1, (last - 1) % 2)

            u = USED["qz"]

            def attention_b(j, fill):
                for s in range(2 * ST):
                    n = (s % ST + 1) * P
                    pool.wait_ge(b_scan, 2 * ST * j + (s + 1))
                    pool.wait_ge(free[1 + s % 2], ST * j + (u[1 + s % 2] + s // 2 + 1))
                    b = bB[s % 4][:, 0:n]
                    pool.tensor_tensor(b, b, bC[s % 2][:, S - n + 1:S + 1], ALU.mult).then_inc(b_a, 1)
                    if fill and s == 1:
                        split_w(2 * j + (C_QZ + 3), 1)
                    if fill and s == ST - 1:
                        split_w(2 * j + (C_QZ + 4), 0)

            with pool.Fori(0, KT - 1) as j:
                attention_b(j, True)
            attention_b(KT - 1, False)
            last = N_CHUNKS + 1
            first = C_BOUT + 1
            with pool.Fori(0, (last - first) // 2) as i:
                for m in range(2):
                    split_w(2 * i + (first + m), (first + m) % 2)
            if (last - first) % 2:
                split_w(last - 1, (last - 1) % 2)


def _chunks(w):
    k, n = w.shape
    a = np.zeros((n // P, P, KT, P), w.dtype)
    a[:, :, :k // P] = w.reshape(k // P, P, n // P, P).transpose(2, 1, 0, 3)
    return a.reshape(n // P, P, D)


def _columns(v):
    return np.asarray(v).reshape(-1, P).T


def kernel(**inputs):
    import concourse.bacc as _bacc
    from concourse.bass_utils import run_bass_kernel_spmd as _run

    f = {k: np.asarray(v) for k, v in inputs.items()}
    ain, kv, qz = _chunks(f["a_w_in"][0]), _chunks(f["w_kv"]), _chunks(f["b_w_qz"][0])
    win, gate = _chunks(f["w_in_2"][0]), _chunks(f["w_gate_2"][0])
    grp = np.zeros((1, P, D), np.float32)
    grp[0, :, 0:4 * P] = f["w_pool_grp_2"][0].transpose(1, 0, 2).reshape(P, 4 * P)
    branch = _chunks(f["w_branch_pool_2"][0])
    up, down = _chunks(f["w_up_2"][0]), f["w_down_2"][0]
    parts = []
    for j in range(KT):
        parts += [ain[KT + j], ain[2 * KT + j], ain[j], ain[3 * KT + j]]
    parts += list(_chunks(f["a_w_out"][0]))
    for j in range(KT):
        parts += [kv[j], kv[KT + j]]
    for j in range(KT):
        parts += [qz[j], qz[KT + j]]
    parts += list(_chunks(f["b_w_out"][0]))
    parts += list(win[0:4]) + [grp[0]]
    for j in range(KT):
        parts += [gate[j], branch[j]]
    parts += list(gate[KT:])
    for j in range(KT):
        parts += [win[4 + j], win[4 + KT + j], win[4 + 2 * KT + j]]
    parts += list(_chunks(f["w_branch_attn_2"][0])) + list(_chunks(f["w_out_2"][0]))
    for q in range(FFQ):
        parts += list(up[q * KT:(q + 1) * KT]) + list(_chunks(down[q * D:(q + 1) * D]))
    parts.append(np.zeros((P, D), np.float32))
    assert len(parts) == N_CHUNKS + 1
    wst = np.stack(parts)
    mods = np.concatenate([f["a_mod_w"][0], f["kv_mod_w"], f["b_mod_w"][0]], axis=1).T.reshape(N_MODS, P, D)
    cb = np.broadcast_to(f["c"], (P, D))

    edge = np.ones((4, PADW), np.float32)
    for g, w in enumerate(POOL_W):
        edge[g, :w] = w / np.arange(1, w + 1)
    two = lambda v: np.concatenate([v, v])
    cols = {
        "mod_b": np.concatenate([f["a_mod_b"][0], f["kv_mod_b"], f["b_mod_b"][0]]),
        "a_g": f["a_norm_g"], "kv_g": f["kv_norm_g"], "b_g": f["b_norm_g"], "conv": f["a_conv_w"][0],
        "final_g": f["final_norm_g"], "mix_g": f["g_mix_2"], "pool_scale": f["pool_scale_2"],
        "gq": two(f["g_q_2"][0]), "gk": two(f["g_k_2"][0]), "gsub": f["g_sub_2"], "b_gate": f["b_gate_2"],
        "ffn_g": f["g_ffn_2"],
    }
    vecs = np.zeros((P, NV), np.float32)
    for name, v in cols.items():
        v = _columns(v)
        vecs[:, _V[name]:_V[name] + v.shape[1]] = v
    vecs[:, _V["slope"]:_V["slope"] + KT] = 2.0 ** -np.arange(1.0, KT + 1)
    vecs[:, _V["edge"]:_V["edge"] + 4 * PADW] = edge.reshape(-1)

    q, k = np.arange(P)[:, None], np.arange(P)[None, :]
    rel = np.arange(S)[None, :] - (S - P)
    consts = np.zeros((P, NC_), np.float32)
    consts[:, K_ID:K_ID + P] = np.eye(P)
    consts[:, K_TRI:K_TRI + P] = np.where(k >= q, -BIG, 0.0)
    consts[:, K_BD:K_BD + P] = q // HD == k // HD
    consts[:, K_DIST:K_DIST + S] = np.where(np.floor_divide(rel, 64) <= q // 64, -np.abs(q - rel), -BIG)
    consts[:, K_LAM:] = f["lambda_qk_2"].reshape(1, 4 * HD)

    xt = f["x"][0].T.reshape(KT, P, S).transpose(1, 0, 2).reshape(P, KT * S)

    nc = _bacc.Bacc("TRN2", target_bir_lowering=False, num_devices=1)
    arrays = {n: np.ascontiguousarray(a, np.float32) for n, a in
              (("xt", xt), ("cb", cb), ("vecs", vecs), ("consts", consts), ("mods", mods), ("wst", wst))}
    args = [nc.dram_tensor(n, a.shape, F32, kind="ExternalInput").ap() for n, a in arrays.items()]
    out = nc.dram_tensor("out", [KT, P, S], F32, kind="ExternalOutput").ap()
    block_kernel(nc, *args, out)
    r = _run(nc, [arrays], core_ids=[0])
    return r.results[0]["out"].reshape(D, S).T.reshape(1, S, D)
```

```python
from contextlib import ExitStack

import numpy as np

import concourse.bass as bass
from concourse import mybir

F32 = mybir.dt.float32
F32R = mybir.dt.float32r
ALU = mybir.AluOpType
ACT = mybir.ActivationFunctionType
AX_X = mybir.AxisListType.X
ds = bass.ds

P = 128
D = 1024
S = 1024
KT = D // P
ST = S // P
HALF = 512
DFF = 4 * D
FFQ = DFF // D
EPS = 1e-6
HD = 64
BIG = 2.0 ** 100

C_AIN = 0
C_AOUT = C_AIN + 4 * KT
C_KV = C_AOUT + KT
C_QZ = C_KV + 2 * KT
C_BOUT = C_QZ + 2 * KT
C_POOL = C_BOUT + KT
C_GA = C_POOL + 4
C_GRP = C_GA + KT
C_GP = C_GRP + 1
C_QKV2 = C_GP + 2 * KT
C_AB = C_QKV2 + 3 * KT
C_WO = C_AB + KT
C_FF = C_WO + KT
N_CHUNKS = C_FF + FFQ * 2 * KT
N_MODS_A = 2 * KT
N_MODS = 8 * KT
MODS_J = (N_MODS - N_MODS_A) // KT

_V = {}
_n = 0
for _name, _w in (("mod_b", 64), ("a_g", 8), ("kv_g", 8), ("b_g", 8), ("conv", 24),
                  ("final_g", 8), ("mix_g", 8), ("pool_scale", 4), ("gq", 1), ("gk", 1),
                  ("gsub", 1), ("b_gate", 16), ("ffn_g", 8), ("slope", 8), ("edge", 64)):
    _V[_name] = _n
    _n += _w
NV = _n
K_ID, K_TRI, K_BD, K_DIST, K_LAM = 0, 128, 256, 384, 384 + S
NC_ = K_LAM + 4 * HD
POOL_W = (2, 4, 8, 16)
PADW = 16
LAMBDA_INIT = 0.2


_USES = (("ain", 16, 16, 0), ("aout", 4, 4, 0), ("kv", 8, 8, 8), ("qz", 15, 65, 64),
         ("bout", 4, 4, 0), ("pool", 2, 2, 0), ("ga", 4, 4, 0), ("gp", 8, 8, 0),
         ("qkv2", 24, 64, 64), ("ab", 4, 4, 0), ("wo", 4, 4, 0), ("ff", 32, 32, 0))
USED = {}
_at = (1, 1, 1)
for _name, *_k in _USES:
    USED[_name] = _at
    _at = tuple(x + y for x, y in zip(_at, _k))

_q = USED["qz"]
USED["qz"] = (_q[0] - 1, _q[1] + 1, _q[2])

FILL = {name: KT * n for n, name in enumerate(("a", "kv", "qz", "y", "mix", "ab", "ffn"))}
SCALED = {name: KT * n for n, name in enumerate(("a", "kv", "qz", "mix", "ffn"))}


class Links:

    def __init__(self, eng, sem):
        self.eng, self.sem, self.n = eng, sem, 0
        self.i = self.per = self.k = None

    def round(self, i, per):
        self.i, self.per, self.k = i, per, 0

    def end(self, rounds):
        assert self.k == self.per, (self.k, self.per)
        self.n += self.per * rounds
        self.i = None

    def __call__(self, ins):
        ins.then_inc(self.sem, 1)
        if self.i is None:
            self.n += 1
            self.eng.wait_ge(self.sem, self.n)
        else:
            self.k += 1
            self.eng.wait_ge(self.sem, self.i * self.per + (self.n + self.k))


def blocks_of(t, g):
    return range(4 * g, min(t + 1, 4 * g + 4))


GROUPS = np.cumsum([len(range(0, t + 1, 4)) for t in range(ST)]).tolist()
NG = GROUPS[-1]
D_STEPS = (0, 3, 3, 2, 3, 5, 3, 5)
GROUP_BLOCKS = [[blocks_of(t, g) for g in range(1 + t // 4)] for t in range(ST)]
B_STEPS = (1, 2, 2, 1, 1, 1, 0, 0) * 2


def group_index(s):
    return NG * (s // ST) + (GROUPS[s % ST - 1] if s % ST else 0)


def block_kernel(nc, xt, cb, vecs, consts, mods, wst, out):
    with ExitStack() as ctx:
        def sem(name):
            return ctx.enter_context(nc.semaphore(name))

        at = [nc.sbuf_base]

        def place(name, cols, dt=F32, where=at):
            where[0] = (where[0] + 31) // 32 * 32
            t = nc.alloc_sbuf_tensor_at(name, [P, cols], dt, offset=where[0])
            where[0] += cols * 4
            assert where[0] <= nc.sbuf_usable_end, (name, where[0] - nc.sbuf_usable_end)
            return t

        X_AT = at[0]
        X = place("X", KT * S)
        HH = place("HH", KT * S, F32R)
        HL = place("HL", KT * S, F32R)
        WR0 = place("WR0", D)
        WH = [place(f"WH{i}", D, F32R) for i in range(2)]
        WL = [place(f"WL{i}", D, F32R) for i in range(2)]
        VEC = place("VEC", NV)
        at[0] = (at[0] + 31) // 32 * 32
        MOD_AT = at[0]
        MOD = place("MOD", N_MODS)
        COEF = place("COEF", 4 * KT + 32)
        IDF = place("IDF", P)
        IDR = place("IDR", P, F32R)
        TRIR = place("TRIR", P, F32R)
        ONES = place("ONES", P)
        SM = place("SM", 16)
        EPSC = place("EPSC", 1)
        NLAM = place("NLAM", 1)
        GQ8 = place("GQ8", 1)
        GS8 = place("GS8", 1)
        ATT0 = at[0]
        TMP = [place(f"TMP{i}", S + (0 if i in (2, 3) else PADW)) for i in range(5)]
        T = [t[:, 0:S] for t in TMP]
        TP = TMP[4][:, PADW:]
        SCR0 = at[0]
        CB = T[1]
        MRAW = nc.alloc_sbuf_tensor_at("MRAW", [P, 2 * KT * D], F32, offset=(SCR0 + 31) // 32 * 32)
        MR = T[0]
        GH = place("GH", KT * S, F32R)
        GL = place("GL", KT * S, F32R)
        r = [SCR0]
        KSH, KSL, VSH, VSL = (place(n, S, F32R, r) for n in ("KSH", "KSL", "VSH", "VSL"))
        VST = place("VST", S, F32, r)
        r = [SCR0]
        YPH = place("YPH", 4 * S, F32R, r)
        YPL = place("YPL", 4 * S, F32R, r)
        MXH = place("MXH", 4 * S, F32R, r)
        MXL = place("MXL", 4 * S, F32R, r)
        r = [ATT0]
        bQH, bQL = ([place(f"b{n}{i}", S, F32R, r) for i in range(2)] for n in ("QH", "QL"))
        bZS = [place(f"bZS{i}", S, F32, r) for i in range(2)]
        bKH, bKL, bVH, bVL = ([place(f"b{n}{i}", S, F32R, r) for i in range(2)] for n in ("KH", "KL", "VH", "VL"))
        bC = [place(f"bC{i}", S + 8, F32, r) for i in range(2)]
        bB = [place(f"bB{i}", S, F32, r) for i in range(4)]
        XAT = (X_AT + 31) // 32 * 32
        ATH = [nc.alloc_sbuf_tensor_at(f"ATH{i}", [P, 2 * S], F32R, offset=XAT + 8 * S * i) for i in range(2)]
        ATL = [nc.alloc_sbuf_tensor_at(f"ATL{i}", [P, 2 * S], F32R, offset=XAT + 8 * S * (2 + i)) for i in range(2)]
        r = [ATT0]
        slots = (ATT0 + 31) // 32 * 32
        STG = {name: [nc.alloc_sbuf_tensor_at(f"STG{name}{i}", [P, S], F32, offset=slots + 4 * S * n)
                      for i, n in enumerate(places)] for name, places in (("y", (6, 8, 10, 12)), ("ab", (0, 2, 4, 6)))}
        r = [ATT0]
        ATT = (ATT0 + 31) // 32 * 32
        dQH, dQL, dKH, dKL, dVH, dVL = ([place(f"d{n}{i}", S, F32R, r) for i in range(2)]
                                        for n in ("QH", "QL", "KH", "KL", "VH", "VL"))
        raw_at = [[ATT + (2 * n + i) * 4 * S for i in range(2)] for n in (1, 3, 5)]
        dQR, dKR, dVR = ([nc.alloc_sbuf_tensor_at(f"d{n}{i}", [P, S], F32, offset=a[i]) for i in range(2)]
                         for n, a in zip(("QR", "KR", "VR"), raw_at))
        dSQ, dRS, dP1 = (place("d" + n, S, F32, r) for n in ("SQ", "RS", "P1"))
        dOT = [place(f"dOT{i}", S, F32, r) for i in range(2)]
        dP0 = [place(f"dP0{i}", S, F32, r) for i in range(2)]
        dDIST = place("dDIST", S, F32R, r)
        dSL = [IDR, TRIR]
        r = [MOD_AT]
        dBD = place("dBD", P, F32, r)
        PS = ctx.enter_context(nc.psum_tensor("PS", [P, 8 * HALF], F32))
        PAIR = [PS[:, p * S:(p + 1) * S] for p in range(4)]
        OSUM = (S + HALF, 2 * S + HALF)
        TB = 3 * S
        OB = 3 * S + HALF

        def scratch(name):
            return nc.dram_tensor(name, [KT, P, S], F32, kind="Internal").ap()

        k_hi, k_lo, v_hi, v_lo = (scratch(n) for n in ("k_hi", "k_lo", "v_hi", "v_lo"))
        y_b, m_p, g_a, y_d, x_b, x_d = (scratch(n) for n in ("y_b", "m_p", "g_a", "y_d", "x_b", "x_d"))

        def at_blocks(t, r, lo, hi):
            return t[:, :].rearrange("p (k r q) -> p k r q", r=2, q=P)[:, lo:hi, r, :]

        def turned_blocks(n):
            return PS[:, TB:TB + n * P].rearrange("p (k q) -> p k q", q=P)

        def row(t, i):
            return t[i] if isinstance(i, int) else t[ds(i, 1)].rearrange("a p c -> (a p) c")

        def kt(t, i):
            return t[:, i * S:(i + 1) * S] if isinstance(i, int) else t[:, ds(i * S, S)]

        def col(t, i):
            return t[:, i:i + 1] if isinstance(i, int) else t[:, ds(i, 1)]

        def vec(name, i=0):
            return col(VEC, i + _V[name])

        ld_c = sem("ld_c")
        ld_cb = sem("ld_cb")
        ld_x = [sem(f"ld_x{i}") for i in range(4)]
        ld_ma = [sem(f"ld_ma{i}") for i in range(KT)]
        ld_mod = sem("ld_mod")
        mod_done = sem("mod_done")
        ld_w = sem("ld_w")
        w_hi = sem("w_hi")
        w_lo = sem("w_lo")
        chunk_done = sem("chunk_done")
        free = [sem(f"free{p}") for p in range(3)]
        dve_link = sem("dve_link")
        act_link = sem("act_link")
        s_sig = sem("s_sig")
        s_sc = sem("s_sc")
        s_const = sem("s_const")
        mod_ready = sem("mod_ready")
        sq = sem("sq")
        sq_added = sem("sq_added")
        ss = sem("ss")
        rs = sem("rs")
        ms2 = sem("ms2")
        ftmp = sem("ftmp")
        f_hi = sem("f_hi")
        f_lo = sem("f_lo")
        g_hi = sem("g_hi")
        g_lo = sem("g_lo")
        back = [sem(f"back{i}") for i in range(4)]
        ain_sg = sem("ain_sg")
        ain_y = sem("ain_y")
        kv_t = sem("kv_t")
        kv_kh = sem("kv_kh")
        kv_vh = sem("kv_vh")
        st_k = sem("st_k")
        st_v = sem("st_v")
        b_ld = sem("b_ld")
        b_sg = sem("b_sg")
        b_qh = sem("b_qh")
        b_s = sem("b_s")
        b_c = sem("b_c")
        b_scan = sem("b_scan")
        b_a = sem("b_a")
        b_t = sem("b_t")
        b_ath = sem("b_ath")
        b_atl = sem("b_atl")
        b_av = sem("b_av")
        b_o = sem("b_o")
        b_st = sem("b_st")
        p_mx = sem("p_mx")
        p_mh = sem("p_mh")
        p_ml = sem("p_ml")
        p_g = sem("p_g")
        p_yh = sem("p_yh")
        p_yl = sem("p_yl")
        gp_st = sem("gp_st")
        ga_st = sem("ga_st")
        d_ld = sem("d_ld")
        d_lam = sem("d_lam")
        d_sq = sem("d_sq")
        d_ss = sem("d_ss")
        d_lo = sem("d_lo")
        d_rs = sem("d_rs")
        d_n = sem("d_n")
        d_v = sem("d_v")
        d_vt = sem("d_vt")
        d_hi = sem("d_hi")
        d_split = sem("d_split")
        d_s = sem("d_s")
        d_max = sem("d_max")
        d_a = sem("d_a")
        d_t = sem("d_t")
        d_ath = sem("d_ath")
        d_atl = sem("d_atl")
        d_av = sem("d_av")
        d_o = sem("d_o")
        d_st = sem("d_st")
        ab_ld = [sem(f"ab_ld{i}") for i in range(2)]
        ab_m = sem("ab_m")
        ff_r = sem("ff_r")
        st_out = sem("st_out")
        st_x = sem("st_x")
        ld_xr = sem("ld_xr")
        x_new = sem("x_new")

        block = ctx.enter_context(nc.Block())

        @block.sync
        def _(sp):
            def load_w(c):
                sp.wait_ge(w_lo, c)
                sp.dma_start(WR0[:, :], row(wst, c)).then_inc(ld_w, 16)

            sp.dma_start(CB, cb).then_inc(ld_cb, 16)
            sp.dma_start(VEC[:, :], vecs).then_inc(ld_c, 16)
            for g in range(4):
                sp.dma_start(X[:, 2 * g * S:2 * (g + 1) * S], xt[:, 2 * g * S:2 * (g + 1) * S]).then_inc(ld_x[g], 16)
                if g == 0:
                    sp.dma_start(IDF[:, :], consts[:, K_ID:K_ID + P]).then_inc(ld_c, 16)
                    sp.dma_start(T[0][:, 0:P], consts[:, K_TRI:K_TRI + P]).then_inc(ld_c, 16)
            sp.dma_start(WR0[:, :], wst[0]).then_inc(ld_w, 16)
            for k in range(KT):
                if k == 3:
                    load_w(1)
                for m in (k, KT + k):
                    sp.dma_start(MRAW[:, m * D:(m + 1) * D], mods[m]).then_inc(ld_ma[k], 16)
            load_w(2)
            sp.wait_ge(f_lo, FILL["a"] + KT)

            def load_mod(m):
                sp.wait_ge(mod_done, m)
                sp.dma_start(MR, row(mods, m)).then_inc(ld_mod, 16)

            with sp.Fori(0, KT) as j:
                m = 0
                for n, k in enumerate((2, 2, 1, 1)):
                    for _ in range(k):
                        load_mod(MODS_J * j + (N_MODS_A + m))
                        m += 1
                    load_w(4 * j + (n + 3))
            with sp.Fori(0, KT) as c:
                load_w(c + (C_AOUT + 3))
            sp.wait_ge(sq_added, 2 * KT)
            with sp.Fori(0, KT) as i:
                load_w(2 * i + (C_KV + 3))
                sp.dma_start(row(x_b, i), kt(X, i)).then_inc(st_x, 16)
                sp.wait_ge(free[2], i + (USED["kv"][2] + 1))
                sp.dma_start(row(v_hi, i), VSH[:, :].bitcast(F32)).then_inc(st_v, 16)
                sp.dma_start(row(v_lo, i), VSL[:, :].bitcast(F32)).then_inc(st_v, 16)
                load_w(2 * i + (C_KV + 4))
                sp.wait_ge(free[1], i + (USED["kv"][1] + 1))
                sp.dma_start(row(k_hi, i), KSH[:, :].bitcast(F32)).then_inc(st_k, 16)
                sp.dma_start(row(k_lo, i), KSL[:, :].bitcast(F32)).then_inc(st_k, 16)
            sp.wait_ge(st_k, KT * 32 + 32)
            sp.wait_ge(st_v, KT * 32 + 32)
            sp.wait_ge(st_x, KT * 16)
            def operand_back(src, name):
                for k in range(KT - 2):
                    if k >= 4:
                        sp.wait_ge(f_lo, FILL[name] + k - 3)
                    sp.dma_start(STG[name][k % 4][:, :], src[k]).then_inc(back[k % 4], 16)

            def load_kv(j, par):
                for src, dst in ((k_hi, bKH), (k_lo, bKL), (v_hi, bVH), (v_lo, bVL)):
                    sp.dma_start(dst[par][:, :].bitcast(F32), row(src, j)).then_inc(b_ld, 16)

            sp.wait_ge(f_lo, FILL["qz"] + KT)
            load_kv(0, 0)
            load_w(C_QZ + 3)

            def attention_b(j, par, first=False):
                load_w(2 * j + (C_QZ + 4))
                if not first:
                    sp.wait_ge(b_o, ST * j)
                    sp.dma_start(row(y_b, j - 1), bZS[1 - par][:, :]).then_inc(b_st, 16)
                load_kv(j + 1, 1 - par)
                load_w(2 * j + (C_QZ + 5))

            attention_b(0, 0, first=True)
            with sp.Fori(0, (KT - 2) // 2) as i:
                for m in range(2):
                    attention_b(2 * i + (1 + m), 1 - m)
            sp.wait_ge(b_o, ST * (KT - 1))
            sp.wait_ge(b_st, 16 * (KT - 2))
            operand_back(y_b, "y")
            sp.wait_ge(b_o, ST * KT)
            for k in range(KT):
                sp.dma_start(kt(X, k), x_b[k]).then_inc(ld_xr, 16)

            with sp.Fori(0, KT) as c:
                load_w(c + (C_BOUT + 2))
            with sp.Fori(0, 4) as c:
                load_w(c + (C_POOL + 2))
            with sp.Fori(0, KT // 2) as i:
                for m in range(2):
                    s = (C_GA + m) % 2
                    load_w(2 * i + (C_GA + 2 + m))
                    sp.wait_ge(free[s], i + (USED["ga"][s] + 1))
                    sp.dma_start(row(g_a, 2 * i + m), T[2]).then_inc(ga_st, 16)
            load_w(C_GRP + 2)
            with sp.Fori(0, KT) as n:
                load_w(2 * n + (C_GP + 2))
                load_w(2 * n + (C_GP + 3))
                sp.wait_ge(free[(C_GP + 1) % 2], n + (USED["gp"][(C_GP + 1) % 2] + 1))
                sp.dma_start(row(m_p, n), T[2]).then_inc(gp_st, 16)
                sp.wait_ge(x_new, n + 1)
                sp.dma_start(row(x_d, n), kt(X, n)).then_inc(st_x, 16)
            sp.wait_ge(gp_st, 16 * KT)
            sp.wait_ge(ga_st, 16 * KT)
            sp.wait_ge(st_x, 2 * KT * 16)
            sp.dma_start(dP1[:, :], consts[:, K_DIST:K_DIST + S]).then_inc(d_ld, 16)
            sp.dma_start(dRS[:, 0:4 * HD], consts[:, K_LAM:K_LAM + 4 * HD]).then_inc(d_ld, 16)
            sp.dma_start(dBD[:, :], consts[:, K_BD:K_BD + P]).then_inc(d_st, 16)
            for c in range(3):
                load_w(C_QKV2 + 2 + c)

            def store_outputs(j, par, norms):
                sp.wait_ge(d_n, norms)
                sp.dma_start(row(y_d, j), dOT[par][:, :]).then_inc(d_st, 16)

            def attention_d(j, par, first=False):
                load_w(3 * j + (C_QKV2 + 5))
                if not first:
                    store_outputs(j - 1, 1 - par, 3 * j + 2)
                load_w(3 * j + (C_QKV2 + 6))
                load_w(3 * j + (C_QKV2 + 7))

            attention_d(0, 0, first=True)
            with sp.Fori(0, (KT - 2) // 2) as i:
                for m in range(2):
                    attention_d(2 * i + (1 + m), 1 - m)
            sp.wait_ge(d_s, 2 * ST * (KT - 1))
            sp.wait_ge(d_st, 16 * (KT - 2) + 16)
            operand_back(y_d, "ab")
            sp.wait_ge(d_n, 3 * KT)
            for k in range(KT):
                sp.dma_start(kt(X, k), x_d[k]).then_inc(ld_xr, 16)
            sp.wait_ge(f_lo, FILL["ab"] + KT)
            for n in range(KT):
                if n >= 2:
                    sp.wait_ge(g_lo, KT + n - 1)
                sp.dma_start(T[n % 2], g_a[n]).then_inc(ab_ld[n % 2], 16)
                sp.dma_start(T[2 + n % 2], m_p[n]).then_inc(ab_ld[n % 2], 16)
                load_w(C_AB + 2 + n)
            with sp.Fori(0, KT) as n:
                load_w(n + (C_WO + 2))
            with sp.Fori(0, FFQ * 2 * KT) as n:
                load_w(n + (C_FF + 2))
            with sp.Fori(0, KT // 2) as i:
                for m in range(2):
                    s = (C_FF + m) % 2
                    sp.wait_ge(free[s], i + (USED["ff"][s] + (2 * FFQ - 1) * KT // 2 + 1))
                    sp.dma_start(row(out, 2 * i + m), kt(X, 2 * i + m)).then_inc(st_out, 16)
            sp.wait_ge(st_out, 16 * KT)

        @block.tensor
        def _(pe):
            def mm3(dst0, lh, ll, RH, RL, k, start, stop):
                for l, rr, a, z in ((lh, RH, start, False), (lh, RL, False, False), (ll, RH, False, stop)):
                    for q in (0, HALF):
                        last = pe.matmul(PS[:, dst0 + q:dst0 + q + HALF], l, rr[:, k * S + q:k * S + q + HALF],
                                         start=a, stop=z)
                return last

            def step(c, slot, pair, RH, RL, k, nk=KT):
                if k == 0:
                    pe.wait_ge(w_hi, c + 1)
                    pe.wait_ge(w_lo, c + 1)
                b = slice(k * P, (k + 1) * P)
                last = mm3(pair * S, WH[slot][:, b], WL[slot][:, b], RH, RL, k, k == 0, k == nk - 1)
                if k == nk - 1:
                    last.then_inc(chunk_done, 1)

            def chunk(c, slot, pair, used, RH=HH, RL=HL, nk=KT, operand=None):
                pe.wait_ge(free[pair], used)
                for k in range(nk):
                    if operand:
                        pe.wait_ge(operand[0], operand[1] + (k + 1))
                    step(c, slot, pair, RH, RL, k, nk)

            def two_chunks(c, slots, pairs, used, operand, RH=HH, RL=HL, between=None):
                pe.wait_ge(free[pairs[0]], used[0])
                for k in range(KT):
                    pe.wait_ge(operand[0], operand[1] + (k + 1))
                    step(c, slots[0], pairs[0], RH, RL, k)
                    if k == 1:
                        pe.wait_ge(free[pairs[1]], used[1])
                    if 1 <= k <= 5:
                        step(c + 1, slots[1], pairs[1], RH, RL, k - 1)
                for k in range(5, KT):
                    if k == KT - 1 and between:
                        between()
                    step(c + 1, slots[1], pairs[1], RH, RL, k)

            def chunks(name, base, n, RH, RL, operand=None, first=0):
                u = USED[name]
                with pe.Fori(first, n // 2) as i:
                    for m in range(2):
                        s = (base + m) % 2
                        chunk(2 * i + (base + m), s, s, i + u[s], RH, RL, operand=operand if m == 0 else None)

            def sum_squares(added, acc, dst=2 * S):
                pe.wait_ge(sq_added, added)
                for h in (0, HALF):
                    last = pe.matmul(PS[:, dst + h:dst + h + HALF], ONES[:, :], acc[:, h:h + HALF], start=True, stop=True)
                last.then_inc(ss, 1)

            pe.wait_ge(s_const, 1)
            for k in range(KT):
                pe.wait_ge(sq, k + 1)
                for h in (HALF, 0) if k == KT - 1 else (0, HALF):
                    last = pe.matmul(PS[:, 2 * S + h:2 * S + h + HALF], ONES[:, :], T[2 + k % 2][:, h:h + HALF],
                                     start=(k == 0), stop=(k == KT - 1))
                    if h:
                        last.then_inc(sq_added, 1)
                    elif k == KT - 1:
                        last.then_inc(ss, 1)
            u = USED["ain"]

            def input_chunks(j, first=False):
                if first:
                    two_chunks(C_AIN, (0, 1), (0, 1), u, (f_lo, FILL["a"]))
                for n in range(2 if first else 0, 4):
                    chunk(4 * j + n, n % 2, n % 2, 2 * j + (u[n % 2] + n // 2))

            input_chunks(0, first=True)
            with pe.Fori(1, KT) as j:
                input_chunks(j)
            chunks("aout", C_AOUT, KT, GH, GL, operand=(g_lo, 0))
            sum_squares(2 * KT, T[1])
            u = USED["kv"]
            def kv_chunks(i, first=False):
                def turn_values():
                    pe.wait_ge(free[0], i + (u[0] + 1))
                    pe.wait_ge(free[2], i + u[2])
                    for t in range(ST):
                        b = slice(t * P, (t + 1) * P)
                        last = pe.transpose(PS[:, 2 * S + t * P:2 * S + (t + 1) * P], VST[:, b], IDF[:, :])
                    last.then_inc(kv_t, 1)

                if first:
                    two_chunks(C_KV, (0, 1), (0, 1), u, (f_lo, FILL["kv"]), between=turn_values)
                else:
                    chunk(2 * i + C_KV, 0, 0, i + u[0])
                    pe.wait_ge(free[1], i + u[1])
                    for k in range(KT):
                        if k == 2:
                            turn_values()
                        step(2 * i + (C_KV + 1), 1, 1, HH, HL, k)

            kv_chunks(0, first=True)
            with pe.Fori(1, KT) as i:
                kv_chunks(i)

            def score_parts(base, rows, q, n, QH, QL, KH, KL, open_bank=None):
                for l, rr, a in ((QH, KH, True), (QH, KL, False), (QL, KH, False)):
                    for c0 in range(0, n, HALF):
                        w = min(HALF, n - c0)
                        pe.matmul(PS[:, base + c0:base + c0 + w], l[rows, q], rr[rows, c0:c0 + w], start=a,
                                  stop=(l is QL and open_bank is not None and c0 != open_bank))

            def value_sum(t, n, VH, VL):
                h, l = ATH[n], ATL[n]
                parts = [(kb, v, a) for kb in (0, t, *range(1, t)) for v, a in ((VH, h), (VH, l), (VL, h))]
                if t == 1:
                    parts = [parts[i] for i in (0, 3, 4, 5, 1, 2)]
                for i, (kb, v, a) in enumerate(parts):
                    r = 1 if kb == t else 0
                    last = pe.matmul(PS[:, OB + (2 * n + r) * P:OB + (2 * n + 2) * P], v[:, kb * P:(kb + 1) * P],
                                     a[:, (2 * kb + r) * P:(2 * kb + 2) * P], start=(i == 0), stop=(i == len(parts) - 1))
                return last

            def next_chunk(c, slot, name, k):
                if k == 0:
                    pe.wait_ge(free[0], USED["bout" if name == "y" else name][0])
                pe.wait_ge(f_lo, FILL[name] + k + 1)
                step(c, slot, 0, HH, HL, k)

            u = USED["qz"]
            two_chunks(C_QZ, (0, 1), (0, 1), (u[0] + 1, u[1] - 1), (f_lo, FILL["qz"]))

            def attention_b(j, par, fill=True, first=False):
                def turn(s, g):
                    if s < 0 and first or g >= len(GROUP_BLOCKS[s % ST]):
                        return
                    pe.wait_ge(b_a, 2 * ST * j + (s + 1))
                    if not (first and s == 0 and g == 0):
                        pe.wait_ge(b_atl, 2 * NG * j + (group_index(s) + g))
                    for n, kb in enumerate(blocks_of(s % ST, g)):
                        last = pe.transpose(PS[:, TB + n * P:TB + (n + 1) * P], bB[s % 4][:, kb * P:(kb + 1) * P], IDF[:, :])
                    last.then_inc(b_t, 1)

                def scores(s):
                    h, t = s // ST, s % ST
                    base = (1 + s % 2) * S
                    pe.wait_ge(free[1 + s % 2], ST * j + (u[1 + s % 2] + s // 2))
                    score_parts(base, slice(h * HD, (h + 1) * HD), slice(t * P, (t + 1) * P), (t + 1) * P,
                                bQH[par], bQL[par], bKH[par], bKL[par], open_bank=t * P // HALF * HALF)
                    pe.matmul(PS[:, base + t * P:base + (t + 1) * P], IDR[:, :], TRIR[:, :],
                              start=False, stop=True).then_inc(b_s, 1)

                def values(s):
                    if s % 2 == 0 or s < 0 and first:
                        return
                    if not (first and s < 4):
                        pe.wait_ge(b_o, ST * j + (s + 1) // 2 - 2)
                    pe.wait_ge(b_atl, 2 * NG * j + group_index(s + 1))
                    v = par if s >= 0 else 1 - par
                    value_sum(s % ST, s // 2 % 2, bVH[v], bVL[v]).then_inc(b_av, 1)

                pe.wait_ge(free[0], (u[0] + 2) if first else 2 * j + (u[0] + 1))
                pe.wait_ge(b_ld, 64 * j + 64)
                k = 0

                def steps(n):
                    nonlocal k
                    for _ in range(n if fill else 0):
                        if k % KT == 0:
                            pe.wait_ge(free[0], 2 * j + (u[0] + 2 + k // KT))
                        step(2 * j + (C_QZ + 2 + k // KT), k // KT, 0, HH, HL, k % KT)
                        k += 1

                for s in range(2 * ST):
                    scores(s)
                    steps(B_STEPS[s] // 2)
                    turn(s - 3, 0)
                    if not fill and 6 <= s < 5 + KT:
                        next_chunk(C_BOUT, 0, "y", s - 6)
                    steps(B_STEPS[s] - B_STEPS[s] // 2)
                    values(s - 4)
                    turn(s - 3, 1)
                if fill:
                    return
                for s in range(2 * ST, 2 * ST + 4):
                    values(s - 4)
                    if s < 2 * ST + 3:
                        turn(s - 3, 0)
                        turn(s - 3, 1)

            attention_b(0, 0, first=True)
            with pe.Fori(0, (KT - 2) // 2) as i:
                for m in range(2):
                    attention_b(2 * i + (1 + m), 1 - m)
            attention_b(KT - 1, 1, fill=False)
            next_chunk(C_BOUT, 0, "y", KT - 1)
            chunk(C_BOUT + 1, 1, 1, USED["bout"][1])
            chunks("bout", C_BOUT, KT, HH, HL, first=1)
            sum_squares(4 * KT, T[1])
            sum_squares(4 * KT, TP, dst=3 * S)

            uu = USED["pool"]
            s0, s1 = C_POOL % 2, (C_POOL + 1) % 2
            two_chunks(C_POOL, (s0, s1), (s0, s1), (uu[s0], uu[s1]), (f_lo, FILL["mix"]))
            for g in (2, 3):
                s = (C_POOL + g) % 2
                chunk(C_POOL + g, s, s, uu[s] + 1)
            chunks("ga", C_GA, KT, HH, HL)
            cg = C_GRP
            u = USED["gp"]
            pe.wait_ge(w_lo, cg + 1)
            for g in range(4):
                b = slice(g * P, (g + 1) * P)
                pe.wait_ge(p_ml, g + 1)
                if g < 2:
                    pe.wait_ge(free[g], u[g])
                else:
                    pe.wait_ge(p_yl, g - 1)
                last = mm3((g % 2) * S, WH[cg % 2][:, b], WL[cg % 2][:, b], MXH, MXL, g, True, True)
                last.then_inc(p_g if g < 3 else chunk_done, 1)
            s0, s1 = C_GP % 2, (C_GP + 1) % 2
            pe.wait_ge(p_yl, 4)
            with pe.Fori(0, KT) as n:
                chunk(2 * n + C_GP, s0, s0, n + u[s0])
                chunk(2 * n + (C_GP + 1), s1, s1, n + u[s1], YPH, YPL, nk=4)

            ud = USED["qkv2"]

            def group_sums(n):
                pe.wait_ge(d_sq, n)
                for h in (0, HALF):
                    last = pe.matmul(PS[:, h:h + HALF], dBD[:, :], dSQ[:, h:h + HALF], start=True, stop=True)
                last.then_inc(d_ss, 1)

            def turn_values(j, par):
                pe.wait_ge(d_v, j + 1)
                for t in range(ST):
                    b = slice(t * P, (t + 1) * P)
                    last = pe.transpose(PS[:, b], dVR[par][:, b], IDF[:, :])
                last.then_inc(d_vt, 1)

            def output_sums(n):
                pe.wait_ge(d_sq, n)
                for h, o in enumerate(OSUM):
                    last = pe.matmul(PS[:, o:o + HALF], ONES[:, :], dSQ[:, h * HALF:(h + 1) * HALF], start=True, stop=True)
                last.then_inc(d_ss, 1)

            pe.wait_ge(d_st, 16)
            for n in range(3):
                chunk(C_QKV2 + n, (C_QKV2 + n) % 2, 0, ud[0] + n)
                if n < 2:
                    group_sums(n + 1)

            def attention_d(j, par, fill=True, first=False):
                used = 3 * j + (ud[0] + 2)

                def turn(s, g):
                    if s < 0 and first or g >= len(GROUP_BLOCKS[s % ST]):
                        return
                    pe.wait_ge(d_a, ST * j + (s + 1))
                    if not (first and s == 0 and g == 0):
                        pe.wait_ge(d_atl, NG * j + (group_index(s) + g))
                    for n, kb in enumerate(blocks_of(s % ST, g)):
                        last = pe.transpose(PS[:, TB + n * P:TB + (n + 1) * P], dP0[s % 2][:, kb * P:(kb + 1) * P], IDF[:, :])
                    last.then_inc(d_t, 1)

                def scores(s, m):
                    n = (s + 1) * P
                    base = (1 + m) * S
                    pe.wait_ge(free[1 + m], ST * j + (ud[1 + m] + s))
                    score_parts(base, slice(m * HD, (m + 1) * HD), slice(s * P, (s + 1) * P), n,
                                dQH[par], dQL[par], dKH[par], dKL[par])
                    for c0 in range(0, n, HALF):
                        w = min(HALF, n - c0)
                        last = pe.matmul(PS[:, base + c0:base + c0 + w], dSL[par][:, :], dDIST[:, S - n + c0:S - n + c0 + w],
                                         start=False, stop=True)
                    last.then_inc(d_s, 1)

                def values(s):
                    if s % 2 == 0 or s < 0 and first:
                        return
                    if not (first and s < 4):
                        pe.wait_ge(d_o, ST // 2 * j + (s + 1) // 2 - 2)
                    if s == 1:
                        pe.wait_ge(free[0], used + 1)
                    pe.wait_ge(d_atl, NG * j + group_index(s + 1))
                    v = par if s >= 0 else 1 - par
                    value_sum(s % ST, s // 2 % 2, dVH[v], dVL[v]).then_inc(d_av, 1)

                k = 0

                def steps(n):
                    nonlocal k
                    for _ in range(n if fill else 0):
                        c = k // KT
                        if k % KT == 0:
                            pe.wait_ge(free[0], used + (1 + c))
                        step(3 * j + (C_QKV2 + 3 + c), (C_QKV2 + 3 * par + 3 + c) % 2, 0, HH, HL, k % KT)
                        k += 1

                pe.wait_ge(d_split, j + 1)
                for s in range(ST):
                    scores(s, 0)
                    scores(s, 1)
                    turn(s - 1, 0)
                    if s == 0:
                        turn_values(j, par)
                    if s == 2 and not first:
                        output_sums(3 * j + 2)
                    if fill and s in (4, 6):
                        group_sums(3 * j + (3 if s == 4 else 4))
                    early = 0 if s in (4, 6) else (D_STEPS[s] + 1) // 2
                    steps(early)
                    if not fill and s >= 3:
                        next_chunk(C_AB, C_AB % 2, "ab", s - 3)
                    turn(s - 1, 1)
                    values(s - 1)
                    steps(D_STEPS[s] - early)
                if fill:
                    return
                turn(ST - 1, 0)
                next_chunk(C_AB, C_AB % 2, "ab", ST - 3)
                turn(ST - 1, 1)
                next_chunk(C_AB, C_AB % 2, "ab", ST - 2)
                values(ST - 1)
                for m in (1, 2):
                    pe.wait_ge(free[m], ud[m] + ST * KT)
                output_sums(3 * KT)

            attention_d(0, 0, first=True)
            with pe.Fori(0, (KT - 2) // 2) as i:
                for m in range(2):
                    attention_d(2 * i + (1 + m), 1 - m)
            attention_d(KT - 1, 1, fill=False)
            next_chunk(C_AB, C_AB % 2, "ab", KT - 1)
            u = USED["ab"]
            pe.wait_ge(d_lo, KT)
            chunk(C_AB + 1, (C_AB + 1) % 2, 1, u[1])
            with pe.Fori(1, KT // 2) as i:
                for m in range(2):
                    chunk(2 * i + (C_AB + m), (C_AB + m) % 2, m, i + u[m])
            chunks("wo", C_WO, KT, GH, GL, operand=(g_lo, KT))
            sum_squares(5 * KT, T[1])

            u = USED["ff"]
            slots = (C_FF % 2, (C_FF + 1) % 2)

            def quarter(q, first=False):
                for down, (RH, RL) in enumerate(((HH, HL), (GH, GL))):
                    start = first and not down
                    if start:
                        two_chunks(C_FF, slots, slots, [u[p] for p in slots], (f_lo, FILL["ffn"]))
                    with pe.Fori(1 if start else 0, KT // 2) as i:
                        for m, p in enumerate(slots):
                            chunk(2 * i + 2 * KT * q + (C_FF + KT * down + m), p, p, i + KT * q + (u[p] + KT // 2 * down),
                                  RH, RL, operand=(g_lo, KT * q + 2 * KT) if down and m == 0 else None)

            quarter(0, first=True)
            with pe.Fori(1, FFQ) as q:
                quarter(q)

        @block.scalar
        def _(act):
            links = Links(act, act_link)

            def split_w(c, slot):
                act.wait_ge(ld_w, 16 * c + 16)
                if not (isinstance(c, int) and c == 0):
                    act.wait_ge(chunk_done, c)
                act.activation(WH[slot][:, :], WR0[:, :], ACT.Identity).then_inc(w_hi, 1)

            def root(dst, src, tmp):
                links(act.activation(tmp, src, ACT.Ln, bias=EPSC[:, 0:1], scale=1.0 / D))
                act.activation(dst, tmp, ACT.Exp, scale=-0.5).then_inc(rs, 1)

            def fill_hi(name, shift=None):
                for k in range(KT):
                    act.wait_ge(ftmp, SCALED[name] + k + 1)
                    kw = {} if shift is None else {"bias": col(MOD, shift + k)}
                    act.activation(kt(HH, k), T[2 + k % 2], ACT.Identity, **kw).then_inc(f_hi, 1)
                    if name == "a" and k == 0:
                        split_w1()

            def operand_hi(name, k, own):
                if k < KT - 2:
                    times = (1 + (k % 4 < 2)) * (name == "ab") + k // 4 + 1
                    act.wait_ge(back[k % 4], 16 * times)
                src = STG[name][k % 4] if k < KT - 2 else own[k % 2]
                act.activation(kt(HH, k), src[:, :], ACT.Identity).then_inc(f_hi, 1)

            def split_w1():
                act.wait_ge(ld_w, 32)
                act.activation(WH[1][:, :], WR0[:, :], ACT.Identity).then_inc(w_hi, 1)

            act.wait_ge(ld_cb, 16)
            act.activation(TP, CB, ACT.Sigmoid).then_inc(s_sig, 1)
            act.wait_ge(ld_c, 48)
            act.activation(IDR[:, :], IDF[:, :], ACT.Identity)
            act.activation(TRIR[:, :], T[0][:, 0:P], ACT.Identity)
            for k in range(KT):
                act.wait_ge(ld_x[k // 2], 16)
                if k >= 2:
                    act.wait_ge(sq_added, k - 1)
                act.activation(T[2 + k % 2], kt(X, k), ACT.Square).then_inc(sq, 1)
            act.wait_ge(s_sc, 1)
            act.wait_ge(ss, 1)
            split_w(0, 0)
            root(T[0], PAIR[2], TP)
            fill_hi("a", 0)
            with act.Fori(0, KT) as j:
                act.wait_ge(chunk_done, 4 * j + 2)
                act.activation(T[2], PAIR[0], ACT.Identity).then_inc(free[0], 1)
                split_w(4 * j + 2, 0)
                split_w(4 * j + 3, 1)
                split_w(4 * j + 4, 0)
                act.wait_ge(chunk_done, 4 * j + 5)
                act.wait_ge(free[1], 2 * j + 2)
                act.activation(T[2], PAIR[1], ACT.Sigmoid).then_inc(ain_sg, 1)
                split_w(4 * j + 5, 1)
                act.wait_ge(ain_y, j + 1)
                act.activation(kt(GH, j), T[3], ACT.Identity).then_inc(g_hi, 1)

            def squares_of_new(name, base, added, ahead):
                with act.Fori(0, KT // 2) as i:
                    for m in range(2):
                        s = (base + m) % 2
                        if not ahead:
                            split_w(2 * i + (base + m + 1), 1 - s)
                        act.wait_ge(free[s], i + (USED[name][s] + 1))
                        act.wait_ge(sq_added, 2 * i + (added + m - 1))
                        act.activation(T[2 + m], kt(X, 2 * i + m), ACT.Square).then_inc(sq, 1)
                        if ahead:
                            split_w(2 * i + (base + m + 2), s)

            squares_of_new("aout", C_AOUT, KT, True)
            act.wait_ge(ss, 2)
            root(T[0], PAIR[2], TP)
            act.wait_ge(mod_ready, 1)
            fill_hi("kv", 3 * KT)
            with act.Fori(0, KT) as i:
                act.wait_ge(chunk_done, 2 * i + (C_KV + 2))
                act.activation(VST[:, :], PAIR[0], ACT.Identity).then_inc(free[0], 1)
                split_w(2 * i + (C_KV + 2), 0)
                act.wait_ge(kv_t, i + 1)
                act.wait_ge(st_v, 32 * i + 32)
                act.activation(VSH[:, :], PAIR[2], ACT.Identity).then_inc(kv_vh, 1)
                act.wait_ge(chunk_done, 2 * i + (C_KV + 3))
                act.wait_ge(st_k, 32 * i + 32)
                act.activation(KSH[:, :], PAIR[1], ACT.Identity).then_inc(kv_kh, 1)
                split_w(2 * i + (C_KV + 3), 1)

            fill_hi("qz", 5 * KT)
            act.wait_ge(f_lo, FILL["qz"] + KT)
            act.wait_ge(chunk_done, C_QZ + 2)
            act.activation(bQH[0][:, :], PAIR[0], ACT.Identity).then_inc(b_qh, 1)
            split_w(C_QZ + 2, 0)
            act.wait_ge(chunk_done, C_QZ + 3)
            act.activation(bZS[0][:, :], PAIR[1], ACT.Sigmoid).then_inc(b_sg, 1)

            def attention_b(j, par, fill=True, first=False):
                def turned(s, g):
                    if s < 0 and first or g >= len(GROUP_BLOCKS[s % ST]):
                        return
                    bl = blocks_of(s % ST, g)
                    act.wait_ge(b_t, 2 * NG * j + (group_index(s) + g + 1))
                    if g == 0 and s % 2 == 0 and not (first and s < 4):
                        act.wait_ge(b_av, ST * j + s // 2 - 1)
                    act.activation(at_blocks(ATH[s // 2 % 2], s % 2, bl[0], bl[-1] + 1), turned_blocks(len(bl)),
                                   ACT.Identity).then_inc(b_ath, 1)

                for s in range(2 * ST):
                    n = (s % ST + 1) * P
                    src = PS[:, (1 + s % 2) * S:(1 + s % 2) * S + n]
                    act.wait_ge(b_s, 2 * ST * j + (s + 1))
                    if not (first and s < 2):
                        act.wait_ge(b_a, 2 * ST * j + (s - 1))
                    act.activation(bC[s % 2][:, S - n:S], src, ACT.Sigmoid, scale=-HD ** -0.5).then_inc(b_c, 1)
                    turned(s - 3, 0)
                    act.activation(bB[s % 4][:, 0:n], src, ACT.Sigmoid, scale=HD ** -0.5).then_inc(free[1 + s % 2], 1)
                    turned(s - 3, 1)
                    if not fill and 5 <= s < 4 + KT:
                        operand_hi("y", s - 5, bZS)
                    if fill and s == 1:
                        split_w(2 * j + (C_QZ + 3), 1)
                    if fill and s == 5:
                        act.wait_ge(chunk_done, 2 * j + (C_QZ + 4))
                        act.activation(bQH[1 - par][:, :], PAIR[0], ACT.Identity).then_inc(b_qh, 1)
                    if fill and s == 9:
                        split_w(2 * j + (C_QZ + 4), 0)
                    if fill and s == 13:
                        act.wait_ge(chunk_done, 2 * j + (C_QZ + 5))
                        if not first:
                            act.wait_ge(b_st, 16 * j)
                        act.activation(bZS[1 - par][:, :], PAIR[0], ACT.Sigmoid).then_inc(b_sg, 1)
                if not fill:
                    for s in range(2 * ST - 3, 2 * ST):
                        turned(s, 0)
                        turned(s, 1)
                    act.wait_ge(b_o, ST * KT)
                    operand_hi("y", KT - 1, bZS)

            attention_b(0, 0, first=True)
            with act.Fori(0, (KT - 2) // 2) as i:
                for m in range(2):
                    attention_b(2 * i + (1 + m), 1 - m)
            attention_b(KT - 1, 1, fill=False)
            act.wait_ge(f_lo, FILL["y"] + KT)
            with act.Fori(0, KT // 2) as i:
                for m in range(2):
                    s = (C_BOUT + m) % 2
                    split_w(2 * i + (C_BOUT + m + 1), 1 - s)
                    act.wait_ge(free[s], i + (USED["bout"][s] + 1))
                    act.wait_ge(sq_added, 4 * i + (2 * KT + 2 * m))
                    act.activation(T[2], kt(X, 2 * i + m), ACT.Square).then_inc(sq, 1)
                    act.activation(T[3], kt(X, 2 * i + m), ACT.Square, scale=vec("final_g", 2 * i + m)).then_inc(sq, 1)
            split_w(C_POOL + 1, (C_POOL + 1) % 2)
            act.wait_ge(ss, 3)
            links(act.activation(T[2], PAIR[2], ACT.Ln, bias=EPSC[:, 0:1], scale=1.0 / D))
            act.activation(T[3], T[2], ACT.Exp, scale=-1.0).then_inc(ms2, 1)
            links(act.activation(T[1], T[2], ACT.Exp, scale=-0.5))
            act.wait_ge(ms2, 2)
            links(act.activation(T[3], T[3], ACT.Ln, bias=EPSC[:, 0:1], scale=1.0 / D))
            act.activation(T[2], T[3], ACT.Exp, scale=-0.5).then_inc(rs, 1)
            fill_hi("mix")

            act.wait_ge(p_mx, 1)
            for g in range(4):
                c = C_POOL + g
                if g:
                    split_w(c + 1, (c + 1) % 2)
                act.wait_ge(chunk_done, c + 2)
                act.activation(TP, PAIR[c % 2], ACT.Identity).then_inc(free[c % 2], 1)
                act.wait_ge(p_mx, g + 2)
                act.activation(kt(MXH, g), T[3], ACT.Identity).then_inc(p_mh, 1)
            with act.Fori(0, KT // 2) as i:
                for m in range(2):
                    s = (C_GA + m) % 2
                    split_w(2 * i + (C_GA + m + 1), 1 - s)
                    act.wait_ge(chunk_done, 2 * i + (C_GA + m + 2))
                    act.activation(T[2], PAIR[s], ACT.Sigmoid, bias=vec("b_gate", 2 * i + (8 + m))).then_inc(free[s], 1)
                    act.wait_ge(ga_st, 32 * i + 16 * (m + 1))
            split_w(C_GRP + 1, (C_GRP + 1) % 2)
            for g in range(4):
                if g < 3:
                    act.wait_ge(p_g, g + 1)
                else:
                    act.wait_ge(chunk_done, C_GRP + 2)
                act.activation(kt(YPH, g), PAIR[g % 2], ACT.Identity, scale=vec("pool_scale", g)).then_inc(p_yh, 1)
            s0, s1 = C_GP % 2, (C_GP + 1) % 2
            with act.Fori(0, KT) as n:
                split_w(2 * n + (C_GP + 1), s1)
                act.wait_ge(chunk_done, 2 * n + (C_GP + 2))
                act.activation(T[1], PAIR[s0], ACT.Sigmoid, bias=vec("b_gate", n)).then_inc(free[s0], 1)
                split_w(2 * n + (C_GP + 2), s0)
                act.wait_ge(free[s1], n + (USED["gp"][s1] + 1))

            act.wait_ge(d_lam, 1)
            act.activation(SM[:, 10:12], SM[:, 8:10], ACT.Exp).then_inc(d_lam, 1)
            act.activation(dDIST[:, :], dP1[:, :], ACT.Identity)
            ud = USED["qkv2"]

            def squares_d(c, raw, n):
                act.wait_ge(chunk_done, c + 2)
                act.activation(raw[:, :], PAIR[0], ACT.Identity)
                if not (isinstance(n, int) and n == 1):
                    act.wait_ge(d_rs, n - 1)
                act.activation(dSQ[:, :], PAIR[0], ACT.Square).then_inc(d_sq, 1)

            def ln_d(n):
                act.wait_ge(d_ss, n)
                act.activation(dSQ[:, :], PAIR[0], ACT.Ln, bias=EPSC[:, 0:1], scale=1.0 / HD).then_inc(free[0], 1)

            def ln_outputs(n):
                act.wait_ge(d_ss, n)
                for h, o in enumerate(OSUM):
                    last = act.activation(dSQ[:, h * HALF:(h + 1) * HALF], PS[:, o:o + HALF], ACT.Ln,
                                          bias=EPSC[:, 0:1], scale=1.0 / P)
                last.then_inc(d_lo, 1)

            def exp_d(n, sem, count):
                act.wait_ge(sem, count)
                if not (isinstance(n, int) and n == 1):
                    act.wait_ge(d_n, n - 1)
                act.activation(dRS[:, :], dSQ[:, :], ACT.Exp, scale=-0.5).then_inc(d_rs, 1)

            def hi_d(dst, src, n):
                act.wait_ge(d_n, n)
                act.activation(dst[:, :], src[:, :], ACT.Identity).then_inc(d_hi, 1)

            def stage_values(c, par):
                act.wait_ge(chunk_done, c + 2)
                act.activation(dVR[par][:, :], PAIR[0], ACT.Identity).then_inc(d_v, 1)

            act.wait_ge(d_lam, 3)
            for n, (hi, raw) in enumerate(((dQH[0], dQR[0]), (dKH[0], dKR[0]))):
                split_w(C_QKV2 + n + 1, (C_QKV2 + n + 1) % 2)
                squares_d(C_QKV2 + n, raw, n + 1)
                ln_d(n + 1)
                exp_d(n + 1, free[0], ud[0] + n + 1)
                hi_d(hi, raw, n + 1)
            split_w(C_QKV2 + 3, (C_QKV2 + 3) % 2)
            stage_values(C_QKV2 + 2, 0)

            def attention_d(j, par, fill=True, first=False):
                used = 3 * j + (ud[0] + 2)
                nxt = 1 - par

                def turned(s, g):
                    if s < 0 and first or g >= len(GROUP_BLOCKS[s % ST]):
                        return
                    bl = blocks_of(s % ST, g)
                    act.wait_ge(d_t, NG * j + (group_index(s) + g + 1))
                    if g == 0 and s % 2 == 0 and not (first and s < 4):
                        act.wait_ge(d_av, ST // 2 * j + s // 2 - 1)
                    act.activation(at_blocks(ATH[s // 2 % 2], s % 2, bl[0], bl[-1] + 1), turned_blocks(len(bl)),
                                   ACT.Identity).then_inc(d_ath, 1)

                for s in range(ST):
                    if fill and s == 5:
                        hi_d(dQH[nxt], dQR[nxt], 3 * j + 3)
                    if fill and s == 7:
                        hi_d(dKH[nxt], dKR[nxt], 3 * j + 4)
                    turned(s - 1, 0)
                    late = s in (5, 7)
                    if not late:
                        turned(s - 1, 1)
                    if s == 2 and not first:
                        ln_outputs(3 * j + 2)
                    if fill and s in (4, 6):
                        ln_d(3 * j + (3 if s == 4 else 4))
                    w = (s + 1) * P
                    act.wait_ge(d_max, ST * j + (s + 1))
                    act.activation(dP0[s % 2][:, 0:w], PS[:, S:S + w], ACT.Exp, bias=SM[:, 2:3],
                                   accum_out=SM[:, 4:5]).then_inc(free[1], 1)
                    act.activation(dP1[:, 0:w], PS[:, 2 * S:2 * S + w], ACT.Exp, bias=SM[:, 3:4],
                                   accum_out=SM[:, 5:6]).then_inc(free[2], 1)
                    if late:
                        turned(s - 1, 1)
                    if s == 0:
                        act.wait_ge(d_vt, j + 1)
                        act.activation(dVH[par][:, :], PAIR[0], ACT.Identity).then_inc(d_hi, 1)
                        if fill:
                            split_w(3 * j + (C_QKV2 + 4), (C_QKV2 + 3 * par + 4) % 2)
                        if not first:
                            act.wait_ge(d_o, ST // 2 * j)
                            act.wait_ge(d_rs, 3 * j + 1)
                            act.activation(dSQ[:, :], dOT[nxt][:, :], ACT.Square).then_inc(d_sq, 1)
                    if s == 2 and not first:
                        exp_d(3 * j + 2, d_lo, j)
                    if not fill:
                        if s >= 2:
                            operand_hi("ab", s - 2, dOT)
                        if s == ST - 1:
                            operand_hi("ab", KT - 2, dOT)
                        continue
                    if s == 3:
                        squares_d(3 * j + (C_QKV2 + 3), dQR[nxt], 3 * j + 3)
                        split_w(3 * j + (C_QKV2 + 5), (C_QKV2 + 3 * par + 5) % 2)
                    if s == 4:
                        exp_d(3 * j + 3, free[0], used + 2)
                    if s == 5:
                        squares_d(3 * j + (C_QKV2 + 4), dKR[nxt], 3 * j + 4)
                        split_w(3 * j + (C_QKV2 + 6), (C_QKV2 + 3 * par + 6) % 2)
                    if s == 6:
                        exp_d(3 * j + 4, free[0], used + 3)
                    if s == 7:
                        stage_values(3 * j + (C_QKV2 + 5), nxt)
                if not fill:
                    turned(ST - 1, 0)
                    turned(ST - 1, 1)
                    act.wait_ge(d_o, ST // 2 * KT)
                    act.wait_ge(d_rs, 3 * KT - 1)
                    act.activation(dSQ[:, :], dOT[par][:, :], ACT.Square).then_inc(d_sq, 1)
                    ln_outputs(3 * KT)
                    exp_d(3 * KT, d_lo, KT)
                    act.wait_ge(d_n, 3 * KT)
                    operand_hi("ab", KT - 1, dOT)

            attention_d(0, 0, first=True)
            with act.Fori(0, (KT - 2) // 2) as i:
                for m in range(2):
                    attention_d(2 * i + (1 + m), 1 - m)
            attention_d(KT - 1, 1, fill=False)
            for n in range(KT):
                c = C_AB + n
                split_w(c + 1, (c + 1) % 2)
                act.wait_ge(ab_m, n + 1)
                act.activation(kt(GH, n), T[2 + n % 2], ACT.Identity).then_inc(g_hi, 1)
            squares_of_new("wo", C_WO, 4 * KT, False)
            split_w(C_FF + 1, (C_FF + 1) % 2)
            act.wait_ge(ss, 5)
            root(T[0], PAIR[2], TP)
            fill_hi("ffn")
            u = USED["ff"]
            with act.Fori(0, FFQ) as q:
                with act.Fori(0, KT // 2) as i:
                    for m in range(2):
                        s = (C_FF + m) % 2
                        act.wait_ge(chunk_done, 2 * i + 2 * KT * q + (C_FF + m + 2))
                        act.activation(T[m], PAIR[s], ACT.Relu).then_inc(ff_r, 1)
                        split_w(2 * i + 2 * KT * q + (C_FF + m + 2), s)
                        act.wait_ge(free[s], i + KT * q + (u[s] + 1))
                        act.activation(kt(GH, 2 * i + m), T[2 + m], ACT.Identity).then_inc(g_hi, 1)
                with act.Fori(0, KT // 2) as i:
                    for m in range(2):
                        split_w(2 * i + 2 * KT * q + (C_FF + KT + m + 2), (C_FF + m) % 2)

        @block.vector
        def _(dve):
            links = Links(dve, dve_link)

            def mul_mul(dst, src, scalar, other):
                return dve.scalar_tensor_tensor(out=dst, in0=src, scalar=scalar, in1=other, op0=ALU.mult, op1=ALU.mult)

            def mul_add(dst, src, scalar, other):
                return dve.scalar_tensor_tensor(out=dst, in0=src, scalar=scalar, in1=other, op0=ALU.mult, op1=ALU.add)

            def low(dst, value, high):
                return dve.tensor_tensor(dst, value, high.bitcast(F32), ALU.subtract)

            def add_square(n, acc, src):
                dve.wait_ge(sq, n + 1)
                if not (isinstance(n, int) and n == 0):
                    dve.wait_ge(sq_added, n)
                dve.tensor_tensor(acc, acc, src, ALU.add).then_inc(sq_added, 1)

            def fill_lo(name, n_rs, scale, shift=None, before=None):
                for k in range(KT + 1):
                    if k < KT:
                        if before:
                            before(k)
                        if k == 0:
                            dve.wait_ge(rs, n_rs)
                        if k >= 2:
                            dve.wait_ge(f_lo, FILL[name] + k - 1)
                        mul_mul(T[2 + k % 2], kt(X, k), scale(k), T[0]).then_inc(ftmp, 1)
                    if k:
                        dve.wait_ge(f_hi, FILL[name] + k)
                        hi = kt(HH, k - 1).bitcast(F32)
                        tmp = T[2 + (k - 1) % 2]
                        if shift is None:
                            lo = dve.tensor_tensor(kt(HL, k - 1), tmp, hi, ALU.subtract)
                        else:
                            lo = dve.scalar_tensor_tensor(out=kt(HL, k - 1), in0=tmp, scalar=col(MOD, shift + k - 1),
                                                          in1=hi, op0=ALU.add, op1=ALU.subtract)
                        lo.then_inc(f_lo, 1)

            def operand_lo(name, k, own):
                dve.wait_ge(f_hi, FILL[name] + k + 1)
                src = STG[name][k % 4] if k < KT - 2 else own[k % 2]
                low(kt(HL, k), src[:, :], kt(HH, k)).then_inc(f_lo, 1)

            def coefficients(a, g, c, done=False):
                ins = dve.scalar_tensor_tensor(out=COEF[:, c:c + KT], in0=MOD[:, a:a + KT], scalar=1.0,
                                               in1=VEC[:, _V[g]:_V[g] + KT], op0=ALU.add, op1=ALU.mult)
                if done:
                    ins.then_inc(mod_ready, 1)

            dve.memset(ONES[:, :], 1.0).then_inc(chunk_done, 1)
            dve.memset(EPSC[:, :], EPS).then_inc(free[0], 1)
            dve.memset(GQ8[:, :], 0.0).then_inc(st_k, 32)
            dve.memset(GS8[:, :], 0.0).then_inc(st_v, 32)
            dve.memset(NLAM[:, :], 0.0).then_inc(free[1], 1)
            dve.memset(TMP[4][:, 0:PADW], 0.0).then_inc(free[2], 1)
            dve.memset(SM[:, :], 0.0).then_inc(s_const, 1)
            dve.wait_ge(s_sig, 1)
            dve.tensor_tensor(CB, CB, TP, ALU.mult).then_inc(s_sc, 1)
            dve.wait_ge(s_sc, 1)

            def modulation(dst, weights):
                dve.tensor_tensor_reduce(out=weights, in0=weights, in1=CB, scale=1.0, scalar=0.0, op0=ALU.mult, op1=ALU.add,
                                         accum_out=dst).then_inc(mod_done, 1)

            def add_bias(lo, hi):
                dve.wait_ge(mod_done, hi)
                links(dve.tensor_tensor(MOD[:, lo:hi], MOD[:, lo:hi], VEC[:, _V["mod_b"] + lo:_V["mod_b"] + hi], ALU.add))

            dve.wait_ge(ld_c, 48)
            links(dve.tensor_scalar(GQ8[:, :], vec("gq"), HD ** -0.5, None, ALU.mult))
            links(dve.tensor_scalar(GS8[:, :], vec("gsub"), 1.0 - LAMBDA_INIT, None, ALU.mult))

            def shift_and_scale(k):
                dve.wait_ge(ld_ma[k], 32)
                for m in (k, KT + k):
                    modulation(MOD[:, m:m + 1], MRAW[:, m * D:(m + 1) * D])
                dve.wait_ge(mod_done, 2 * k + 2)
                dve.tensor_tensor(col(MOD, k), col(MOD, k), vec("mod_b", k), ALU.add)
                links(dve.tensor_tensor(col(MOD, KT + k), col(MOD, KT + k), vec("mod_b", KT + k), ALU.add))
                links(dve.scalar_tensor_tensor(out=col(COEF, k), in0=col(MOD, KT + k), scalar=1.0, in1=vec("a_g", k),
                                               op0=ALU.add, op1=ALU.mult))

            fill_lo("a", 1, lambda k: col(COEF, k), 0, before=shift_and_scale)

            def modulations(j, first, n):
                for m in range(first, first + n):
                    dve.wait_ge(ld_mod, 16 * MODS_J * j + 16 * (m + 1))
                    modulation(SM[:, m:m + 1], MR)

            with dve.Fori(0, KT) as j:
                links.round(j, 4)
                modulations(j, 0, 2)
                dve.wait_ge(free[0], 2 * j + 2)
                dve.wait_ge(chunk_done, 4 * j + 3)
                dve.tensor_tensor(TP, PAIR[1], T[2], ALU.mult).then_inc(free[1], 1)
                dve.wait_ge(free[1], 2 * j + 2)
                links(dve.tensor_scalar(T[3], TP, vec("conv", j + 2 * KT), None, ALU.mult))
                links(mul_add(T[3], TMP[4][:, PADW - 1:PADW - 1 + S], vec("conv", j + KT), T[3]))
                links(mul_add(T[3], TMP[4][:, PADW - 2:PADW - 2 + S], vec("conv", j), T[3]))
                modulations(j, 2, 2)
                dve.wait_ge(chunk_done, 4 * j + 4)
                dve.tensor_tensor(T[3], PAIR[0], T[3], ALU.mult).then_inc(free[0], 1)
                modulations(j, 4, 2)
                dve.wait_ge(mod_done, MODS_J * j + (N_MODS_A + MODS_J))
                links(dve.tensor_copy(MOD[:, ds(MODS_J * j + N_MODS_A, MODS_J)], SM[:, 0:MODS_J]))
                dve.wait_ge(ain_sg, j + 1)
                dve.tensor_tensor(T[2], PAIR[1], T[2], ALU.mult).then_inc(free[1], 1)
                dve.wait_ge(free[0], 2 * j + 3)
                dve.wait_ge(free[1], 2 * j + 3)
                dve.tensor_tensor(T[3], T[3], T[2], ALU.mult).then_inc(ain_y, 1)
                dve.wait_ge(g_hi, j + 1)
                low(kt(GL, j), T[3], kt(GH, j)).then_inc(g_lo, 1)
            links.end(KT)
            add_bias(N_MODS_A, N_MODS)
            coefficients(4 * KT, "kv_g", KT)
            coefficients(6 * KT, "b_g", 2 * KT, True)

            def new_residual(name, base, gate, added):
                links(dve.memset(T[1], 0.0))
                with dve.Fori(0, KT // 2) as i:
                    for m in range(2):
                        s = (base + m) % 2
                        dve.wait_ge(chunk_done, 2 * i + (base + m + 2))
                        x = kt(X, 2 * i + m)
                        if gate is None:
                            dve.tensor_tensor(x, PAIR[s], x, ALU.add).then_inc(free[s], 1)
                        else:
                            mul_add(x, PAIR[s], col(MOD, 2 * i + (gate + m)), x).then_inc(free[s], 1)
                        add_square(2 * i + (added + m), T[1], T[2 + m])

            new_residual("aout", C_AOUT, 2 * KT, KT)
            dve.wait_ge(mod_ready, 1)
            fill_lo("kv", 2, lambda k: col(COEF, KT + k), 3 * KT)
            with dve.Fori(0, KT) as i:
                dve.wait_ge(kv_vh, i + 1)
                low(VSL[:, :], PAIR[2], VSH[:, :]).then_inc(free[2], 1)
                dve.wait_ge(kv_kh, i + 1)
                low(KSL[:, :], PAIR[1], KSH[:, :]).then_inc(free[1], 1)
            fill_lo("qz", 2, lambda k: col(COEF, 2 * KT + k), 5 * KT)

            dve.wait_ge(f_lo, FILL["qz"] + KT)
            for c in bC:
                links(dve.memset(c[:, S:S + 1], 1.0))

            def queries_lo(j, par):
                dve.wait_ge(b_qh, j + 1)
                low(bQL[par][:, :], PAIR[0], bQH[par][:, :]).then_inc(free[0], 1)

            def gate(j, par):
                pair = 1 if isinstance(j, int) and j == 0 else 0
                dve.wait_ge(b_sg, j + 1)
                dve.tensor_tensor(bZS[par][:, :], PAIR[pair], bZS[par][:, :], ALU.mult).then_inc(free[pair], 1)

            queries_lo(0, 0)
            gate(0, 0)
            dve.wait_ge(free[1], USED["qz"][1])

            def attention_b(j, par, fill=True, first=False):
                def turned(s, g):
                    if s < 0 and first or g >= len(GROUP_BLOCKS[s % ST]):
                        return
                    bl = blocks_of(s % ST, g)
                    dve.wait_ge(b_ath, 2 * NG * j + (group_index(s) + g + 1))
                    b = (s % 2, bl[0], bl[-1] + 1)
                    low(at_blocks(ATL[s // 2 % 2], *b), turned_blocks(len(bl)), at_blocks(ATH[s // 2 % 2], *b)).then_inc(b_atl, 1)

                def outputs(s):
                    if s % 2 == 0 or s < 0 and first:
                        return
                    h, t = s % (2 * ST) // ST, s % ST
                    rows, b = slice(h * HD, (h + 1) * HD), slice((t - 1) * P, (t + 1) * P)
                    y = bZS[par if s >= 0 else 1 - par][rows, b]
                    o = OB + s // 2 % 2 * 2 * P
                    dve.wait_ge(b_av, ST * j + (s + 1) // 2)
                    dve.tensor_tensor(y, PS[rows, o:o + 2 * P], y, ALU.mult).then_inc(b_o, 1)

                for s in range(2 * ST):
                    n = (s % ST + 1) * P
                    dve.wait_ge(b_c, 2 * ST * j + (s + 1))
                    c = bC[s % 2][:, S - n:S]
                    dve.tensor_tensor_scan(c[:, ::-1], c[:, ::-1], c[:, ::-1], 1.0, ALU.mult, ALU.bypass).then_inc(b_scan, 1)
                    turned(s - 3, 0)
                    outputs(s - 4)
                    turned(s - 3, 1)
                    if not fill and 5 <= s < 4 + KT:
                        operand_lo("y", s - 5, bZS)
                    if fill and s == 5:
                        queries_lo(j + 1, 1 - par)
                    if fill and s == 13:
                        gate(j + 1, 1 - par)
                if not fill:
                    for s in range(2 * ST, 2 * ST + 4):
                        outputs(s - 4)
                        if s < 2 * ST + 3:
                            turned(s - 3, 0)
                            turned(s - 3, 1)
                    operand_lo("y", KT - 1, bZS)

            attention_b(0, 0, first=True)
            with dve.Fori(0, (KT - 2) // 2) as i:
                for m in range(2):
                    attention_b(2 * i + (1 + m), 1 - m)
            attention_b(KT - 1, 1, fill=False)
            dve.wait_ge(f_lo, FILL["y"] + KT)
            links(dve.memset(T[1], 0.0))
            links(dve.memset(TP, 0.0))
            dve.wait_ge(ld_xr, 16 * KT)
            with dve.Fori(0, KT // 2) as i:
                for m in range(2):
                    s = (C_BOUT + m) % 2
                    dve.wait_ge(chunk_done, 2 * i + (C_BOUT + m + 2))
                    x = kt(X, 2 * i + m)
                    mul_add(x, PAIR[s], col(MOD, 2 * i + (7 * KT + m)), x).then_inc(free[s], 1)
                    add_square(4 * i + (2 * KT + 2 * m), T[1], T[2])
                    add_square(4 * i + (2 * KT + 2 * m + 1), TP, T[3])
            dve.wait_ge(ms2, 1)
            dve.wait_ge(ss, 4)
            dve.tensor_tensor(T[3], PAIR[3], T[3], ALU.mult).then_inc(ms2, 1)
            dve.wait_ge(rs, 3)
            links(dve.tensor_tensor(T[0], T[1], T[2], ALU.mult))
            links(dve.tensor_tensor(COEF[:, 3 * KT:4 * KT], VEC[:, _V["final_g"]:_V["final_g"] + KT],
                                    VEC[:, _V["mix_g"]:_V["mix_g"] + KT], ALU.mult))
            dve.memset(TMP[4][:, 0:PADW], 0.0).then_inc(p_mx, 1)
            fill_lo("mix", 3, lambda k: col(COEF, 3 * KT + k))
            for k in range(KT):
                mul_mul(kt(X, k), kt(X, k), vec("final_g", k), T[1]).then_inc(x_new, 1)

            links(dve.memset(TMP[0][:, 0:PADW], 0.0))
            links(dve.memset(TMP[1][:, 0:PADW], 0.0))
            for g, w in enumerate(POOL_W):
                c = C_POOL + g
                dve.wait_ge(free[c % 2], USED["pool"][c % 2] + g // 2 + 1)
                cur, sh = TMP[4], 1
                while sh < w:
                    dst = TMP[1] if cur is not TMP[1] else TMP[0]
                    links(dve.tensor_tensor(dst[:, PADW:], cur[:, PADW:], cur[:, PADW - sh:PADW - sh + S], ALU.add))
                    cur, sh = dst, 2 * sh
                e = _V["edge"] + PADW * g
                links(dve.tensor_tensor(cur[:, PADW:2 * PADW], cur[:, PADW:2 * PADW], VEC[:, e:e + PADW], ALU.mult))
                dve.scalar_tensor_tensor(out=T[3], in0=cur[:, PADW:], scalar=1.0 / w, in1=TP,
                                         op0=ALU.mult, op1=ALU.subtract).then_inc(p_mx, 1)
                dve.wait_ge(p_mh, g + 1)
                low(kt(MXL, g), T[3], kt(MXH, g)).then_inc(p_ml, 1)
            for g in range(4):
                dve.wait_ge(p_yh, g + 1)
                dve.scalar_tensor_tensor(out=kt(YPL, g), in0=PAIR[g % 2], scalar=vec("pool_scale", g),
                                         in1=kt(YPH, g).bitcast(F32), op0=ALU.mult, op1=ALU.subtract).then_inc(p_yl, 1)
            s0, s1 = C_GP % 2, (C_GP + 1) % 2
            with dve.Fori(0, KT) as n:
                dve.wait_ge(free[s0], n + (USED["gp"][s0] + 1))
                dve.wait_ge(chunk_done, 2 * n + (C_GP + 3))
                dve.tensor_tensor(T[2], PAIR[s1], T[1], ALU.mult).then_inc(free[s1], 1)
                dve.wait_ge(gp_st, 16 * n + 16)

            dve.wait_ge(d_ld, 32)
            links(dve.tensor_tensor(dSQ[:, 0:HD], dRS[:, 0:HD], dRS[:, HD:2 * HD], ALU.mult))
            links(dve.tensor_tensor(dSQ[:, HD:2 * HD], dRS[:, 2 * HD:3 * HD], dRS[:, 3 * HD:4 * HD], ALU.mult))
            dve.reduce_sum(SM[:, 8:9], dSQ[:, 0:HD], AX_X)
            dve.reduce_sum(SM[:, 9:10], dSQ[:, HD:2 * HD], AX_X).then_inc(d_lam, 1)
            dve.wait_ge(d_lam, 2)
            links(mul_add(NLAM[:, :], SM[:, 10:11], -1.0, SM[:, 11:12]))
            dve.tensor_scalar(NLAM[:, :], NLAM[:, :], -LAMBDA_INIT, None, ALU.add).then_inc(d_lam, 1)

            def norm_d(raw, gain, n):
                dve.wait_ge(d_rs, n)
                mul_mul(raw[:, :], raw[:, :], gain, dRS[:, :]).then_inc(d_n, 1)

            def lo_d(dst, raw, hi, n):
                dve.wait_ge(d_hi, n)
                return low(dst[:, :], raw[:, :], hi[:, :])

            def slope(j, par):
                dve.tensor_scalar(dSL[par][:, :], IDF[:, :], vec("slope", j), None, ALU.mult).then_inc(d_split, 1)

            norm_d(dQR[0], GQ8[:, 0:1], 1)
            lo_d(dQL[0], dQR[0], dQH[0], 1)
            norm_d(dKR[0], vec("gk"), 2)
            lo_d(dKL[0], dKR[0], dKH[0], 2)
            slope(0, 0)
            ud = USED["qkv2"]

            def attention_d(j, par, fill=True, first=False):
                nxt = 1 - par

                def turned(s, g):
                    if s < 0 and first or g >= len(GROUP_BLOCKS[s % ST]):
                        return
                    bl = blocks_of(s % ST, g)
                    dve.wait_ge(d_ath, NG * j + (group_index(s) + g + 1))
                    b = (s % 2, bl[0], bl[-1] + 1)
                    low(at_blocks(ATL[s // 2 % 2], *b), turned_blocks(len(bl)), at_blocks(ATH[s // 2 % 2], *b)).then_inc(d_atl, 1)

                def outputs(s):
                    if s % 2 == 0 or s < 0 and first:
                        return
                    o = OB + s // 2 % 2 * 2 * P
                    t = s % ST
                    dve.wait_ge(d_av, ST // 2 * j + (s + 1) // 2)
                    if s == 1 and not first:
                        dve.wait_ge(d_st, 16 * j)
                    dve.tensor_copy(dOT[par if s >= 0 else nxt][:, (t - 1) * P:(t + 1) * P], PS[:, o:o + 2 * P]).then_inc(d_o, 1)

                for s in range(ST):
                    n = (s + 1) * P
                    dve.wait_ge(d_s, 2 * ST * j + (2 * s + 1))
                    dve.reduce_max(SM[:, 0:1], PS[:, S:S + n], AX_X)
                    dve.wait_ge(d_s, 2 * ST * j + (2 * s + 2))
                    links(dve.reduce_max(SM[:, 1:2], PS[:, 2 * S:2 * S + n], AX_X))
                    dve.tensor_scalar(SM[:, 2:4], SM[:, 0:2], -1.0, None, ALU.mult).then_inc(d_max, 1)
                    turned(s - 1, 0)
                    if fill and s == 5:
                        lo_d(dQL[nxt], dQR[nxt], dQH[nxt], 3 * j + 4)
                    if fill and s == 7:
                        lo_d(dKL[nxt], dKR[nxt], dKH[nxt], 3 * j + 5)
                        slope(j + 1, nxt)
                    late = s in (5, 7)
                    if not late:
                        turned(s - 1, 1)
                    dve.wait_ge(free[1], ST * j + (ud[1] + s + 1))
                    dve.wait_ge(free[2], ST * j + (ud[2] + s + 1))
                    links(dve.reciprocal(SM[:, 6:8], SM[:, 4:6]))
                    links(dve.tensor_scalar(SM[:, 8:9], SM[:, 7:8], NLAM[:, 0:1], None, ALU.mult))
                    links(dve.tensor_scalar(dP1[:, 0:n], dP1[:, 0:n], SM[:, 8:9], None, ALU.mult))
                    mul_add(dP0[s % 2][:, 0:n], dP0[s % 2][:, 0:n], SM[:, 6:7], dP1[:, 0:n]).then_inc(d_a, 1)
                    if late:
                        turned(s - 1, 1)
                    outputs(s - 1)
                    if s == 0:
                        dve.wait_ge(d_hi, 3 * j + 3)
                        low(dVL[par][:, :], PAIR[0], dVH[par][:, :]).then_inc(free[0], 1)
                    if s == 2 and not first:
                        norm_d(dOT[nxt], GS8[:, 0:1], 3 * j + 2)
                    if not fill:
                        if s >= 2:
                            operand_lo("ab", s - 2, dOT)
                        if s == ST - 1:
                            operand_lo("ab", KT - 2, dOT)
                        continue
                    if s == 4:
                        norm_d(dQR[nxt], GQ8[:, 0:1], 3 * j + 3)
                    if s == 6:
                        norm_d(dKR[nxt], vec("gk"), 3 * j + 4)
                if not fill:
                    turned(ST - 1, 0)
                    turned(ST - 1, 1)
                    outputs(ST - 1)
                    norm_d(dOT[par], GS8[:, 0:1], 3 * KT)
                    operand_lo("ab", KT - 1, dOT)

            attention_d(0, 0, first=True)
            with dve.Fori(0, (KT - 2) // 2) as i:
                links.round(i, 2 * 4 * ST)
                for m in range(2):
                    attention_d(2 * i + (1 + m), 1 - m)
            links.end((KT - 2) // 2)
            attention_d(KT - 1, 1, fill=False)
            for n in range(KT):
                s = n % 2
                gate, part = T[n % 2], T[2 + n % 2]
                dve.wait_ge(chunk_done, C_AB + n + 2)
                dve.wait_ge(ab_ld[n % 2], 32 * (n // 2 + 1))
                dve.tensor_tensor(gate, PAIR[s], gate, ALU.mult).then_inc(free[s], 1)
                dve.wait_ge(free[s], USED["ab"][s] + n // 2 + 1)
                dve.tensor_tensor(part, part, gate, ALU.add).then_inc(ab_m, 1)
                dve.wait_ge(g_hi, KT + n + 1)
                low(kt(GL, n), part, kt(GH, n)).then_inc(g_lo, 1)
            dve.wait_ge(ld_xr, 2 * KT * 16)
            new_residual("wo", C_WO, None, 4 * KT)
            fill_lo("ffn", 4, lambda k: vec("ffn_g", k))
            with dve.Fori(0, FFQ) as q:
                with dve.Fori(0, KT // 2) as i:
                    for m in range(2):
                        s = (C_FF + m) % 2
                        dve.wait_ge(ff_r, 2 * i + KT * q + (m + 1))
                        dve.scalar_tensor_tensor(out=T[2 + m], in0=PAIR[s], scalar=0.0, in1=T[m],
                                                 op0=ALU.max, op1=ALU.mult).then_inc(free[s], 1)
                        dve.wait_ge(g_hi, 2 * i + KT * q + (2 * KT + m + 1))
                        low(kt(GL, 2 * i + m), T[2 + m], kt(GH, 2 * i + m)).then_inc(g_lo, 1)
                with dve.Fori(0, KT // 2) as i:
                    for m in range(2):
                        s = (C_FF + m) % 2
                        dve.wait_ge(chunk_done, 2 * i + 2 * KT * q + (C_FF + KT + m + 2))
                        x = kt(X, 2 * i + m)
                        dve.tensor_tensor(x, PAIR[s], x, ALU.add).then_inc(free[s], 1)

        @block.gpsimd
        def _(pool):
            def split_w(c, slot):
                pool.wait_ge(w_hi, c + 1)
                pool.tensor_tensor(WL[slot][:, :], WR0[:, :], WH[slot][:, :].bitcast(F32), ALU.subtract).then_inc(w_lo, 1)

            last = C_QZ + 3
            with pool.Fori(0, last // 2) as i:
                for m in range(2):
                    split_w(2 * i + m, m)
            split_w(last - 1, (last - 1) % 2)

            u = USED["qz"]

            def attention_b(j, fill):
                for s in range(2 * ST):
                    n = (s % ST + 1) * P
                    pool.wait_ge(b_scan, 2 * ST * j + (s + 1))
                    pool.wait_ge(free[1 + s % 2], ST * j + (u[1 + s % 2] + s // 2 + 1))
                    b = bB[s % 4][:, 0:n]
                    pool.tensor_tensor(b, b, bC[s % 2][:, S - n + 1:S + 1], ALU.mult).then_inc(b_a, 1)
                    if fill and s == 1:
                        split_w(2 * j + (C_QZ + 3), 1)
                    if fill and s == 9:
                        split_w(2 * j + (C_QZ + 4), 0)

            with pool.Fori(0, KT - 1) as j:
                attention_b(j, True)
            attention_b(KT - 1, False)
            first, last = C_BOUT + 1, N_CHUNKS + 2
            with pool.Fori(0, (last - first) // 2) as i:
                for m in range(2):
                    split_w(2 * i + (first + m), (first + m) % 2)
            if (last - first) % 2:
                split_w(last - 1, (last - 1) % 2)


def _chunks(w):
    k, n = w.shape
    a = np.zeros((n // P, P, KT, P), w.dtype)
    a[:, :, :k // P] = w.reshape(k // P, P, n // P, P).transpose(2, 1, 0, 3)
    return a.reshape(n // P, P, D)


def _columns(v):
    return np.asarray(v).reshape(-1, P).T


def kernel(**inputs):
    import concourse.bacc as _bacc
    from concourse.bass_utils import run_bass_kernel_spmd as _run

    f = {k: np.asarray(v) for k, v in inputs.items()}
    ain, kv, qz = _chunks(f["a_w_in"][0]), _chunks(f["w_kv"]), _chunks(f["b_w_qz"][0])
    win, gate = _chunks(f["w_in_2"][0]), _chunks(f["w_gate_2"][0])
    grp = np.zeros((1, P, D), np.float32)
    grp[0, :, 0:4 * P] = f["w_pool_grp_2"][0].transpose(1, 0, 2).reshape(P, 4 * P)
    branch = _chunks(f["w_branch_pool_2"][0])
    up, down = _chunks(f["w_up_2"][0]), f["w_down_2"][0]
    parts = []
    for j in range(KT):
        parts += [ain[KT + j], ain[2 * KT + j], ain[j], ain[3 * KT + j]]
    parts += list(_chunks(f["a_w_out"][0]))
    for j in range(KT):
        parts += [kv[KT + j], kv[j]]
    for j in range(KT):
        parts += [qz[j], qz[KT + j]]
    parts += list(_chunks(f["b_w_out"][0]))
    parts += list(win[0:4]) + list(gate[KT:]) + [grp[0]]
    for j in range(KT):
        parts += [gate[j], branch[j]]
    for j in range(KT):
        parts += [win[4 + j], win[4 + KT + j], win[4 + 2 * KT + j]]
    parts += list(_chunks(f["w_branch_attn_2"][0])) + list(_chunks(f["w_out_2"][0]))
    for q in range(FFQ):
        parts += list(up[q * KT:(q + 1) * KT]) + list(_chunks(down[q * D:(q + 1) * D]))
    parts += [np.zeros((P, D), np.float32)] * 2
    assert len(parts) == N_CHUNKS + 2
    wst = np.stack(parts)
    mods = np.concatenate([f["a_mod_w"][0], f["kv_mod_w"], f["b_mod_w"][0]], axis=1).T.reshape(N_MODS, P, D)
    cb = np.broadcast_to(f["c"], (P, D))

    edge = np.ones((4, PADW), np.float32)
    for g, w in enumerate(POOL_W):
        edge[g, :w] = w / np.arange(1, w + 1)
    two = lambda v: np.concatenate([v, v])
    cols = {
        "mod_b": np.concatenate([f["a_mod_b"][0], f["kv_mod_b"], f["b_mod_b"][0]]),
        "a_g": f["a_norm_g"], "kv_g": f["kv_norm_g"], "b_g": f["b_norm_g"], "conv": f["a_conv_w"][0],
        "final_g": f["final_norm_g"], "mix_g": f["g_mix_2"], "pool_scale": f["pool_scale_2"],
        "gq": two(f["g_q_2"][0]), "gk": two(f["g_k_2"][0]), "gsub": f["g_sub_2"], "b_gate": f["b_gate_2"],
        "ffn_g": f["g_ffn_2"],
    }
    vecs = np.zeros((P, NV), np.float32)
    for name, v in cols.items():
        v = _columns(v)
        vecs[:, _V[name]:_V[name] + v.shape[1]] = v
    vecs[:, _V["slope"]:_V["slope"] + KT] = 2.0 ** -np.arange(1.0, KT + 1)
    vecs[:, _V["edge"]:_V["edge"] + 4 * PADW] = edge.reshape(-1)

    q, k = np.arange(P)[:, None], np.arange(P)[None, :]
    rel = np.arange(S)[None, :] - (S - P)
    consts = np.zeros((P, NC_), np.float32)
    consts[:, K_ID:K_ID + P] = np.eye(P)
    consts[:, K_TRI:K_TRI + P] = np.where(k >= q, -BIG, 0.0)
    consts[:, K_BD:K_BD + P] = q // HD == k // HD
    consts[:, K_DIST:K_DIST + S] = np.where(np.floor_divide(rel, 64) <= q // 64, -np.abs(q - rel), -BIG)
    consts[:, K_LAM:] = f["lambda_qk_2"].reshape(1, 4 * HD)

    xt = f["x"][0].T.reshape(KT, P, S).transpose(1, 0, 2).reshape(P, KT * S)

    nc = _bacc.Bacc("TRN2", target_bir_lowering=False, num_devices=1)
    arrays = {n: np.ascontiguousarray(a, np.float32) for n, a in
              (("xt", xt), ("cb", cb), ("vecs", vecs), ("consts", consts), ("mods", mods), ("wst", wst))}
    args = [nc.dram_tensor(n, a.shape, F32, kind="ExternalInput").ap() for n, a in arrays.items()]
    out = nc.dram_tensor("out", [KT, P, S], F32, kind="ExternalOutput").ap()
    block_kernel(nc, *args, out)
    r = _run(nc, [arrays], core_ids=[0])
    return r.results[0]["out"].reshape(D, S).T.reshape(1, S, D)
```
